# Optimizing a Trainium2 kernel written in Bass

```python
import jax, jax.numpy as jnp
from jax import lax
import numpy as np

'''Two consecutive layers of a hybrid autoregressive decoder trunk, run for a prompt group and a
sample group that share the same weights.

Layer (post-norm, DeepNorm):
  mix = W_out [ GLA heads | RetNet retention heads | HGRN2 heads ](x W_in)   (parallel head groups)
  x   = LayerNorm(ALPHA * x + mix)
  x   = LayerNorm(ALPHA * x + PEER(x))                                      (product-key single-neuron experts)
  x   = x + (p[i] W_ple) * sigmoid(x W_ple_gate)                            (per-layer input embedding)

Inputs:
  x_prompt (BATCH, SEQ, D_MODEL), x_sample (DEC_BATCH, DEC_SEQ, D_MODEL)
  p_prompt (DEPTH, BATCH, SEQ, PLE_DIM), p_sample (DEPTH, DEC_BATCH, DEC_SEQ, PLE_DIM)
  state_gla  (DEPTH, DEC_BATCH, GLA_HEADS, GLA_DK, GLA_DV)    GLA recurrent state after PAST_LEN tokens
  state_ret  (DEPTH, DEC_BATCH, RET_HEADS, RET_DK, RET_DV)    retention recurrent state
  state_hgrn (DEPTH, DEC_BATCH, HGRN_HEADS, HGRN_DK, HGRN_DV) HGRN2 expanded state
  weights stacked over a leading DEPTH axis.
Returns the tuple
  (y_prompt (BATCH, SEQ, D_MODEL), y_sample (DEC_BATCH, DEC_SEQ, D_MODEL),
   new_gla_prompt (DEPTH, BATCH, 4, 48, 96), new_ret_prompt (DEPTH, BATCH, 4, 48, 96),
   new_hgrn_prompt (DEPTH, BATCH, 4, 64, 64),
   new_gla_sample (DEPTH, DEC_BATCH, 4, 48, 96), new_ret_sample (DEPTH, DEC_BATCH, 4, 48, 96),
   new_hgrn_sample (DEPTH, DEC_BATCH, 4, 64, 64))
'''

D_MODEL = 1024
BATCH = 1
SEQ = 512
DEPTH = 2
DEC_BATCH = 8
DEC_SEQ = 1
PAST_LEN = 4096
PAGE_SIZE = 128

GLA_HEADS = 4
GLA_DK = 48
GLA_DV = 96
GLA_LOWRANK = 16
GLA_TAU = 16.0
RET_HEADS = 4
RET_DK = 48
RET_DV = 96
ROPE_BASE = 10000.0
HGRN_HEADS = 4
HGRN_DK = 64
HGRN_DV = 64
MIX_WIDTH = GLA_HEADS * GLA_DV + RET_HEADS * RET_DV + HGRN_HEADS * HGRN_DV
IN_SIZES = (GLA_HEADS * GLA_DK, GLA_HEADS * GLA_DK, GLA_HEADS * GLA_DV, GLA_HEADS * GLA_DV, GLA_LOWRANK,
            RET_HEADS * RET_DK, RET_HEADS * RET_DK, RET_HEADS * RET_DV, RET_HEADS * RET_DV,
            HGRN_HEADS * HGRN_DK, HGRN_HEADS * HGRN_DK, HGRN_HEADS * HGRN_DV, HGRN_HEADS * HGRN_DV)
N_IN = sum(IN_SIZES)
CHUNK = 64
PEER_HEADS = 8
PEER_DQ = 256
N_KEYS = 128
N_EXPERTS = N_KEYS * N_KEYS
PEER_TOPK = 16
PEER_BLOCK = 128
PLE_DIM = 256
ALPHA = (2 * DEPTH) ** 0.25
BETA = (8 * DEPTH) ** -0.25
NORM_EPS = 1e-5

kernel_name = 'hymba_gla_retnet_hgrn2_peer_step'

def layer_norm(x, g, b):
    xf = x.astype(jnp.float32)
    mu = jnp.mean(xf, axis=-1, keepdims=True)
    var = jnp.mean(jnp.square(xf - mu), axis=-1, keepdims=True)
    return (xf - mu) * lax.rsqrt(var + NORM_EPS) * g + b

def head_rms_norm(o, g):
    of = o.astype(jnp.float32)
    return of * lax.rsqrt(jnp.mean(jnp.square(of), axis=-1, keepdims=True) + NORM_EPS) * g[:, None, :]

def head_group_norm(o, g):
    of = o.astype(jnp.float32)
    mu = jnp.mean(of, axis=-1, keepdims=True)
    var = jnp.mean(jnp.square(of - mu), axis=-1, keepdims=True)
    return (of - mu) * lax.rsqrt(var + NORM_EPS) * g[:, None, :]

def split_heads(t, n):
    B, L, _ = t.shape
    return t.reshape(B, L, n, -1).transpose(0, 2, 1, 3)

def merge_heads(o):
    B, H, L, d = o.shape
    return o.transpose(0, 2, 1, 3).reshape(B, L, H * d)

def rotary(t, pos):
    d = t.shape[-1]
    inv = 1.0 / (ROPE_BASE ** (jnp.arange(0, d, 2, dtype=jnp.float32) / d))
    ang = pos[:, None] * inv[None, :]
    cos, sin = jnp.cos(ang), jnp.sin(ang)
    t1, t2 = t[..., : d // 2], t[..., d // 2:]
    return jnp.concatenate([t1 * cos - t2 * sin, t1 * sin + t2 * cos], axis=-1)

def gated_linear_recurrence(q, k, v, log_decay, s0):
    B, H, L, _ = q.shape
    dv = v.shape[-1]
    C = CHUNK if L % CHUNK == 0 else L
    n = L // C

    def to_chunks(a):
        a = a.astype(jnp.float32)
        return a.reshape(B, H, n, C, a.shape[-1]).transpose(2, 0, 1, 3, 4)

    causal = jnp.tril(jnp.ones((C, C), dtype=bool))[:, :, None]

    def step(S, inp):
        qc, kc, vc, gc = inp
        b = jnp.cumsum(gc, axis=2)
        diff = b[:, :, :, None, :] - b[:, :, None, :, :]
        decay = jnp.where(causal, jnp.exp(jnp.where(causal, diff, 0.0)), 0.0)
        scores = jnp.sum(qc[:, :, :, None, :] * kc[:, :, None, :, :] * decay, axis=-1)
        o = (jnp.einsum('bhij,bhjv->bhiv', scores, vc)
             + jnp.einsum('bhik,bhkv->bhiv', qc * jnp.exp(b), S))
        b_last = b[:, :, -1:, :]
        S_new = (S * jnp.exp(b_last[:, :, 0, :, None])
                 + jnp.einsum('bhjk,bhjv->bhkv', kc * jnp.exp(b_last - b), vc))
        return S_new, o

    S, o = lax.scan(step, s0.astype(jnp.float32),
                    (to_chunks(q), to_chunks(k), to_chunks(v), to_chunks(log_decay)))
    return o.transpose(1, 2, 0, 3, 4).reshape(B, H, L, dv), S

def mixer_block(x, pos, s_gla, s_ret, s_hgrn, w_in, gla_w_gate, gla_b_gate, gla_norm,
                ret_norm, hgrn_lb, hgrn_norm, w_out):
    B, L, _ = x.shape
    z = jnp.einsum('bld,dn->bln', x, w_in)
    offsets = [int(c) for c in np.cumsum(IN_SIZES)[:-1]]
    (gq, gk, gv, gg, glr, rq, rk, rv, rg, hq, hf, hi, hg) = jnp.split(z, offsets, axis=-1)

    log_a = jax.nn.log_sigmoid((jnp.einsum('blr,rk->blk', glr, gla_w_gate) + gla_b_gate).astype(jnp.float32)) / GLA_TAU
    o_gla, s_gla_new = gated_linear_recurrence(
        split_heads(gq, GLA_HEADS) * GLA_DK ** -0.5, split_heads(gk, GLA_HEADS),
        split_heads(gv, GLA_HEADS), split_heads(log_a, GLA_HEADS), s_gla)
    o_gla = merge_heads(head_rms_norm(o_gla, gla_norm)) * jax.nn.silu(gg)

    log_gamma = jnp.log1p(-jnp.exp2(-5.0 - jnp.arange(RET_HEADS, dtype=jnp.float32)))
    g_ret = jnp.broadcast_to(log_gamma[None, :, None, None], (B, RET_HEADS, L, 1))
    o_ret, s_ret_new = gated_linear_recurrence(
        rotary(split_heads(rq, RET_HEADS), pos),
        rotary(split_heads(rk, RET_HEADS), pos) * RET_DK ** -0.5,
        split_heads(rv, RET_HEADS), g_ret, s_ret)
    o_ret = merge_heads(head_group_norm(o_ret, ret_norm)) * jax.nn.silu(rg)

    log_f = jnp.logaddexp(jnp.log(hgrn_lb), jnp.log1p(-hgrn_lb) + jax.nn.log_sigmoid(hf.astype(jnp.float32)))
    o_h, s_hgrn_new = gated_linear_recurrence(
        split_heads(jax.nn.silu(hq), HGRN_HEADS), split_heads(-jnp.expm1(log_f), HGRN_HEADS),
        split_heads(hi, HGRN_HEADS), split_heads(log_f, HGRN_HEADS), s_hgrn)
    o_h = merge_heads(head_rms_norm(o_h, hgrn_norm)) * jax.nn.silu(hg)

    o = jnp.concatenate([o_gla, o_ret, o_h], axis=-1)
    return jnp.einsum('blm,md->bld', o, w_out), s_gla_new, s_ret_new, s_hgrn_new

def peer_ffn(x, w_q, subkeys, u_tab, v_tab):
    B, L, D = x.shape
    T = B * L
    xt = x.reshape(T, D)
    q = jnp.einsum('td,dn->tn', xt, w_q).reshape(T, PEER_HEADS, PEER_DQ).astype(jnp.float32)
    half = PEER_DQ // 2
    s1 = jnp.einsum('thd,hnd->thn', q[..., :half], subkeys[:, 0].astype(jnp.float32))
    s2 = jnp.einsum('thd,hnd->thn', q[..., half:], subkeys[:, 1].astype(jnp.float32))
    v1, i1 = lax.top_k(s1, PEER_TOPK)
    v2, i2 = lax.top_k(s2, PEER_TOPK)
    cand = (v1[..., :, None] + v2[..., None, :]).reshape(T, PEER_HEADS, PEER_TOPK * PEER_TOPK)
    best, ci = lax.top_k(cand, PEER_TOPK)
    expert = (jnp.take_along_axis(i1, ci // PEER_TOPK, axis=-1) * N_KEYS
              + jnp.take_along_axis(i2, ci % PEER_TOPK, axis=-1))
    gate = jax.nn.softmax(best, axis=-1)
    nb = -(-T // PEER_BLOCK)
    pad = nb * PEER_BLOCK - T
    xb = jnp.pad(xt, ((0, pad), (0, 0))).reshape(nb, PEER_BLOCK, D)
    eb = jnp.pad(expert, ((0, pad), (0, 0), (0, 0))).reshape(nb, PEER_BLOCK, PEER_HEADS, PEER_TOPK)
    gb = jnp.pad(gate, ((0, pad), (0, 0), (0, 0))).reshape(nb, PEER_BLOCK, PEER_HEADS, PEER_TOPK)

    def expert_block(args):
        xc, ec, gc = args
        act = jax.nn.gelu(jnp.einsum('thkd,td->thk', u_tab[ec], xc), approximate=False)
        return jnp.einsum('thk,thkd->td', gc * act, v_tab[ec])

    out = lax.map(expert_block, (xb, eb, gb))
    return out.reshape(nb * PEER_BLOCK, D)[:T].reshape(B, L, D)

def trunk(x, p, pos, s_gla, s_ret, s_hgrn, weights):
    (w_in, gla_w_gate, gla_b_gate, gla_norm, ret_norm, hgrn_lb, hgrn_norm, w_out,
     ln1_g, ln1_b, ln2_g, ln2_b, peer_w_q, peer_subkeys, peer_u, peer_v, ple_proj, ple_gate) = weights
    new_gla, new_ret, new_hgrn = [], [], []
    for i in range(DEPTH):
        mix, sg, sr, sh = mixer_block(x, pos, s_gla[i], s_ret[i], s_hgrn[i], w_in[i], gla_w_gate[i],
                                      gla_b_gate[i], gla_norm[i], ret_norm[i], hgrn_lb[i],
                                      hgrn_norm[i], w_out[i])
        x = layer_norm(ALPHA * x + mix, ln1_g[i], ln1_b[i])
        x = layer_norm(ALPHA * x + peer_ffn(x, peer_w_q[i], peer_subkeys[i], peer_u[i], peer_v[i]),
                       ln2_g[i], ln2_b[i])
        x = x + jnp.einsum('blp,pd->bld', p[i], ple_proj[i]) * jax.nn.sigmoid(
            jnp.einsum('bld,de->ble', x, ple_gate[i]))
        new_gla.append(sg)
        new_ret.append(sr)
        new_hgrn.append(sh)
    return x, jnp.stack(new_gla), jnp.stack(new_ret), jnp.stack(new_hgrn)

def setup_inputs(seed: int = 0) -> dict:
    key = jax.random.key(seed)
    ks = jax.random.split(key, 26)

    def nrm(k, shape, s):
        return s * jax.random.normal(k, shape, jnp.float32)

    return {
        'x_prompt': nrm(ks[0], (BATCH, SEQ, D_MODEL), 1.0),
        'x_sample': nrm(ks[1], (DEC_BATCH, DEC_SEQ, D_MODEL), 1.0),
        'p_prompt': nrm(ks[2], (DEPTH, BATCH, SEQ, PLE_DIM), 1.0),
        'p_sample': nrm(ks[3], (DEPTH, DEC_BATCH, DEC_SEQ, PLE_DIM), 1.0),
        'state_gla': nrm(ks[4], (DEPTH, DEC_BATCH, GLA_HEADS, GLA_DK, GLA_DV), 1.0),
        'state_ret': nrm(ks[5], (DEPTH, DEC_BATCH, RET_HEADS, RET_DK, RET_DV), 1.0),
        'state_hgrn': nrm(ks[6], (DEPTH, DEC_BATCH, HGRN_HEADS, HGRN_DK, HGRN_DV), 1.0),
        'w_in': nrm(ks[7], (DEPTH, D_MODEL, N_IN), D_MODEL ** -0.5),
        'gla_w_gate': nrm(ks[8], (DEPTH, GLA_LOWRANK, GLA_HEADS * GLA_DK), GLA_LOWRANK ** -0.5),
        'gla_b_gate': nrm(ks[9], (DEPTH, GLA_HEADS * GLA_DK), 0.1),
        'gla_norm': 1.0 + nrm(ks[10], (DEPTH, GLA_HEADS, GLA_DV), 0.02),
        'ret_norm': 1.0 + nrm(ks[11], (DEPTH, RET_HEADS, RET_DV), 0.02),
        'hgrn_lb_logits': nrm(ks[12], (DEPTH, HGRN_HEADS * HGRN_DK), 0.5),
        'hgrn_norm': 1.0 + nrm(ks[13], (DEPTH, HGRN_HEADS, HGRN_DV), 0.02),
        'w_out': nrm(ks[14], (DEPTH, MIX_WIDTH, D_MODEL), BETA * MIX_WIDTH ** -0.5),
        'ln1_g': 1.0 + nrm(ks[15], (DEPTH, D_MODEL), 0.02),
        'ln1_b': nrm(ks[16], (DEPTH, D_MODEL), 0.02),
        'ln2_g': 1.0 + nrm(ks[17], (DEPTH, D_MODEL), 0.02),
        'ln2_b': nrm(ks[18], (DEPTH, D_MODEL), 0.02),
        'peer_w_q': nrm(ks[19], (DEPTH, D_MODEL, PEER_HEADS * PEER_DQ), D_MODEL ** -0.5),
        'peer_subkeys': nrm(ks[20], (DEPTH, PEER_HEADS, 2, N_KEYS, PEER_DQ // 2), (PEER_DQ // 2) ** -0.5),
        'peer_u': nrm(ks[21], (DEPTH, N_EXPERTS, D_MODEL), D_MODEL ** -0.5),
        'peer_v': nrm(ks[22], (DEPTH, N_EXPERTS, D_MODEL), BETA),
        'ple_proj': nrm(ks[23], (DEPTH, PLE_DIM, D_MODEL), PLE_DIM ** -0.5),
        'ple_gate': nrm(ks[24], (DEPTH, D_MODEL, D_MODEL), D_MODEL ** -0.5),
    }

def reference(x_prompt, x_sample, p_prompt, p_sample, state_gla, state_ret, state_hgrn,
              w_in, gla_w_gate, gla_b_gate, gla_norm, ret_norm, hgrn_lb_logits, hgrn_norm, w_out,
              ln1_g, ln1_b, ln2_g, ln2_b, peer_w_q, peer_subkeys, peer_u, peer_v, ple_proj, ple_gate):
    lb = jnp.cumsum(jax.nn.softmax(hgrn_lb_logits.astype(jnp.float32), axis=0), axis=0)
    lb = lb - lb[0:1]
    weights = (w_in, gla_w_gate, gla_b_gate, gla_norm, ret_norm, lb, hgrn_norm, w_out,
               ln1_g, ln1_b, ln2_g, ln2_b, peer_w_q, peer_subkeys, peer_u, peer_v, ple_proj, ple_gate)

    Bp, Lp = x_prompt.shape[0], x_prompt.shape[1]
    pos_prompt = jnp.arange(Lp, dtype=jnp.float32)
    y_prompt, gla_p, ret_p, hgrn_p = trunk(
        x_prompt, p_prompt, pos_prompt,
        jnp.zeros((DEPTH, Bp, GLA_HEADS, GLA_DK, GLA_DV), jnp.float32),
        jnp.zeros((DEPTH, Bp, RET_HEADS, RET_DK, RET_DV), jnp.float32),
        jnp.zeros((DEPTH, Bp, HGRN_HEADS, HGRN_DK, HGRN_DV), jnp.float32),
        weights)

    pos_sample = PAST_LEN + jnp.arange(x_sample.shape[1], dtype=jnp.float32)
    y_sample, gla_s, ret_s, hgrn_s = trunk(
        x_sample, p_sample, pos_sample, state_gla, state_ret, state_hgrn, weights)

    return (y_prompt, y_sample, gla_p, ret_p, hgrn_p, gla_s, ret_s, hgrn_s)


_drawn_inputs = setup_inputs


def setup_inputs(seed=0):
    import zlib

    import numpy as np

    out = dict(_drawn_inputs(seed))
    spreads = {}
    factors = {'gla_norm': 3.295, 'ret_norm': 3.188, 'hgrn_norm': 3.67}
    for name, (base, spread) in spreads.items():
        noise = np.random.default_rng([zlib.crc32(name.encode()), seed]).standard_normal(out[name].shape)
        drawn = base * np.exp(spread * noise) if base else spread * noise
        out[name] = __import__('jax').numpy.asarray(drawn.astype(out[name].dtype))
    for name, factor in factors.items():
        out[name] = (out[name] * factor).astype(out[name].dtype)
    return out
```

```python
import concourse.bass as bass
from concourse import mybir
from contextlib import ExitStack

D, T, NP, NS = 1024, 520, 512, 8
WID = [128, 128, 128, 128, 8]
KT = D // 128
HALF = T // 2
CH = 16
NC = NP // CH
CT = 128 // CH
DEPTH = 2
ALPHA = (2 * DEPTH) ** 0.25
EPS = 1e-5
PH, TOPK, NKEY = 8, 16, 128
SLOTS = PH * TOPK
NEXP = NKEY * NKEY
RING = 8
NGRP = SLOTS // RING
USES = 2 * 4 * NGRP + 2
DV = [96, 96, 64, 64, 96, 96]
VCOL = [0, 192, 768, 896, 384, 576]
ITEMS, SLOTW = 32, 4

FEATURES = ["hf0", "hf1", "glr", "hq0", "hq1", "gk0", "gk1", "gq0", "gq1", "rq0", "rq1", "rk0", "rk1"]
ZSLOT = {"hf0": 2, "hf1": 3, "hq0": 10, "hq1": 11, "gk0": 4, "gk1": 5, "gq0": 8, "gq1": 9,
         "rq0": 12, "rq1": 13, "rk0": 14, "rk1": 15}
I_V, I_GATE, I_WQ, I_SUB, I_PP, I_PT, I_PG = 7, 11, 16, 24, 26, 27, 28

CONSTS = {}
_at = 0
for _n, _w in (("ident", 128), ("perm", 128), ("onesg", 96), ("onesh", 128), ("dmat", 512), ("cos", 520),
               ("sin", 520), ("chunkmask", 520), ("mask16", 8), ("causal", 256), ("rqdec", 256),
               ("rkdec", 256), ("headsel", 2), ("g128", 2), ("gam", 2), ("eye8", 64), ("eps", 1),
               ("aident", 128), ("iota", 16)):
    CONSTS[_n] = (_at, _w)
    _at += _w
NCONST = _at
NSMALL = 268


def jobs():
    found, count = {}, {"A": 0, "D": 0}

    def add(ring, *name):
        found[name] = (ring, count[ring])
        count[ring] += 1

    def to_features(stage):
        for n in range(5):
            add("A", "xt", stage, n, 0)
            add("D", "xt", stage, n, 1)

    to_features(0)
    for m, name in enumerate(FEATURES):
        add("A", "z", m, 0)
        add("D", "z", m, 1)
        if name == "hq0":
            for g in range(2):
                for half in range(2):
                    add("D", "ga", g, half)
    for i in range(4):
        for n in range(5):
            add("A", "v", i, n)
    for s in range(4):
        for half in range(2):
            add("D", "rot", s, half)
    for f in range(6):
        if f < 4:
            add("D", "sc", f)
        else:
            add("D", "rsc", f, 0)
            add("D", "rsc", f, 1)
        add("D", "kt", f)
        add("D", "kts", f)
        if f < 4:
            for n in range(4):
                for half in range(2):
                    add("A", "dl", f, n, half)
        else:
            add("A", "rdl", f)
        for half in range(2):
            add("D", "dls", f, half)
        for h in range(2):
            add("A", "os", f, h)
        for h in range(2):
            add("A", "o", f, h)
    for m in range(10):
        for half in range(2):
            add("A", "g", m, half)
    for s in range(4):
        for half in range(2):
            add("D", "mu", s, half)
    for s in range(10):
        for half in range(2):
            add("A", "ms", s, half)
    for n in range(5):
        for half in range(2):
            add("D", "mix", n, half)
    to_features(1)
    for m in range(16):
        add("A", "q", m, 0)
        add("D", "q", m, 1)
    for n in (4, 0, 1, 2, 3):
        for c in range(4):
            add("D", "s", n, c)
        if n == 4:
            add("D", "et")
            add("D", "gt")
    for half in range(2):
        for n in range(5):
            add("A", "pp", half, n)
    to_features(2)
    for c in range(4):
        for n in range(5):
            add("A", "pg", c, n)
    return found


SIGNALS = """w_consumed layer_arrived sigm_ready abs_ready log1p_ready hdiff_ready hlog_ready b_ready
dec_ready eq_ready ek_ready kq_ready diff_ready min_ready pexp_ready p_ready p_used sct_ready
km_ready kms_ready dls_done s_ready rs_ready rq_ready ss_scaled z_ready mu_done sq_ready
rms_ready on_ready mv_ready rstd_ready x1_ready idx_staged xb_used lb_ready
u_used v_used score_ready gelu_ready w_ready diag_ready acc_ready idx_ready et_ready
xb_ready wsam_ready x2_ready ple_sig_ready x_ready silu_ready rprod_ready small_init places_free all_arrived
""".split()
DMASIGNALS = "x_loaded small_loaded lnp_loaded wout_loaded".split()
KEPT = "consts_loaded layer_go layer_done y_stored".split()


def build(nc, x_in, wstream, wout, small, lnp, lblog, st_in, consts, utab, vtab, y_out, st_p, st_s):
    fp32, i32, u32 = mybir.dt.float32, mybir.dt.int32, mybir.dt.uint32
    ALU = mybir.AluOpType
    ACT = mybir.ActivationFunctionType
    AX = mybir.AxisListType
    JOB = jobs()
    ds = bass.ds

    ctx = ExitStack()
    with ctx:
        def sb(name, *shape, dt=fp32):
            return ctx.enter_context(nc.sbuf_tensor(name, list(shape), dt))

        X = sb("X", 128, 5, D)
        XT = sb("XT", 128, KT, T)
        C = sb("C", 128, NCONST)
        WR = sb("WR", 128, SLOTW, 2048)
        SM = sb("SM", 128, NSMALL)
        LB = sb("LB", 128, 16)
        ST = sb("ST", 128, 5, 16)
        R = sb("R", 128, 30288)

        def view(at, *dims):
            n = 1
            for d in dims:
                n *= d
            v = R[:, at:at + n]
            if len(dims) == 1:
                return v
            names = "abcde"[:len(dims)]
            return v.rearrange(f"p ({' '.join(names)}) -> p {' '.join(names)}",
                               **{names[i]: dims[i] for i in range(1, len(dims))})

        Z = view(0, 16, T)
        ZG = view(0, 10, T)
        SQ = view(5200, 2, T)
        RS = view(6240, 2, T)
        OT = view(8320, 10, T)
        V = view(13520, 5, D)
        P = view(18640, 2, 4, NC, CH)
        T1 = view(18640, 4, T)
        T2 = view(20720, 4, T)
        S = view(22736, NC, 96)
        ROT = view(22800, 2, HALF)
        WO = view(13520, 10, D)
        SR = view(25808, 4, 96)
        KM = view(26192, 2, CT, 128)
        KMS = view(28240, CT, 128)
        SCT = view(29264, 2, 4, 128)
        LNP = view(25808, 4, D)
        QT = view(0, 16, T)
        G = view(8320, RING, D)
        IDX = view(16512, 4, SLOTS).bitcast(i32)
        GATE = view(17024, 5, SLOTS)
        WGT = view(17664, SLOTS)
        SCORE = view(17792, SLOTS)
        SC = view(17920, 2 * PH, NKEY)
        EQT = view(17920, PH, TOPK, TOPK)
        CAND = view(19968, PH, TOPK, TOPK)
        VV = view(22016, 2 * PH, TOPK)
        II = view(22272, 2 * PH, TOPK).bitcast(u32)
        IF = view(22528, 2 * PH, TOPK)
        BEST = view(22784, PH, TOPK)
        CI = view(22912, PH, TOPK).bitcast(u32)
        CAB = view(23040, 2, PH, TOPK).bitcast(u32)
        ABF = view(23296, 2, PH, TOPK)
        SEL = view(23552, 2, PH, TOPK)
        SUM = view(23808, 2, PH)
        EF = view(23824, PH, TOPK)
        IST = view(23952, 2, RING).bitcast(i32)
        IDXS = view(23968, NS).bitcast(i32)
        GATES = view(23976, NS)
        SSC = view(23984, NS)
        WS = view(23992, NS)
        WS8 = view(24000, NS, NS)
        DIAG = view(24064, RING, 128)
        PP = view(0, 5, D)
        SG = view(5120, 5, 256)
        SS = sb("SS", 128, NS, 96)
        DEC = sb("DEC", 128, 4, NC + NS)
        LBASE = sb("LBASE", 128, 1)

        A = [ctx.enter_context(nc.psum_tensor(f"A{i}", [128, 512], fp32)) for i in range(3)]
        DB = [ctx.enter_context(nc.psum_tensor(f"D{i}", [128, 512], fp32)) for i in range(3)]
        Y = ctx.enter_context(nc.psum_tensor("Y", [128, D], fp32))
        BANKS = {"A": A, "D": DB}

        sems = {n: ctx.enter_context(nc.semaphore(n)) for n in SIGNALS + DMASIGNALS + KEPT}
        full = {r: ctx.enter_context(nc.semaphore(f"{r}_full")) for r in "AD"}
        free = {r: ctx.enter_context(nc.semaphore(f"{r}_free")) for r in "AD"}
        w_loaded = [ctx.enter_context(nc.semaphore(f"w_loaded{i}")) for i in range(SLOTW)]
        fetched = [ctx.enter_context(nc.semaphore(f"fetched{i}")) for i in range(RING)]
        ss_loaded = ctx.enter_context(nc.semaphore("ss_loaded"))
        ss_stored = ctx.enter_context(nc.semaphore("ss_stored"))
        s_stored = ctx.enter_context(nc.semaphore("s_stored"))
        cleared = [sems[n] for n in SIGNALS + DMASIGNALS] + list(full.values()) + list(free.values()) \
            + w_loaded + [ss_loaded, ss_stored, s_stored]

        block = ctx.enter_context(nc.Block())

        def const(name, rows=128):
            at, n = CONSTS[name]
            return C[0:rows, at:at + n]

        ident = const("ident")

        def wait_full(eng, *name):
            ring, j = JOB[name]
            eng.wait_ge(full[ring], j + 1)
            return BANKS[ring][j % 3]

        def wait_emptied(eng, *name):
            ring, j = JOB[name]
            eng.wait_ge(free[ring], j + 1)

        def arrive(eng, L):
            eng.drain()
            eng.sem_inc(sems["layer_done"], 1)
            eng.wait_ge(sems["layer_go"], L + 1)

        def oplace(f, h):
            if f in (2, 3):
                return 8 + f - 2, h * 64, 64
            return (2 * f + h if f < 2 else 4 + 2 * (f - 4) + h), 0, 96

        def vcols(f, h):
            return slice(VCOL[f] + h * DV[f], VCOL[f] + (h + 1) * DV[f])

        @block.sync
        def _(sp):
            sp.dma_start(C[:, :], consts).then_inc(sems["consts_loaded"], 16)
            sp.dma_start(X[:, 0:4, :], x_in[0:NP].rearrange("(n p) d -> p n d", p=128)) \
                .then_inc(sems["consts_loaded"], 16)
            sp.dma_start(X[0:NS, 4, :], x_in[NP:T]).then_inc(sems["consts_loaded"], 16)
            sp.dma_start(LB[:, 0:4], lblog).then_inc(sems["consts_loaded"], 16)

            def item(L, i):
                if i >= SLOTW:
                    sp.wait_ge(sems["w_consumed"], i - SLOTW + 1)
                n = {I_SUB: 1024, I_SUB + 1: 1024, I_PT: 2 * T}.get(i, 2048)
                sp.dma_start(WR[:, i % SLOTW, 0:n], wstream[L, i, :, 0:n]).then_inc(w_loaded[i % SLOTW], 16)

            with sp.Fori(0, DEPTH) as L:
                sp.dma_start(SM[:, :], small[L]).then_inc(sems["small_loaded"], 16)
                for i in range(I_GATE):
                    item(L, i)
                for f in range(6):
                    if f == 4:
                        for i in range(I_GATE, I_GATE + SLOTW):
                            item(L, i)
                    if f >= 1:
                        sp.wait_ge(sems["dls_done"], f)
                        sp.dma_start(st_s[L, f - 1], SS[:, :, :]).then_inc(ss_stored, 16)
                        wait_full(sp, "os", f - 1, 1)
                        sp.wait_ge(ss_stored, 16 * f)
                    sp.dma_start(SS[:, :, :], st_in[L, f]).then_inc(ss_loaded, 16)
                    if 1 <= f <= 4:
                        sp.wait_ge(sems["s_ready"], f)
                        sp.dma_start(st_p[L, f - 1], S[:, NC - 1, :]).then_inc(s_stored, 16)
                    if f == 5:
                        sp.wait_ge(sems["rs_ready"], 1)
                        sp.dma_start(st_p[L, 4], SR[:, 3, :]).then_inc(s_stored, 16)
                sp.wait_ge(sems["dls_done"], 6)
                sp.dma_start(st_s[L, 5], SS[:, :, :]).then_inc(ss_stored, 16)
                sp.wait_ge(sems["rs_ready"], 2)
                sp.dma_start(st_p[L, 5], SR[:, 3, :]).then_inc(s_stored, 16)
                wait_full(sp, "o", 5, 1)
                sp.wait_ge(s_stored, 96)
                sp.dma_start(WO, wout[L].rearrange("p s n -> p s n")).then_inc(sems["wout_loaded"], 16)
                item(L, I_WQ - 1)
                sp.wait_ge(ss_stored, 96)
                for j in range(4):
                    sp.dma_start(LNP[:, j, :], lnp[L, j:j + 1, :].to_broadcast([128, D])) \
                        .then_inc(sems["lnp_loaded"], 16)
                for i in range(I_WQ, ITEMS):
                    item(L, i)
                for s in range(SLOTW):
                    sp.wait_ge(w_loaded[s], 16 * (ITEMS // SLOTW))
                sp.sem_inc(sems["layer_done"], 1)
                sp.wait_ge(sems["layer_done"], L * 5 + 5)
                sp.sem_inc(sems["all_arrived"], 1)
                for s in cleared:
                    sp.sem_clear(s)
                sp.sem_inc(sems["layer_go"], 1)
            sp.dma_start(y_out[0:NP].rearrange("(n p) d -> p n d", p=128), X[:, 0:4, :]) \
                .then_inc(sems["y_stored"], 16)
            sp.dma_start(y_out[NP:T], X[0:NS, 4, :]).then_inc(sems["y_stored"], 16)
            sp.wait_ge(sems["y_stored"], 32)

        @block.tensor
        def _(pe):
            def bank(*name):
                ring, j = JOB[name]
                if j >= 3:
                    pe.wait_ge(free[ring], j - 2)
                return BANKS[ring][j % 3]

            def done(last, *name):
                last.then_inc(full[JOB[name][0]], 1)

            def weights(i):
                pe.wait_ge(w_loaded[i % SLOTW], 16 * (i // SLOTW + 1))
                return WR[:, i % SLOTW, :]

            def consumed(last):
                last.then_inc(sems["w_consumed"], 1)

            def to_features(stage):
                for n in range(5):
                    w = WID[n]
                    if stage == 1:
                        pe.wait_ge(sems["x1_ready"], n + 1)
                    if stage == 2:
                        pe.wait_ge(sems["x2_ready"], n + 1)
                    for kg in range(2):
                        b = bank("xt", stage, n, kg)
                        for k in range(4):
                            last = nc.tensor.transpose(b[:, k * w:(k + 1) * w],
                                                       X[0:w, n, (4 * kg + k) * 128:(4 * kg + k + 1) * 128],
                                                       ident[0:w, 0:w])
                        done(last, "xt", stage, n, kg)
                wait_emptied(pe, "xt", stage, 4, 0)
                wait_emptied(pe, "xt", stage, 4, 1)

            def project(i, c, rhs, *name):
                w = weights(i).rearrange("p (k n) -> p k n", k=KT)
                for half in range(2):
                    b = bank(*name, half)
                    for k in range(KT):
                        last = nc.tensor.matmul(b[:, 0:HALF], w[:, k, c * 128:(c + 1) * 128],
                                                rhs[:, k, half * HALF:(half + 1) * HALF],
                                                start=(k == 0), stop=(k == KT - 1))
                    done(last, *name, half)
                return last

            pe.wait_ge(sems["consts_loaded"], 64)
            with pe.Fori(0, DEPTH) as L:
                to_features(0)
                for m, name in enumerate(FEATURES):
                    last = project(m // 2, m % 2, XT, "z", m)
                    if m % 2 or m == len(FEATURES) - 1:
                        pe.wait_ge(full["D"], JOB["z", m, 1][1] + 1)
                        pe.sem_inc(sems["w_consumed"], 1)
                    if name == "hq0":
                        pe.wait_ge(sems["small_loaded"], 16)
                        wait_emptied(pe, "z", 2, 0)
                        wait_emptied(pe, "z", 2, 1)
                        for g in range(2):
                            for half in range(2):
                                b = bank("ga", g, half)
                                done(nc.tensor.matmul(b[:, 0:HALF], SM[0:16, 12 + g * 128:12 + (g + 1) * 128],
                                                      T1[0:16, 0, half * HALF:(half + 1) * HALF],
                                                      start=True, stop=True), "ga", g, half)
                for i in range(4):
                    w = weights(I_V + i).rearrange("p (k n) -> p k n", k=KT)
                    for n in range(5):
                        b = bank("v", i, n)
                        for k in range(KT):
                            last = nc.tensor.matmul(b[0:WID[n], 0:256], XT[:, k, n * 128:n * 128 + WID[n]],
                                                    w[:, k, :], start=(k == 0), stop=(k == KT - 1))
                        done(last, "v", i, n)
                    pe.wait_ge(full["A"], JOB["v", i, 4][1] + 1)
                    pe.sem_inc(sems["w_consumed"], 1)
                wait_emptied(pe, "v", 3, 4)
                for s in range(4):
                    m = FEATURES.index(("rq0", "rq1", "rk0", "rk1")[s])
                    wait_emptied(pe, "z", m, 0)
                    wait_emptied(pe, "z", m, 1)
                    for half in range(2):
                        b = bank("rot", s, half)
                        done(nc.tensor.matmul(b[:, 0:HALF], const("perm"),
                                              Z[:, 12 + s, half * HALF:(half + 1) * HALF],
                                              start=True, stop=True), "rot", s, half)

                for f in range(6):
                    q, k = (8 + f, 4 + f) if f < 4 else (8 + f, 10 + f)
                    if f < 4:
                        b = bank("sc", f)[:, 0:128].rearrange("p (n i h) -> p n i h", n=4, h=2)
                        for iq in range(4):
                            step = 4 * f + iq
                            pe.wait_ge(sems["p_ready"], step + 1)
                            for n in range(4):
                                for i in range(4):
                                    last = nc.tensor.matmul(
                                        b[:, n, 4 * iq + i, :],
                                        P[:, step % 2, i, n * CT:(n + 1) * CT, :].rearrange("p c j -> p (c j)"),
                                        const("headsel"), start=True, stop=True)
                            if iq < 3:
                                last.then_inc(sems["p_used"], 1)
                        last.then_inc(full["D"], 1)
                    else:
                        if f == 4:
                            pe.wait_ge(sems["z_ready"], 1)
                        for h in range(2):
                            b = bank("rsc", f, h)
                            r = slice(h * 64, h * 64 + 64)
                            for n in range(4):
                                c = slice(n * 128, (n + 1) * 128)
                                last = nc.tensor.matmul(b[:, c], Z[r, k, c], Z[r, q, c], start=True, stop=True)
                            done(last, "rsc", f, h)
                    pe.wait_ge(sems["kq_ready"], f + 1)
                    b = bank("kt", f)
                    for n in range(4):
                        last = nc.tensor.transpose(b[:, n * 128:(n + 1) * 128], Z[:, k, n * 128:(n + 1) * 128],
                                                   ident)
                    done(last, "kt", f)
                    b = bank("kts", f)
                    done(nc.tensor.transpose(b[0:NS, 0:128], Z[:, k, NP:T], ident), "kts", f)
                    if f < 4:
                        for n in range(4):
                            pe.wait_ge(sems["km_ready"], 4 * f + n + 1)
                            for half in range(2):
                                b = bank("dl", f, n, half)[:, 0:384].rearrange("p (c v) -> p c v", c=4)
                                for c in range(4):
                                    for h in range(2):
                                        last = nc.tensor.matmul(
                                            b[h * 64:h * 64 + 64, c, 0:DV[f]],
                                            KM[:, n % 2, 4 * half + c, h * 64:h * 64 + 64],
                                            V[:, n, vcols(f, h)], start=True, stop=True)
                                done(last, "dl", f, n, half)
                    else:
                        pe.wait_ge(sems["km_ready"], 16 + f - 3)
                        b = bank("rdl", f)[:, 0:384].rearrange("p (c v) -> p c v", c=4)
                        for n in range(4):
                            for h in range(2):
                                last = nc.tensor.matmul(b[h * 64:h * 64 + 64, n, :],
                                                        KM[:, 0, n, h * 64:h * 64 + 64],
                                                        V[:, n, vcols(f, h)], start=True, stop=True)
                        done(last, "rdl", f)
                    pe.wait_ge(sems["kms_ready"], f + 1)
                    for half in range(2):
                        b = bank("dls", f, half)[:, 0:384].rearrange("p (c v) -> p c v", c=4)
                        for c in range(4):
                            for h in range(2):
                                last = nc.tensor.matmul(b[h * 64:h * 64 + 64, c, 0:DV[f]],
                                                        KMS[0:NS, 4 * half + c, h * 64:h * 64 + 64],
                                                        V[0:NS, 4, vcols(f, h)], start=True, stop=True)
                        done(last, "dls", f, half)
                    pe.wait_ge(sems["dls_done"], f + 1)
                    for h in range(2):
                        _, r0, rows = oplace(f, h)
                        r = slice(h * 64, h * 64 + 64)
                        b = bank("os", f, h)
                        for t in range(NS):
                            last = nc.tensor.matmul(b[r0:r0 + rows, t:t + 1], SS[r, t, 0:rows],
                                                    Z[r, q, NP + t:NP + t + 1], start=True, stop=True)
                        done(last, "os", f, h)
                    pe.wait_ge(sems["sct_ready"], f + 1)
                    if f < 4:
                        pe.wait_ge(sems["s_ready"], f + 1)
                    else:
                        pe.wait_ge(sems["rs_ready"], f - 3)
                    for h in range(2):
                        _, r0, rows = oplace(f, h)
                        r = slice(h * 64, h * 64 + 64)
                        b = bank("o", f, h)
                        step = CH if f < 4 else 128
                        for n in range(4):
                            chunks = [c for c in range(128 // step) if n or c]
                            last = nc.tensor.matmul(b[r0:r0 + rows, n * 128:(n + 1) * 128], V[:, n, vcols(f, h)],
                                                    SCT[:, h, n, :], start=True, stop=not chunks)
                            for c in chunks:
                                g = n * (128 // step) + c
                                state = S[r, g - 1, 0:rows] if f < 4 else SR[r, g - 1, 0:rows]
                                cols = slice(g * step, (g + 1) * step)
                                last = nc.tensor.matmul(b[r0:r0 + rows, cols], state, Z[r, q, cols],
                                                        start=False, stop=(c == chunks[-1]))
                        done(last, "o", f, h)

                for m in range(10):
                    last = project(I_GATE + m // 2, m % 2, XT, "g", m)
                    if m % 2:
                        pe.wait_ge(full["A"], JOB["g", m, 1][1] + 1)
                        pe.sem_inc(sems["w_consumed"], 1)
                wait_emptied(pe, "o", 5, 1)
                for s in range(4):
                    for half in range(2):
                        b = bank("mu", s, half)
                        done(nc.tensor.matmul(b[0:96, 0:HALF], const("onesg", 96),
                                              OT[0:96, 4 + s, half * HALF:(half + 1) * HALF],
                                              start=True, stop=True), "mu", s, half)
                for s in range(10):
                    rows = 96 if s < 8 else 128
                    pe.wait_ge(sems["sq_ready"], s + 1)
                    for half in range(2):
                        b = bank("ms", s, half)
                        done(nc.tensor.matmul(b[0:rows, 0:HALF], const("onesg" if s < 8 else "onesh", rows),
                                              SQ[0:rows, s % 2, half * HALF:(half + 1) * HALF],
                                              start=True, stop=True), "ms", s, half)
                pe.wait_ge(sems["on_ready"], 10)
                pe.wait_ge(sems["wout_loaded"], 16)
                for n in range(5):
                    for half in range(2):
                        b = bank("mix", n, half)
                        for s in range(10):
                            rows = 96 if s < 8 else 128
                            last = nc.tensor.matmul(b[0:WID[n], :], OT[0:rows, s, n * 128:n * 128 + WID[n]],
                                                    WO[0:rows, s, half * 512:(half + 1) * 512],
                                                    start=(s == 0), stop=(s == 9))
                        done(last, "mix", n, half)
                to_features(1)
                for m in range(16):
                    last = project(I_WQ + m // 2, m % 2, XT, "q", m)
                    if m % 2:
                        pe.wait_ge(full["D"], JOB["q", m, 1][1] + 1)
                        pe.sem_inc(sems["w_consumed"], 1)
                wait_emptied(pe, "q", 15, 0)
                wait_emptied(pe, "q", 15, 1)
                subs = [weights(I_SUB + i)[:, 0:1024].rearrange("p (s n) -> p s n", s=8) for i in range(2)]

                def scores(n):
                    for c in range(4):
                        b = bank("s", n, c)
                        for j in range(4):
                            hs = 4 * c + j
                            last = nc.tensor.matmul(b[0:WID[n], j * 128:(j + 1) * 128],
                                                    QT[:, hs, n * 128:n * 128 + WID[n]],
                                                    subs[hs // 8][:, hs % 8, :], start=True, stop=True)
                        done(last, "s", n, c)

                scores(4)
                pe.wait_ge(sems["et_ready"], 1)
                b = bank("et")
                done(nc.tensor.transpose(b[:, 0:NS], EF[0:NS].rearrange("p a b -> p (a b)"),
                                         ident[0:NS, 0:NS]), "et")
                b = bank("gt")
                done(nc.tensor.transpose(b[:, 0:NS], GATE[0:NS, 4, :], ident[0:NS, 0:NS]), "gt")
                scores(0)

                for n in range(4):
                    if n < 3:
                        scores(n + 1)
                    if n == 2:
                        wait_full(pe, "s", 3, 3)
                        pe.sem_inc(sems["w_consumed"], 2)
                    pe.wait_ge(sems["w_ready"], n + 1)
                    for half in range(2):
                        c = slice(half * 512, (half + 1) * 512)
                        nc.tensor.matmul(Y[:, c], const("aident", 64), X[0:64, n, c], start=True, stop=False)
                    with pe.Fori(0, NGRP) as g:
                        for k in range(RING):
                            pe.wait_ge(sems["diag_ready"], g * RING + (n * SLOTS + k + 1))
                            pe.wait_ge(fetched[k], L * (16 * USES) + g * 16 + 16 * (n * 2 * NGRP + NGRP + 1))
                            for half in range(2):
                                c = slice(half * 512, (half + 1) * 512)
                                last = nc.tensor.matmul(Y[:, c], DIAG[:, k, :], G[:, k, c],
                                                        start=False, stop=False)
                            last.then_inc(sems["v_used"], 1)
                    for half in range(2):
                        c = slice(half * 512, (half + 1) * 512)
                        last = nc.tensor.matmul(Y[:, c], const("aident")[64:128], X[64:128, n, c], start=False,
                                                stop=True)
                    last.then_inc(sems["acc_ready"], 1)
                pw = weights(I_PP).rearrange("p (k n) -> p k n", k=2)
                pt = weights(I_PT)[:, 0:2 * T].rearrange("p (k n) -> p k n", k=2)
                for half in range(2):
                    for n in range(5):
                        b = bank("pp", half, n)
                        for k in range(2):
                            last = nc.tensor.matmul(b[0:WID[n], :], pt[:, k, n * 128:n * 128 + WID[n]],
                                                    pw[:, k, half * 512:(half + 1) * 512],
                                                    start=(k == 0), stop=(k == 1))
                        done(last, "pp", half, n)
                wait_full(pe, "pp", 1, 4)
                pe.sem_inc(sems["w_consumed"], 2)
                pe.wait_ge(sems["x2_ready"], 4)
                for t in range(NS):
                    if t:
                        pe.wait_ge(sems["xb_used"], t)
                    for half in range(2):
                        c = slice(half * 512, (half + 1) * 512)
                        last = nc.tensor.matmul(Y[:, c], ident[0:NS, t:t + 1].to_broadcast([NS, 128]),
                                                X[0:NS, 4, c], start=True, stop=True)
                    last.then_inc(sems["xb_ready"], 1)
                pe.wait_ge(sems["wsam_ready"], 1)
                for half in range(2):
                    c = slice(half * 512, (half + 1) * 512)
                    nc.tensor.matmul(Y[0:NS, c], const("aident", NS)[:, 0:NS], X[0:NS, 4, c],
                                     start=True, stop=False)
                for t in range(NS):
                    pe.wait_ge(fetched[t], L * (16 * USES) + 16 * USES)
                    for half in range(2):
                        c = slice(half * 512, (half + 1) * 512)
                        last = nc.tensor.matmul(Y[0:NS, c], WS8[:, t, :], G[:, t, c], start=False,
                                                stop=(t == NS - 1))
                last.then_inc(sems["acc_ready"], 1)

                to_features(2)
                for c in range(4):
                    w = weights(I_PG + c).rearrange("p (k n) -> p k n", k=KT)
                    for n in range(5):
                        b = bank("pg", c, n)
                        for k in range(KT):
                            last = nc.tensor.matmul(b[0:WID[n], 0:256], XT[:, k, n * 128:n * 128 + WID[n]],
                                                    w[:, k, :], start=(k == 0), stop=(k == KT - 1))
                        done(last, "pg", c, n)
                arrive(pe, L)

        @block.gpsimd
        def _(pool):
            def fetch(L, n, phase, table):
                with pool.Fori(0, NGRP // 2) as gg:
                    for par in range(2):
                        nc.gpsimd.tensor_copy(IST[:, par, :], IDX[:, n, ds(gg * (2 * RING) + par * RING, RING)]) \
                            .then_inc(sems["idx_staged"], 1)
                        pool.wait_ge(sems["idx_staged"],
                                     gg * 2 + ((n * 2 + phase) * NGRP + par + 1))
                        for half in range(2):
                            upto = RING // 2 * (half + 1)
                            if phase == 0:
                                pool.wait_ge(sems["u_used"], gg * (2 * RING) + (n * SLOTS + par * RING + upto))
                                pool.wait_ge(sems["v_used"], n * SLOTS + upto)
                            else:
                                pool.wait_ge(sems["v_used"], gg * (2 * RING) + (n * SLOTS + par * RING + upto))
                                pool.wait_ge(sems["u_used"], (n + 1) * SLOTS + upto)
                            pool.sem_inc(sems["places_free"], 1)
                            for k in range(half * RING // 2, (half + 1) * RING // 2):
                                pool.indirect_dma_start(
                                    G[:, k, :], None, table,
                                    bass.IndirectOffsetOnAxis(ap=IST[:, par, k:k + 1], axis=0)) \
                                    .then_inc(fetched[k], 16)

            pool.wait_ge(sems["consts_loaded"], 64)
            with pool.Fori(0, DEPTH) as L:
                pool.sem_inc(sems["u_used"], RING)
                pool.sem_inc(sems["v_used"], RING)
                pool.wait_ge(sems["b_ready"], 1)
                for step in range(16):
                    f, iq = step // 4, step % 4
                    w = 4 * iq + 4
                    if step >= 2:
                        if (step - 2) % 4 == 3:
                            wait_full(pool, "sc", (step - 2) // 4)
                        else:
                            pool.wait_ge(sems["p_used"], (step - 2) - (step - 2) // 4 + 1)
                    b = Z[:, f, 0:NP].rearrange("p (c i) -> p c i", i=CH)
                    if w < CH:
                        nc.gpsimd.memset(P[:, step % 2, :, :, w:CH], 0.0)
                    for i in range(4):
                        at = 4 * iq + i
                        last = nc.gpsimd.tensor_tensor(P[:, step % 2, i, :, 0:w],
                                                       b[:, :, at:at + 1].to_broadcast([128, NC, w]),
                                                       b[:, :, 0:w], ALU.subtract)
                    last.then_inc(sems["diff_ready"], 1)
                for s in range(10):
                    rows = 96 if s < 8 else 128
                    if s >= 2:
                        wait_full(pool, "ms", s - 2, 1)
                    if s == 0:
                        wait_emptied(pool, "o", 5, 1)
                        wait_emptied(pool, "g", 9, 1)
                    if 4 <= s < 8:
                        pool.wait_ge(sems["mu_done"], s - 3)
                    nc.gpsimd.tensor_tensor(SQ[0:rows, s % 2, :], OT[0:rows, s, :], OT[0:rows, s, :], ALU.mult) \
                        .then_inc(sems["sq_ready"], 1)
                for n in range(4):
                    pool.wait_ge(sems["idx_ready"], n + 2)
                    fetch(L, n, 0, utab)
                    fetch(L, n, 1, vtab)
                for phase, table in ((0, utab), (1, vtab)):
                    for t in range(NS):
                        pool.wait_ge(sems["u_used"], RING + 4 * SLOTS + (t + 1) * phase)
                        pool.wait_ge(sems["v_used"], t + 1 + 4 * SLOTS)
                        pool.indirect_dma_start(G[:, t, :], None, table,
                                                bass.IndirectOffsetOnAxis(ap=IDXS[:, t:t + 1], axis=0)) \
                            .then_inc(fetched[t], 16)
                arrive(pool, L)

        @block.scalar
        def _(act):
            def emptied(ins, *name):
                ins.then_inc(free[JOB[name][0]], 1)

            def to_features(stage):
                for n in range(5):
                    w = WID[n]
                    b = wait_full(act, "xt", stage, n, 0)
                    emptied(nc.scalar.activation(XT[:, 0:4, n * 128:n * 128 + w],
                                                 b[:, 0:4 * w].rearrange("p (k t) -> p k t", k=4), ACT.Copy),
                            "xt", stage, n, 0)

            def rstd(n, count):
                w = WID[n]
                act.wait_ge(sems["mv_ready"], count)
                nc.scalar.activation(ST[0:w, n, 14:15], ST[0:w, n, 13:14], ACT.Ln, bias=const("eps", w))
                act.drain()
                nc.scalar.activation(ST[0:w, n, 15:16], ST[0:w, n, 14:15], ACT.Exp, scale=-0.5) \
                    .then_inc(sems["rstd_ready"], 1)

            def value(i, n):
                b = wait_full(act, "v", i, n)
                emptied(nc.scalar.activation(V[0:WID[n], n, i * 256:(i + 1) * 256], b[0:WID[n], 0:256],
                                             ACT.Copy), "v", i, n)

            act.wait_ge(sems["consts_loaded"], 64)
            act.wait_ge(sems["small_init"], 1)
            nc.scalar.activation(LB[:, 0:4], LB[:, 0:4], ACT.Exp).then_inc(sems["small_init"], 1)
            with act.Fori(0, DEPTH) as L:
                to_features(0)
                act.wait_ge(sems["lb_ready"], 1)
                nc.scalar.activation(LB[:, 10:14], LB[:, 6:10], ACT.Ln).then_inc(sems["lb_ready"], 1)
                for m, name in enumerate(FEATURES):
                    b = wait_full(act, "z", m, 0)
                    if name == "glr":
                        emptied(nc.scalar.activation(T1[0:16, 0, 0:HALF], b[0:16, 0:HALF], ACT.Copy), "z", m, 0)
                    else:
                        emptied(nc.scalar.activation(Z[:, ZSLOT[name], 0:HALF], b[:, 0:HALF], ACT.Copy,
                                                     scale=48 ** -0.5 if name[:2] == "gq" else 1.0), "z", m, 0)
                wait_emptied(act, "z", len(FEATURES) - 1, 1)
                act.drain()
                nc.scalar.activation(Z[:, 6:8, :], Z[:, 2:4, :], ACT.Sigmoid, scale=-1.0)
                nc.scalar.activation(Z[:, 10:12, :], Z[:, 10:12, :], ACT.Silu).then_inc(sems["sigm_ready"], 1)
                for n in range(5):
                    value(0, n)
                act.wait_ge(sems["abs_ready"], 1)
                nc.scalar.activation(T1, T1, ACT.Exp, scale=-1.0)
                act.drain()
                nc.scalar.activation(T2, T1, ACT.Ln, bias=1.0).then_inc(sems["log1p_ready"], 1)
                for n in range(5):
                    value(1, n)
                act.wait_ge(sems["hdiff_ready"], 1)
                nc.scalar.activation(T1[:, 0:2, :], T1[:, 0:2, :], ACT.Exp, scale=-1.0)
                act.drain()
                nc.scalar.activation(T2[:, 0:2, :], T1[:, 0:2, :], ACT.Ln, bias=1.0) \
                    .then_inc(sems["hlog_ready"], 1)
                for n in range(5):
                    value(2, n)
                act.wait_ge(sems["b_ready"], 1)
                nc.scalar.activation(DEC[:, :, 1:NC],
                                     Z[:, 0:4, 0:NP].rearrange("p f (c i) -> p f c i", i=CH)[:, :, 1:NC, CH - 1],
                                     ACT.Exp)
                nc.scalar.activation(DEC[:, :, NC:NC + NS], Z[:, 0:4, NP:T], ACT.Exp) \
                    .then_inc(sems["dec_ready"], 1)
                for n in range(5):
                    value(3, n)

                def pexp(step):
                    w = 4 * (step % 4) + 4
                    act.wait_ge(sems["min_ready"], step + 1)
                    p = P[:, step % 2, :, :, 0:w]
                    nc.scalar.activation(p, p, ACT.Exp).then_inc(sems["pexp_ready"], 1)

                def outputs(f):
                    if f < 4:
                        act.wait_ge(sems["ek_ready"], f + 1)
                        nc.scalar.activation(SCT, SCT, ACT.Exp).then_inc(sems["eq_ready"], 1)
                    if f < 4:
                        if f >= 1:
                            act.wait_ge(s_stored, 16 * f)
                        for n in range(4):
                            for half in range(2):
                                b = wait_full(act, "dl", f, n, half)
                                emptied(nc.scalar.activation(
                                    S[:, n * CT + 4 * half:n * CT + 4 * half + 4, 0:DV[f]],
                                    b[:, 0:384].rearrange("p (c v) -> p c v", c=4)[:, :, 0:DV[f]],
                                    ACT.Copy), "dl", f, n, half)
                    else:
                        if f == 5:
                            act.wait_ge(s_stored, 16 * f)
                        b = wait_full(act, "rdl", f)
                        emptied(nc.scalar.activation(SR, b[:, 0:384].rearrange("p (c v) -> p c v", c=4),
                                                     ACT.Copy), "rdl", f)
                    for kind, c0, c1 in (("os", NP, T), ("o", 0, NP)):
                        for h in range(2):
                            at, r0, rows = oplace(f, h)
                            b = wait_full(act, kind, f, h)
                            emptied(nc.scalar.activation(OT[r0:r0 + rows, at, c0:c1],
                                                         b[r0:r0 + rows, 0:c1 - c0], ACT.Copy), kind, f, h)

                for f in range(4):
                    for iq in range(4):
                        pexp(4 * f + iq)
                    outputs(f)
                outputs(4)
                outputs(5)
                for m in range(10):
                    for half in range(2):
                        b = wait_full(act, "g", m, half)
                        emptied(nc.scalar.activation(ZG[:, m, half * HALF:(half + 1) * HALF], b[:, 0:HALF],
                                                     ACT.Silu), "g", m, half)
                for s in range(10):
                    rows = 96 if s < 8 else 128
                    if s >= 2:
                        act.wait_ge(sems["on_ready"], s - 1)
                    for half in range(2):
                        b = wait_full(act, "ms", s, half)
                        emptied(nc.scalar.activation(RS[0:rows, s % 2, half * HALF:(half + 1) * HALF],
                                                     b[0:rows, 0:HALF], ACT.Ln, bias=const("eps", rows)),
                                "ms", s, half)
                    act.drain()
                    nc.scalar.activation(RS[0:rows, s % 2, :], RS[0:rows, s % 2, :], ACT.Exp, scale=-0.5) \
                        .then_inc(sems["rms_ready"], 1)
                for n in range(5):
                    rstd(n, n + 1)
                to_features(1)
                for m in range(16):
                    b = wait_full(act, "q", m, 0)
                    emptied(nc.scalar.activation(QT[:, m, 0:HALF], b[:, 0:HALF], ACT.Copy), "q", m, 0)
                def gates(n, count):
                    w = WID[n]
                    g = GATE[0:w, n, :]
                    act.wait_ge(sems["rprod_ready"], count)
                    nc.scalar.activation(g, g, ACT.Exp).then_inc(sems["silu_ready"], 1)

                gates(4, 1)
                gates(0, 2)
                for n in range(4):
                    act.wait_ge(sems["score_ready"], n + 1)
                    nc.scalar.activation(WGT, SCORE, ACT.Gelu).then_inc(sems["gelu_ready"], 1)
                    act.wait_ge(sems["w_ready"], n + 1)
                    with act.Fori(0, NGRP) as g:
                        act.wait_ge(sems["v_used"], g * RING + (n * SLOTS + RING))
                        for k in range(RING):
                            nc.scalar.activation(DIAG[:, k, :], ident, ACT.Copy,
                                                 scale=WGT[:, ds(g * RING + k, 1)]) \
                                .then_inc(sems["diag_ready"], 1)
                    if n < 3:
                        gates(n + 1, n + 3)
                    rstd(n, n + 6)
                for half in range(2):
                    for n in range(5):
                        b = wait_full(act, "pp", half, n)
                        emptied(nc.scalar.activation(PP[0:WID[n], n, half * 512:(half + 1) * 512],
                                                     b[0:WID[n], :], ACT.Copy), "pp", half, n)
                act.wait_ge(sems["score_ready"], 5)
                nc.scalar.activation(WS, SSC, ACT.Gelu).then_inc(sems["gelu_ready"], 1)
                rstd(4, 10)
                to_features(2)
                for c in range(4):
                    for n in range(5):
                        b = wait_full(act, "pg", c, n)
                        if c * 5 + n >= 5:
                            act.wait_ge(sems["x_ready"], c * 5 + n - 4)
                        emptied(nc.scalar.activation(SG[0:WID[n], n, :], b[0:WID[n], 0:256], ACT.Sigmoid),
                                "pg", c, n)
                arrive(act, L)

        @block.vector
        def _(dve):
            def emptied(ins, *name):
                ins.then_inc(free[JOB[name][0]], 1)

            def to_features(stage):
                for n in range(5):
                    w = WID[n]
                    b = wait_full(dve, "xt", stage, n, 1)
                    emptied(nc.vector.tensor_copy(XT[:, 4:8, n * 128:n * 128 + w],
                                                  b[:, 0:4 * w].rearrange("p (k t) -> p k t", k=4)),
                            "xt", stage, n, 1)

            def statistics(n, src):
                w = WID[n]
                for j in range(2):
                    nc.vector.bn_stats(ST[0:w, n, 6 * j:6 * j + 6], src[0:w, j * 512:(j + 1) * 512])
                dve.drain()
                nc.vector.bn_aggr(ST[0:w, n, 12:14], ST[0:w, n, 0:12].rearrange("p (a b) -> p a b", a=2)) \
                    .then_inc(sems["mv_ready"], 1)

            def normalize(n, src, which, count, signal):
                w = WID[n]
                dve.wait_ge(sems["rstd_ready"], count)
                x = X[0:w, n, :]
                nc.vector.tensor_scalar(x, src[0:w, :], ST[0:w, n, 12:13], ST[0:w, n, 15:16],
                                        ALU.subtract, ALU.mult)
                dve.drain()
                nc.vector.tensor_tensor(x, x, LNP[0:w, 2 * which, :], ALU.mult)
                dve.drain()
                return nc.vector.tensor_tensor(x, x, LNP[0:w, 2 * which + 1, :], ALU.add) \
                    .then_inc(sems[signal], 1)

            def top(n, count):
                w = WID[n]
                for c in range(4):
                    b = wait_full(dve, "s", n, c)
                    emptied(nc.vector.tensor_copy(SC[0:w, 4 * c:4 * c + 4, :],
                                                  b[0:w, :].rearrange("p (s n) -> p s n", s=4)), "s", n, c)
                dve.drain()

                def best16(src, count, vals, inds):
                    for part in range(2):
                        c = slice(part * 8, part * 8 + 8)
                        for s in range(count):
                            nc.vector.max(vals[0:w, s, c], src(s))
                        dve.drain()
                        for s in range(count):
                            nc.vector.max_index(inds[0:w, s, c], vals[0:w, s, c], src(s))
                        dve.drain()
                        if part == 0:
                            for s in range(count):
                                nc.vector.match_replace(src(s), vals[0:w, s, c], src(s), -3.0e38)
                            dve.drain()

                best16(lambda s: SC[0:w, s, :], 2 * PH, VV, II)
                nc.vector.tensor_copy(IF[0:w], II[0:w])
                v = VV[0:w].rearrange("p (h s) k -> p h s k", s=2)
                for h in range(PH):
                    nc.vector.tensor_tensor(CAND[0:w, h], v[:, h, 0, :].unsqueeze(2).to_broadcast([w, 16, 16]),
                                            v[:, h, 1, :].unsqueeze(1).to_broadcast([w, 16, 16]), ALU.add)
                dve.drain()
                best16(lambda h: CAND[0:w, h].rearrange("p a b -> p (a b)"), PH, BEST, CI)
                gate = GATE[0:w, n, :].rearrange("p (h k) -> p h k", k=TOPK)
                nc.vector.tensor_tensor(gate, BEST[0:w], BEST[0:w, :, 0:1].to_broadcast([w, PH, TOPK]),
                                        ALU.subtract).then_inc(sems["rprod_ready"], 1)
                nc.vector.tensor_single_scalar(CAB[0:w, 0], CI[0:w], 4, ALU.logical_shift_right)
                nc.vector.tensor_single_scalar(CAB[0:w, 1], CI[0:w], 15, ALU.bitwise_and)
                dve.drain()
                nc.vector.tensor_copy(ABF[0:w], CAB[0:w])
                dve.drain()
                for side in range(2):
                    ii = IF[0:w].rearrange("p (h s) k -> p h s k", s=2)[:, :, side, :]
                    for h in range(PH):
                        nc.vector.tensor_tensor(EQT[0:w, h], ABF[0:w, side, h].unsqueeze(2).to_broadcast([w, 16, 16]),
                                                iota16[0:w, :].unsqueeze(1).to_broadcast([w, 16, 16]),
                                                ALU.is_equal)
                    dve.drain()
                    for h in range(PH):
                        nc.vector.tensor_tensor(EQT[0:w, h], EQT[0:w, h],
                                                ii[:, h, :].unsqueeze(1).to_broadcast([w, 16, 16]), ALU.mult)
                    dve.drain()
                    nc.vector.tensor_reduce(SEL[0:w, side], EQT[0:w], AX.X, ALU.add)
                    dve.drain()
                nc.vector.scalar_tensor_tensor(out=EF[0:w], in0=SEL[0:w, 0], scalar=float(NKEY),
                                               in1=SEL[0:w, 1], op0=ALU.mult, op1=ALU.add)
                dve.drain()
                last = nc.vector.tensor_scalar(EF[0:w], EF[0:w], LBASE[0:w, 0:1], None, ALU.add)
                dve.drain()
                if n < 4:
                    nc.vector.tensor_copy(IDX[:, n, :], EF[:, :, :].rearrange("p a b -> p (a b)")) \
                        .then_inc(sems["idx_ready"], 1)
                dve.wait_ge(sems["silu_ready"], count)
                nc.vector.tensor_reduce(SUM[0:w, 0], gate, AX.X, ALU.add)
                dve.drain()
                nc.vector.reciprocal(SUM[0:w, 1], SUM[0:w, 0])
                dve.drain()
                last = nc.vector.tensor_tensor(gate, gate, SUM[0:w, 1].unsqueeze(2).to_broadcast([w, PH, TOPK]),
                                               ALU.mult)
                if n == 4:
                    last.then_inc(sems["et_ready"], 1)
                    b = wait_full(dve, "et")
                    emptied(nc.vector.tensor_copy(IDXS, b[:, 0:NS]), "et")
                    b = wait_full(dve, "gt")
                    emptied(nc.vector.tensor_copy(GATES, b[:, 0:NS]), "gt")
                    dve.drain()
                    dve.sem_inc(sems["idx_ready"], 1)

            iota16 = const("iota")
            dve.wait_ge(sems["consts_loaded"], 64)
            nc.vector.tensor_tensor(LB[:, 4:6], LB[:, 0:2], LB[:, 2:4], ALU.max)
            dve.drain()
            nc.vector.tensor_tensor(LB[:, 0:2], LB[:, 0:2], LB[:, 4:6], ALU.subtract)
            nc.vector.tensor_tensor(LB[:, 2:4], LB[:, 2:4], LB[:, 4:6], ALU.subtract).then_inc(sems["small_init"], 1)
            dve.wait_ge(sems["small_init"], 2)
            nc.vector.tensor_tensor(LB[:, 4:6], LB[:, 0:2], LB[:, 2:4], ALU.add)
            dve.drain()
            nc.vector.reciprocal(LB[:, 6:8], LB[:, 4:6])
            dve.drain()
            nc.vector.tensor_tensor(LB[:, 14:16], LB[:, 2:4], LB[:, 6:8], ALU.mult)
            nc.vector.memset(LB[:, 4:6], 0.0)
            nc.vector.memset(LBASE[:, :], 0.0)

            with dve.Fori(0, DEPTH) as L:
                dve.drain()
                nc.vector.tensor_scalar(LB[:, 6:8], LB[:, 4:6], 2.0 ** -63, None, ALU.max)
                nc.vector.tensor_scalar(LB[:, 8:10], LB[:, 4:6], -1.0, 1.0, ALU.mult, ALU.add)
                dve.drain()
                nc.vector.tensor_scalar(LB[:, 8:10], LB[:, 8:10], 2.0 ** -63, None, ALU.max)
                dve.drain().then_inc(sems["lb_ready"], 1)
                to_features(0)
                for m, name in enumerate(FEATURES):
                    b = wait_full(dve, "z", m, 1)
                    if name == "glr":
                        emptied(nc.vector.tensor_copy(T1[0:16, 0, HALF:T], b[0:16, 0:HALF]), "z", m, 1)
                    else:
                        emptied(nc.vector.tensor_scalar(Z[:, ZSLOT[name], HALF:T], b[:, 0:HALF],
                                                        48 ** -0.5 if name[:2] == "gq" else 1.0, None, ALU.mult),
                                "z", m, 1)
                    if name == "hq0":
                        for g in range(2):
                            for half in range(2):
                                b = wait_full(dve, "ga", g, half)
                                emptied(nc.vector.tensor_scalar(Z[:, g, half * HALF:(half + 1) * HALF],
                                                                b[:, 0:HALF], SM[:, g:g + 1], None, ALU.add),
                                        "ga", g, half)
                dve.wait_ge(sems["sigm_ready"], 1)
                nc.vector.scalar_tensor_tensor(out=T1, in0=Z[:, 0:4, :], scalar=-1.0, in1=Z[:, 0:4, :],
                                               op0=ALU.mult, op1=ALU.max).then_inc(sems["abs_ready"], 1)
                for h in range(2):
                    nc.vector.tensor_scalar(Z[:, 6 + h, :], Z[:, 6 + h, :], LB[:, 8 + h:9 + h], None, ALU.mult)
                dve.wait_ge(sems["log1p_ready"], 1)
                nc.vector.scalar_tensor_tensor(out=Z[:, 0:4, :], in0=Z[:, 0:4, :], scalar=0.0, in1=T2,
                                               op0=ALU.min, op1=ALU.subtract)
                dve.wait_ge(sems["lb_ready"], 2)
                dve.drain()
                nc.vector.tensor_scalar(Z[:, 0:2, :], Z[:, 0:2, :], 1.0 / 16.0, None, ALU.mult)
                for h in range(2):
                    nc.vector.tensor_scalar(Z[:, 2 + h, :], Z[:, 2 + h, :], LB[:, 12 + h:13 + h], None, ALU.add)
                dve.drain()
                for h in range(2):
                    nc.vector.tensor_scalar(T1[:, h, :], Z[:, 2 + h, :], LB[:, 10 + h:11 + h], None, ALU.subtract)
                dve.drain()
                nc.vector.scalar_tensor_tensor(out=T1[:, 0:2, :], in0=T1[:, 0:2, :], scalar=-1.0,
                                               in1=T1[:, 0:2, :], op0=ALU.mult, op1=ALU.max).then_inc(sems["hdiff_ready"], 1)
                dve.wait_ge(sems["hlog_ready"], 1)
                for h in range(2):
                    nc.vector.scalar_tensor_tensor(out=Z[:, 2 + h, :], in0=Z[:, 2 + h, :],
                                                   scalar=LB[:, 10 + h:11 + h], in1=T2[:, h, :],
                                                   op0=ALU.max, op1=ALU.add)
                dve.drain()
                for f in range(4):
                    last = nc.vector.tensor_tensor_scan(Z[:, f, :], const("chunkmask"), Z[:, f, :], 0.0,
                                                        ALU.mult, ALU.add)
                last.then_inc(sems["b_ready"], 1)
                for s in range(4):
                    scale = 1.0 if s < 2 else 48 ** -0.5
                    for half in range(2):
                        c = slice(half * HALF, (half + 1) * HALF)
                        b = wait_full(dve, "rot", s, half)
                        emptied(nc.vector.scalar_tensor_tensor(out=ROT[:, half, :], in0=b[:, 0:HALF], scalar=scale,
                                                               in1=const("sin")[:, c], op0=ALU.mult,
                                                               op1=ALU.mult), "rot", s, half)
                        nc.vector.scalar_tensor_tensor(out=Z[:, 12 + s, c], in0=Z[:, 12 + s, c], scalar=scale,
                                                       in1=const("cos")[:, c], op0=ALU.mult, op1=ALU.mult)
                        dve.drain()
                        last = nc.vector.tensor_tensor(Z[:, 12 + s, c], Z[:, 12 + s, c], ROT[:, half, :], ALU.add)
                        if s == 3 and half == 1:
                            last.then_inc(sems["z_ready"], 1)

                def low(step):
                    iq = step % 4
                    w = 4 * iq + 4
                    dve.wait_ge(sems["diff_ready"], step + 1)
                    m = const("causal").rearrange("p (i j) -> p i j", j=CH)
                    for i in range(4):
                        p = P[:, step % 2, i, :, 0:w]
                        last = nc.vector.tensor_tensor(
                            p, p, m[:, 4 * iq + i:4 * iq + i + 1, 0:w].to_broadcast([128, NC, w]), ALU.min)
                    last.then_inc(sems["min_ready"], 1)

                def products(step):
                    f, iq = step // 4, step % 4
                    w = 4 * iq + 4
                    dve.wait_ge(sems["pexp_ready"], step + 1)
                    kk = Z[:, 4 + f, 0:NP].rearrange("p (c j) -> p c j", j=CH)
                    qq = Z[:, 8 + f, 0:NP].rearrange("p (c i) -> p c i", i=CH)
                    for i in range(4):
                        p = P[:, step % 2, i, :, 0:w]
                        nc.vector.tensor_tensor(p, p, kk[:, :, 0:w], ALU.mult)
                    dve.drain()
                    for i in range(4):
                        p = P[:, step % 2, i, :, 0:w]
                        at = 4 * iq + i
                        last = nc.vector.tensor_tensor(p, p, qq[:, :, at:at + 1].to_broadcast([128, NC, w]),
                                                       ALU.mult)
                    last.then_inc(sems["p_ready"], 1)

                def keys_and_states(f):
                    k = 4 + f if f < 4 else 10 + f
                    mask = const("mask16")
                    b = wait_full(dve, "kt", f)
                    for n in range(4):
                        if f < 4:
                            if 4 * f + n >= 2:
                                g = 4 * f + n - 2
                                wait_full(dve, "dl", g // 4, g % 4, 1)
                            last = nc.vector.tensor_tensor(
                                KM[:, n % 2], b[:, n * 128:(n + 1) * 128].unsqueeze(1).to_broadcast([128, CT, 128]),
                                mask.unsqueeze(2).to_broadcast([128, CT, 128]), ALU.mult)
                            last.then_inc(sems["km_ready"], 1)
                    if f < 4:
                        dve.wait_ge(sems["km_ready"], 4 * f + 4)
                        dve.sem_inc(free["D"], 1)
                    else:
                        if f == 4:
                            wait_full(dve, "dl", 3, 3, 1)
                        else:
                            wait_full(dve, "rdl", 4)
                        last = nc.vector.tensor_copy(KM[:, 0, 0:4, :], b[:, :].rearrange("p (n d) -> p n d", n=4))
                        emptied(last, "kt", f)
                        dve.wait_ge(free["D"], JOB["kt", f][1] + 1)
                        dve.sem_inc(sems["km_ready"], 1)
                    b = wait_full(dve, "kts", f)
                    if f:
                        wait_full(dve, "dls", f - 1, 1)
                    emptied(nc.vector.tensor_tensor(
                        KMS[0:NS], b[0:NS, 0:128].unsqueeze(1).to_broadcast([NS, NS, 128]),
                        ident[0:NS, 0:NS].unsqueeze(2).to_broadcast([NS, NS, 128]), ALU.mult), "kts", f)
                    wait_emptied(dve, "kts", f)
                    dve.sem_inc(sems["kms_ready"], 1)
                    dve.wait_ge(ss_loaded, 16 * (f + 1))
                    if f < 4:
                        nc.vector.tensor_tensor(SS[:, :, 0:DV[f]], SS[:, :, 0:DV[f]],
                                                DEC[:, f, NC:NC + NS].unsqueeze(2).to_broadcast([128, NS, DV[f]]),
                                                ALU.mult)
                    else:
                        nc.vector.tensor_scalar(SS[:, :, :], SS[:, :, :], const("gam")[:, f - 4:f - 3], None,
                                                ALU.mult)
                    dve.drain()
                    for half in range(2):
                        b = wait_full(dve, "dls", f, half)
                        ss = SS[:, 4 * half:4 * half + 4, 0:DV[f]]
                        emptied(nc.vector.tensor_tensor(
                            ss, ss, b[:, 0:384].rearrange("p (c v) -> p c v", c=4)[:, :, 0:DV[f]], ALU.add),
                            "dls", f, half)
                    wait_emptied(dve, "dls", f, 1)
                    dve.sem_inc(sems["dls_done"], 1)
                    if f < 4:
                        wait_emptied(dve, "dl", f, 3, 1)
                        for c in range(1, NC):
                            last = nc.vector.scalar_tensor_tensor(
                                out=S[:, c, 0:DV[f]], in0=S[:, c - 1, 0:DV[f]], scalar=DEC[:, f, c:c + 1],
                                in1=S[:, c, 0:DV[f]], op0=ALU.mult, op1=ALU.add)
                            if c < NC - 1:
                                dve.drain()
                        last.then_inc(sems["s_ready"], 1)
                    else:
                        wait_emptied(dve, "rdl", f)
                        for n in range(1, 4):
                            last = nc.vector.scalar_tensor_tensor(
                                out=SR[:, n, :], in0=SR[:, n - 1, :], scalar=const("g128")[:, f - 4:f - 3],
                                in1=SR[:, n, :], op0=ALU.mult, op1=ALU.add)
                            if n < 3:
                                dve.drain()
                        last.then_inc(sems["rs_ready"], 1)

                dve.wait_ge(sems["dec_ready"], 1)
                low(0)
                for f in range(4):
                    for iq in range(4):
                        step = 4 * f + iq
                        if iq < 3:
                            low(step + 1)
                        products(step)
                    if f:
                        wait_full(dve, "o", f - 1, 1)
                    q, k, bb = Z[:, 8 + f, 0:NP], Z[:, 4 + f, 0:NP], Z[:, f, 0:NP]
                    qx = SCT[:, 0].rearrange("p n t -> p (n t)")
                    kx = SCT[:, 1].rearrange("p n t -> p (n t)")
                    nc.vector.tensor_copy(qx, bb)
                    b3 = bb.rearrange("p (c i) -> p c i", i=CH)
                    nc.vector.tensor_tensor(kx.rearrange("p (c i) -> p c i", i=CH),
                                            b3[:, :, CH - 1:CH].to_broadcast([128, NC, CH]), b3, ALU.subtract) \
                        .then_inc(sems["ek_ready"], 1)
                    dve.wait_ge(sems["eq_ready"], f + 1)
                    nc.vector.tensor_tensor(q, q, qx, ALU.mult)
                    nc.vector.tensor_tensor(k, k, kx, ALU.mult).then_inc(sems["kq_ready"], 1)
                    b = wait_full(dve, "sc", f)[:, 0:128].rearrange("p (n i h) -> p n i h", n=4, h=2)
                    dve.wait_ge(sems["kq_ready"], f + 1)
                    for h in range(2):
                        for n in range(4):
                            last = nc.vector.tensor_tensor(
                                SCT[:, h, n, :].rearrange("p (c i) -> p c i", i=CH),
                                b[:, n, :, h].unsqueeze(1).to_broadcast([128, CT, CH]),
                                const("mask16").unsqueeze(2).to_broadcast([128, CT, CH]), ALU.mult)
                    last.then_inc(free["D"], 1)
                    wait_emptied(dve, "sc", f)
                    dve.sem_inc(sems["sct_ready"], 1)
                    keys_and_states(f)
                    if f < 3:
                        low(4 * f + 4)
                for f in (4, 5):
                    wait_full(dve, "o", f - 1, 1)
                    for h in range(2):
                        b = wait_full(dve, "rsc", f, h)
                        dm = const("dmat").rearrange("p (h i) -> p h i", h=4)[:, 2 * (f - 4) + h, :]
                        emptied(nc.vector.tensor_tensor(SCT[:, h], b[:, :].rearrange("p (n i) -> p n i", n=4),
                                                        dm.unsqueeze(1).to_broadcast([128, 4, 128]), ALU.mult),
                                "rsc", f, h)
                    wait_emptied(dve, "rsc", f, 1)
                    dve.sem_inc(sems["sct_ready"], 1)
                    for at, table in ((8 + f, "rqdec"), (10 + f, "rkdec")):
                        z = Z[:, at, 0:NP].rearrange("p (n i) -> p n i", n=4)
                        t = const(table).rearrange("p (f i) -> p f i", f=2)[:, f - 4, :]
                        last = nc.vector.tensor_tensor(z, z, t.unsqueeze(1).to_broadcast([128, 4, 128]), ALU.mult)
                    last.then_inc(sems["kq_ready"], 1)
                    keys_and_states(f)

                for s in range(4):
                    for half in range(2):
                        b = wait_full(dve, "mu", s, half)
                        o = OT[0:96, 4 + s, half * HALF:(half + 1) * HALF]
                        last = nc.vector.tensor_tensor(o, o, b[0:96, 0:HALF], ALU.subtract)
                        emptied(last, "mu", s, half)
                    wait_emptied(dve, "mu", s, 1)
                    dve.sem_inc(sems["mu_done"], 1)
                for s in range(10):
                    rows = 96 if s < 8 else 128
                    o = OT[0:rows, s, :]
                    dve.wait_ge(sems["rms_ready"], s + 1)
                    nc.vector.scalar_tensor_tensor(out=o, in0=o, scalar=SM[0:rows, 2 + s:3 + s],
                                                   in1=RS[0:rows, s % 2, :], op0=ALU.mult, op1=ALU.mult)
                    dve.drain()
                    nc.vector.tensor_tensor(o, o, ZG[0:rows, s, :], ALU.mult).then_inc(sems["on_ready"], 1)
                dve.wait_ge(sems["lnp_loaded"], 64)
                for n in range(5):
                    w = WID[n]
                    for half in range(2):
                        c = slice(half * 512, (half + 1) * 512)
                        b = wait_full(dve, "mix", n, half)
                        emptied(nc.vector.scalar_tensor_tensor(out=X[0:w, n, c], in0=X[0:w, n, c], scalar=ALPHA,
                                                               in1=b[0:w, :], op0=ALU.mult, op1=ALU.add),
                                "mix", n, half)
                    dve.drain()
                    statistics(n, X[:, n, :])
                    if n:
                        normalize(n - 1, X[:, n - 1, :], 0, n, "x1_ready")
                normalize(4, X[:, 4, :], 0, 5, "x1_ready")
                to_features(1)
                for m in range(16):
                    b = wait_full(dve, "q", m, 1)
                    emptied(nc.vector.tensor_copy(QT[:, m, HALF:T], b[:, 0:HALF]), "q", m, 1)
                top(4, 1)
                top(0, 2)
                for n in range(4):
                    with dve.Fori(0, NGRP) as g:
                        for k in range(RING):
                            dve.wait_ge(fetched[k], L * (16 * USES) + g * 16 + 16 * (n * 2 * NGRP + 1))
                            nc.vector.scalar_tensor_tensor(
                                out=G[:, k, :], in0=G[:, k, :], scalar=1.0, in1=X[:, n, :], op0=ALU.mult,
                                op1=ALU.mult, accum_out=SCORE[:, ds(g * RING + k, 1)]) \
                                .then_inc(sems["u_used"], 1)
                    dve.drain().then_inc(sems["score_ready"], 1)
                    dve.wait_ge(sems["gelu_ready"], n + 1)
                    nc.vector.tensor_tensor(WGT, WGT, GATE[:, n, :], ALU.mult).then_inc(sems["w_ready"], 1)
                    if n < 3:
                        top(n + 1, n + 3)
                    dve.wait_ge(sems["acc_ready"], n + 1)
                    statistics(n, Y)
                    normalize(n, Y, 1, n + 6, "x2_ready")
                    dve.wait_ge(sems["x2_ready"], n + 1)
                for t in range(NS):
                    dve.wait_ge(fetched[t], L * (16 * USES) + 16 * (USES - 1))
                    dve.wait_ge(sems["xb_ready"], t + 1)
                    nc.vector.scalar_tensor_tensor(out=G[:, t, :], in0=G[:, t, :], scalar=1.0, in1=Y[:, :],
                                                   op0=ALU.mult, op1=ALU.mult, accum_out=SSC[:, t:t + 1]) \
                        .then_inc(sems["u_used"], 1)
                    dve.wait_ge(sems["u_used"], RING + 4 * SLOTS + t + 1)
                    dve.sem_inc(sems["xb_used"], 1)
                dve.drain().then_inc(sems["score_ready"], 1)
                dve.wait_ge(sems["gelu_ready"], 5)
                nc.vector.tensor_tensor(WS, WS, GATES, ALU.mult)
                dve.drain()
                nc.vector.tensor_tensor(WS8, WS.unsqueeze(2).to_broadcast([128, NS, NS]),
                                        const("eye8").rearrange("p (a b) -> p a b", a=8), ALU.mult) \
                    .then_inc(sems["wsam_ready"], 1)
                dve.wait_ge(sems["acc_ready"], 5)
                statistics(4, Y)
                normalize(4, Y, 1, 10, "x2_ready")
                to_features(2)
                for c in range(4):
                    for n in range(5):
                        w = WID[n]
                        wait_emptied(dve, "pg", c, n)
                        sg, cc = SG[0:w, n, :], slice(c * 256, (c + 1) * 256)
                        nc.vector.tensor_tensor(sg, sg, PP[0:w, n, cc], ALU.mult)
                        dve.drain()
                        nc.vector.tensor_tensor(X[0:w, n, cc], X[0:w, n, cc], sg, ALU.add) \
                            .then_inc(sems["x_ready"], 1)
                nc.vector.tensor_scalar(LBASE[:, :], LBASE[:, :], float(NEXP), None, ALU.add)
                nc.vector.tensor_copy(LB[:, 4:6], LB[:, 14:16])
                arrive(dve, L)


def kernel(x_prompt, x_sample, p_prompt, p_sample, state_gla, state_ret, state_hgrn,
           w_in, gla_w_gate, gla_b_gate, gla_norm, ret_norm, hgrn_lb_logits, hgrn_norm, w_out,
           ln1_g, ln1_b, ln2_g, ln2_b, peer_w_q, peer_subkeys, peer_u, peer_v, ple_proj, ple_gate):
    import numpy as np
    import concourse.bacc as bacc
    from concourse.bass_utils import run_bass_kernel_spmd

    f32 = np.float32
    cols = {n: np.zeros((128, w), f32) for n, (_, w) in CONSTS.items()}
    p = np.arange(128)
    cols["ident"][:] = np.eye(128)
    cols["aident"][:] = np.eye(128) * ALPHA
    cols["onesg"][:96] = f32(1 / 96)
    cols["onesh"][:] = (p[:, None] // 64 == p[None] // 64) / 64
    cols["headsel"][:] = p[:, None] // 64 == np.arange(2)
    cols["mask16"][:] = p[:, None] // CH == np.arange(CT)
    cols["causal"][:] = np.where(np.arange(CH)[:, None] >= np.arange(CH)[None], 0.0, -1e30).reshape(1, -1)
    cols["eye8"][:] = np.eye(8).reshape(1, 64)
    cols["eps"][:] = EPS
    cols["iota"][:] = np.arange(16)
    t = np.arange(T)
    cols["chunkmask"][:] = (t < NP) & (t % CH != 0)
    inv = (f32(1) / (f32(10000.0) ** (np.arange(0, 48, 2, dtype=f32) / f32(48)))).astype(f32)
    pos = np.where(t < NP, t, 4096).astype(f32)
    ang = pos[None, :] * inv[:, None]
    gamma = np.log1p(-np.exp2(-5.0 - np.arange(4)))
    for h in range(2):
        for i in range(24):
            a, b = 64 * h + i, 64 * h + 24 + i
            cols["perm"][a, b] = cols["perm"][b, a] = 1
            cols["cos"][a] = cols["cos"][b] = np.cos(ang[i])
            cols["sin"][a], cols["sin"][b] = -np.sin(ang[i]), np.sin(ang[i])
    i = np.arange(128)
    for h in range(4):
        f, rows = h // 2, slice(64 * (h % 2), 64 * (h % 2) + 64)
        dist = i[None, :] - i[:, None]
        cols["dmat"][:, h * 128:(h + 1) * 128] = np.where(dist >= 0, np.exp(gamma[h] * np.maximum(dist, 0)), 0)
        cols["rqdec"][rows, f * 128:(f + 1) * 128] = np.exp(gamma[h] * (i + 1))
        cols["rkdec"][rows, f * 128:(f + 1) * 128] = np.exp(gamma[h] * (127 - i))
        cols["g128"][rows, f] = np.exp(gamma[h] * 128)
        cols["gam"][rows, f] = np.exp(gamma[h])
    consts = np.concatenate(list(cols.values()), axis=1)

    def arr(a):
        return np.ascontiguousarray(a)

    w_in, w_out = arr(w_in), arr(w_out)

    def pairs(at, width, f):
        out = np.zeros((DEPTH, D, 128), f32)
        for h in range(2):
            o = at + (2 * f + h) * width
            out[:, :, 64 * h:64 * h + width] = w_in[:, :, o:o + width]
        return out

    def wide(at, width, count):
        out = np.zeros((DEPTH, D, 128), f32)
        out[:, :, :width] = w_in[:, :, at:at + width]
        return out

    tiles = {"hf0": pairs(2576, 64, 0), "hf1": pairs(2576, 64, 1), "glr": wide(1152, 16, 1),
             "hq0": pairs(2320, 64, 0), "hq1": pairs(2320, 64, 1), "gk0": pairs(192, 48, 0),
             "gk1": pairs(192, 48, 1), "gq0": pairs(0, 48, 0), "gq1": pairs(0, 48, 1),
             "rq0": pairs(1168, 48, 0), "rq1": pairs(1168, 48, 1), "rk0": pairs(1360, 48, 0),
             "rk1": pairs(1360, 48, 1)}
    feat = np.concatenate([tiles[n] for n in FEATURES] + [np.zeros((DEPTH, D, 128), f32)], axis=2)
    vals = np.concatenate([w_in[:, :, 384:768], w_in[:, :, 1552:1936], w_in[:, :, 2832:3088]], axis=2)
    gate = np.concatenate([wide(768 + 96 * h, 96, 1) for h in range(4)]
                          + [wide(1936 + 96 * h, 96, 1) for h in range(4)]
                          + [pairs(3088, 64, 0), pairs(3088, 64, 1)], axis=2)
    ws = np.zeros((DEPTH, ITEMS, 128, 2048), f32)

    def put(first, m):
        n = m.shape[2] // 256
        v = m.reshape(DEPTH, KT, 128, n, 256).transpose(0, 3, 2, 1, 4)
        ws[:, first:first + n] = v.reshape(DEPTH, n, 128, 2048)

    put(0, feat)
    put(I_V, vals)
    put(I_GATE, gate)
    put(I_WQ, arr(peer_w_q))
    put(I_PG, arr(ple_gate))
    sub = arr(peer_subkeys).reshape(DEPTH, 16, 128, 128).transpose(0, 3, 1, 2)
    ws[:, I_SUB, :, :1024] = sub[:, :, :8].reshape(DEPTH, 128, 1024)
    ws[:, I_SUB + 1, :, :1024] = sub[:, :, 8:].reshape(DEPTH, 128, 1024)
    ws[:, I_PP] = arr(ple_proj).reshape(DEPTH, 2, 128, D).transpose(0, 2, 1, 3).reshape(DEPTH, 128, 2048)
    pt = np.concatenate([arr(p_prompt).reshape(DEPTH, NP, 256), arr(p_sample).reshape(DEPTH, NS, 256)], axis=1)
    pt = pt.transpose(0, 2, 1).reshape(DEPTH, 2, 128, T).transpose(0, 2, 1, 3)
    ws[:, I_PT, :, :2 * T] = pt.reshape(DEPTH, 128, 2 * T)
    wo = np.zeros((DEPTH, 128, 10, D), f32)
    for h in range(8):
        wo[:, :96, h] = w_out[:, 96 * h:96 * h + 96]
    wo[:, :, 8], wo[:, :, 9] = w_out[:, 768:896], w_out[:, 896:1024]
    small = np.zeros((DEPTH, 128, NSMALL), f32)
    for f in range(2):
        for h in range(2):
            c = slice((2 * f + h) * 48, (2 * f + h + 1) * 48)
            small[:, 64 * h:64 * h + 48, f] = arr(gla_b_gate)[:, c]
            small[:, :16, 12 + f * 128 + 64 * h:12 + f * 128 + 64 * h + 48] = arr(gla_w_gate)[:, :, c]
    small[:, :96, 2:6] = arr(gla_norm).transpose(0, 2, 1)
    small[:, :96, 6:10] = arr(ret_norm).transpose(0, 2, 1)
    small[:, :, 10:12] = arr(hgrn_norm).reshape(DEPTH, 2, 128).transpose(0, 2, 1)
    lnp = np.stack([arr(a) for a in (ln1_g, ln1_b, ln2_g, ln2_b)], axis=1)
    lblog = arr(arr(hgrn_lb_logits).reshape(DEPTH, 2, 128).transpose(2, 0, 1).reshape(128, 4))
    st_in = np.zeros((DEPTH, 6, 128, NS, 96), f32)
    places = ((arr(state_gla), 0, 48, 96), (arr(state_hgrn), 2, 64, 64), (arr(state_ret), 4, 48, 96))
    for state, f0, dk, dv in places:
        for h in range(4):
            st_in[:, f0 + h // 2, 64 * (h % 2):64 * (h % 2) + dk, :, :dv] = state[:, :, h].transpose(0, 2, 1, 3)
    x = np.concatenate([arr(x_prompt).reshape(NP, D), arr(x_sample).reshape(NS, D)])
    u, v = arr(peer_u).reshape(DEPTH * NEXP, D), arr(peer_v).reshape(DEPTH * NEXP, D)

    nc = bacc.Bacc("TRN2", target_bir_lowering=False, num_devices=1)
    arrays = {"x": x, "wstream": ws, "wout": wo, "small": small, "lnp": lnp, "lblog": lblog, "st_in": st_in,
              "consts": consts, "utab": u, "vtab": v}
    outs = {"y": (T, D), "st_p": (DEPTH, 6, 128, 96), "st_s": (DEPTH, 6, 128, NS, 96)}
    fp32 = mybir.dt.float32
    args = [nc.dram_tensor(f"in_{n}", a.shape, fp32, kind="ExternalInput").ap() for n, a in arrays.items()]
    args += [nc.dram_tensor(f"out_{n}", s, fp32, kind="ExternalOutput").ap() for n, s in outs.items()]
    build(nc, *args)
    r = run_bass_kernel_spmd(nc, [{f"in_{n}": a for n, a in arrays.items()}], core_ids=[0]).results[0]
    y, st_p, st_s = (r[f"out_{n}"] for n in outs)

    def heads(st, f0, dk, dv):
        return np.stack([st[:, f0 + h // 2, 64 * (h % 2):64 * (h % 2) + dk, ..., :dv] for h in range(4)], axis=2)

    new_p, new_s = [], []
    for f0, dk, dv in ((0, 48, 96), (4, 48, 96), (2, 64, 64)):
        new_p.append(heads(st_p, f0, dk, dv).transpose(0, 2, 1, 3)[:, None])
        new_s.append(heads(st_s, f0, dk, dv).transpose(0, 3, 2, 1, 4))
    return (y[:NP].reshape(1, NP, D), y[NP:].reshape(NS, 1, D), *map(arr, new_p), *map(arr, new_s))
```

```python
import concourse.bass as bass
from concourse import mybir
from contextlib import ExitStack

D, T, NP, NS = 1024, 520, 512, 8
WID = [128, 128, 128, 128, 8]
KT = D // 128
HALF = T // 2
CH = 16
NC = NP // CH
CT = 128 // CH
DEPTH = 2
ALPHA = (2 * DEPTH) ** 0.25
EPS = 1e-5
PH, TOPK, NKEY = 8, 16, 128
SLOTS = PH * TOPK
NEXP = NKEY * NKEY
RING = 8
NGRP = SLOTS // RING
USES = 2 * 4 * NGRP + 2
GPH = TOPK // RING
PE_ROWS, DVE_ROWS = [0, 1, 2, 4, 5, 6], [3, 7]
PEG, DVG = len(PE_ROWS), len(DVE_ROWS)
DV = [96, 96, 64, 64, 96, 96]
VCOL = [0, 192, 768, 896, 384, 576]
ITEMS, SLOTW = 32, 4

FEATURES = ["hf0", "hf1", "glr", "hq0", "hq1", "gk0", "gk1", "gq0", "gq1", "rq0", "rq1", "rk0", "rk1"]
ZSLOT = {"hf0": 2, "hf1": 3, "hq0": 10, "hq1": 11, "gk0": 4, "gk1": 5, "gq0": 8, "gq1": 9,
         "rq0": 12, "rq1": 13, "rk0": 14, "rk1": 15}
I_V, I_GATE, I_WQ, I_SUB, I_PP, I_PT, I_PG = 7, 11, 16, 24, 26, 27, 28

CONSTS = {}
_at = 0
for _n, _w in (("ident", 128), ("perm", 128), ("onesg", 96), ("onesh", 128), ("dmat", 512), ("cos", 520),
               ("sin", 520), ("chunkmask", 520), ("mask16", 8), ("causal", 256), ("rqdec", 256),
               ("rkdec", 256), ("headsel", 2), ("g128", 2), ("gam", 2), ("eye8", 64), ("eps", 1),
               ("aident", 128), ("iota", 16)):
    CONSTS[_n] = (_at, _w)
    _at += _w
NCONST = _at
NSMALL = 268


def jobs():
    found, count = {}, {"A": 0, "D": 0}

    def add(ring, *name):
        found[name] = (ring, count[ring])
        count[ring] += 1

    def to_features(stage):
        for n in range(5):
            add("A", "xt", stage, n, 0)
            add("D", "xt", stage, n, 1)

    to_features(0)
    for m, name in enumerate(FEATURES):
        add("A", "z", m, 0)
        add("D", "z", m, 1)
        if name == "hq0":
            for g in range(2):
                for half in range(2):
                    add("D", "ga", g, half)
    for i in range(4):
        for n in range(5):
            add("A", "v", i, n)
    for s in range(4):
        for half in range(2):
            add("D", "rot", s, half)
    for f in range(6):
        if f < 4:
            add("D", "sc", f)
        else:
            add("D", "rsc", f, 0)
            add("D", "rsc", f, 1)
        add("D", "kt", f)
        add("D", "kts", f)
        if f < 4:
            for n in range(4):
                for half in range(2):
                    add("A", "dl", f, n, half)
        else:
            add("A", "rdl", f)
        for half in range(2):
            add("D", "dls", f, half)
        for h in range(2):
            add("A", "os", f, h)
        for h in range(2):
            add("A", "o", f, h)
    for m in range(10):
        for half in range(2):
            add("A", "g", m, half)
    for s in range(4):
        for half in range(2):
            add("D", "mu", s, half)
    for s in range(10):
        for half in range(2):
            add("A", "ms", s, half)
    for n in range(5):
        for half in range(2):
            add("D", "mix", n, half)
    to_features(1)
    for m in range(16):
        add("A", "q", m, 0)
        add("D", "q", m, 1)
    for n in range(5):
        for c in range(4):
            add("A", "s", n, c)
    for n in range(5):
        for half in range(2):
            add("A", "pp", n, half)
    add("D", "et")
    add("D", "gt")
    for n in range(5):
        for kg in range(2):
            add("A", "x2t", n, kg)
        for c in range(4):
            add("A", "pg", n, c)
    return found


SIGNALS = """w_consumed layer_arrived sigm_ready abs_ready log1p_ready hdiff_ready hlog_ready b_ready
dec_ready eq_ready ek_ready kq_ready diff_ready min_ready pexp_ready p_ready p_used sct_ready
km_ready kms_ready dls_done s_ready rs_ready rq_ready ss_scaled z_ready mu_done sq_ready
rms_ready on_ready mv_ready rstd_ready x1_ready idx_staged xb_used lb_ready
u_used v_used vd_used y_read idx_known score_ready gelu_ready w_ready diag_ready acc_ready idx_ready et_ready
xb_ready wsam_ready x2_ready ple_sig_ready x_ready silu_ready rprod_ready small_init places_free all_arrived
""".split()
DMASIGNALS = "x_loaded small_loaded lnp_loaded wout_loaded".split()
KEPT = "consts_loaded layer_go layer_done y_stored".split()


def build(nc, x_in, wstream, wout, small, lnp, lblog, st_in, consts, utab, vtab, y_out, st_p, st_s):
    fp32, i32, u32 = mybir.dt.float32, mybir.dt.int32, mybir.dt.uint32
    ALU = mybir.AluOpType
    ACT = mybir.ActivationFunctionType
    AX = mybir.AxisListType
    JOB = jobs()
    ds = bass.ds

    ctx = ExitStack()
    with ctx:
        def sb(name, *shape, dt=fp32):
            return ctx.enter_context(nc.sbuf_tensor(name, list(shape), dt))

        X = sb("X", 128, 5, D)
        XT = sb("XT", 128, KT, T)
        C = sb("C", 128, NCONST)
        WR = sb("WR", 128, SLOTW, 2048)
        SM = sb("SM", 128, NSMALL)
        LB = sb("LB", 128, 16)
        ST = sb("ST", 128, 5, 16)
        R = sb("R", 128, 30288)

        def view(at, *dims):
            n = 1
            for d in dims:
                n *= d
            v = R[:, at:at + n]
            if len(dims) == 1:
                return v
            names = "abcde"[:len(dims)]
            return v.rearrange(f"p ({' '.join(names)}) -> p {' '.join(names)}",
                               **{names[i]: dims[i] for i in range(1, len(dims))})

        Z = view(0, 16, T)
        ZG = view(0, 10, T)
        SQ = view(5200, 2, T)
        RS = view(6240, 2, T)
        OT = view(8320, 10, T)
        V = view(13520, 5, D)
        P = view(18640, 2, 4, NC, CH)
        T1 = view(18640, 4, T)
        T2 = view(20720, 4, T)
        S = view(22736, NC, 96)
        ROT = view(22800, 2, HALF)
        WO = view(13520, 10, D)
        SR = view(25808, 4, 96)
        KM = view(26192, 2, CT, 128)
        KMS = view(28240, CT, 128)
        SCT = view(29264, 2, 4, 128)
        LNP = view(25808, 4, D)
        QT = view(0, 16, T)
        G = view(8320, RING, D)
        PP = view(0, 5, D)
        SG = view(5120, D)
        X2T = view(6144, KT, 128)
        IDXS = view(7168, NS).bitcast(i32)
        GATES = view(7176, NS)
        SSC = view(7184, NS)
        WS = view(7192, NS)
        WS8 = view(7200, NS, NS)
        IDX = view(16512, 4, SLOTS).bitcast(i32)
        GATE = view(17024, 5, SLOTS)
        WGT = view(17664, SLOTS)
        SCORE = view(17792, SLOTS)
        XTF = XT.rearrange("p k t -> p (k t)")
        SC = [view(17920, 2 * PH * NKEY), XTF[:, 0:2048], XTF[:, 2048:4096], view(22016, 2 * PH * NKEY),
              view(19968, 2 * PH * NKEY)]
        DIAG = view(24064, RING, 128)
        STG = view(25088, 2, NKEY)
        CAND = view(25344, TOPK, TOPK)
        EQT = view(25088, 2, TOPK, TOPK)
        VV = view(25600, 2, TOPK)
        II = view(25632, 2, TOPK).bitcast(u32)
        IF = view(25664, 2, TOPK)
        BEST = view(25696, TOPK)
        CI = view(25712, TOPK).bitcast(u32)
        CAB = view(25728, 2, TOPK).bitcast(u32)
        ABF = view(25760, 2, TOPK)
        IST = view(25792, 2, RING).bitcast(i32)
        SEL = view(29904, 2, TOPK)
        SUM = view(29936, 2, PH)
        EF = view(29952, TOPK)
        EFS = view(29968, SLOTS)
        SS = sb("SS", 128, NS, 96)
        DEC = sb("DEC", 128, 4, NC + NS)
        LBASE = sb("LBASE", 128, 1)

        A = [ctx.enter_context(nc.psum_tensor(f"A{i}", [128, 512], fp32)) for i in range(3)]
        DB = [ctx.enter_context(nc.psum_tensor(f"D{i}", [128, 512], fp32)) for i in range(3)]
        Y = ctx.enter_context(nc.psum_tensor("Y", [128, D], fp32))
        BANKS = {"A": A, "D": DB}

        sems = {n: ctx.enter_context(nc.semaphore(n)) for n in SIGNALS + DMASIGNALS + KEPT}
        full = {r: ctx.enter_context(nc.semaphore(f"{r}_full")) for r in "AD"}
        free = {r: ctx.enter_context(nc.semaphore(f"{r}_free")) for r in "AD"}
        w_loaded = [ctx.enter_context(nc.semaphore(f"w_loaded{i}")) for i in range(SLOTW)]
        fetched = [ctx.enter_context(nc.semaphore(f"fetched{i}")) for i in range(RING)]
        ss_loaded = ctx.enter_context(nc.semaphore("ss_loaded"))
        ss_stored = ctx.enter_context(nc.semaphore("ss_stored"))
        s_stored = ctx.enter_context(nc.semaphore("s_stored"))
        cleared = [sems[n] for n in SIGNALS + DMASIGNALS] + list(full.values()) + list(free.values()) \
            + w_loaded + [ss_loaded, ss_stored, s_stored]

        block = ctx.enter_context(nc.Block())

        def const(name, rows=128):
            at, n = CONSTS[name]
            return C[0:rows, at:at + n]

        ident = const("ident")

        def wait_full(eng, *name):
            ring, j = JOB[name]
            eng.wait_ge(full[ring], j + 1)
            return BANKS[ring][j % 3]

        def wait_emptied(eng, *name):
            ring, j = JOB[name]
            eng.wait_ge(free[ring], j + 1)

        def arrive(eng, L):
            eng.drain()
            eng.sem_inc(sems["layer_done"], 1)
            eng.wait_ge(sems["layer_go"], L + 1)

        def oplace(f, h):
            if f in (2, 3):
                return 8 + f - 2, h * 64, 64
            return (2 * f + h if f < 2 else 4 + 2 * (f - 4) + h), 0, 96

        def vcols(f, h):
            return slice(VCOL[f] + h * DV[f], VCOL[f] + (h + 1) * DV[f])

        @block.sync
        def _(sp):
            sp.dma_start(C[:, :], consts).then_inc(sems["consts_loaded"], 16)
            sp.dma_start(X[:, 0:4, :], x_in[0:NP].rearrange("(n p) d -> p n d", p=128)) \
                .then_inc(sems["consts_loaded"], 16)
            sp.dma_start(X[0:NS, 4, :], x_in[NP:T]).then_inc(sems["consts_loaded"], 16)
            sp.dma_start(LB[:, 0:4], lblog).then_inc(sems["consts_loaded"], 16)

            def item(L, i):
                if i >= SLOTW:
                    sp.wait_ge(sems["w_consumed"], i - SLOTW + 1)
                n = {I_SUB: 1024, I_SUB + 1: 1024, I_PT: 2 * T}.get(i, 2048)
                sp.dma_start(WR[:, i % SLOTW, 0:n], wstream[L, i, :, 0:n]).then_inc(w_loaded[i % SLOTW], 16)

            with sp.Fori(0, DEPTH) as L:
                sp.dma_start(SM[:, :], small[L]).then_inc(sems["small_loaded"], 16)
                for i in range(I_GATE):
                    item(L, i)
                for f in range(6):
                    if f == 4:
                        for i in range(I_GATE, I_GATE + SLOTW):
                            item(L, i)
                    if f >= 1:
                        sp.wait_ge(sems["dls_done"], f)
                        sp.dma_start(st_s[L, f - 1], SS[:, :, :]).then_inc(ss_stored, 16)
                        wait_full(sp, "os", f - 1, 1)
                        sp.wait_ge(ss_stored, 16 * f)
                    sp.dma_start(SS[:, :, :], st_in[L, f]).then_inc(ss_loaded, 16)
                    if 1 <= f <= 4:
                        sp.wait_ge(sems["s_ready"], f)
                        sp.dma_start(st_p[L, f - 1], S[:, NC - 1, :]).then_inc(s_stored, 16)
                    if f == 5:
                        sp.wait_ge(sems["rs_ready"], 1)
                        sp.dma_start(st_p[L, 4], SR[:, 3, :]).then_inc(s_stored, 16)
                sp.wait_ge(sems["dls_done"], 6)
                sp.dma_start(st_s[L, 5], SS[:, :, :]).then_inc(ss_stored, 16)
                sp.wait_ge(sems["rs_ready"], 2)
                sp.dma_start(st_p[L, 5], SR[:, 3, :]).then_inc(s_stored, 16)
                wait_full(sp, "o", 5, 1)
                sp.wait_ge(s_stored, 96)
                sp.dma_start(WO, wout[L].rearrange("p s n -> p s n")).then_inc(sems["wout_loaded"], 16)
                item(L, I_WQ - 1)
                sp.wait_ge(ss_stored, 96)
                for j in range(4):
                    sp.dma_start(LNP[:, j, :], lnp[L, j:j + 1, :].to_broadcast([128, D])) \
                        .then_inc(sems["lnp_loaded"], 16)
                for i in range(I_WQ, ITEMS):
                    item(L, i)
                for s in range(SLOTW):
                    sp.wait_ge(w_loaded[s], 16 * (ITEMS // SLOTW))
                sp.sem_inc(sems["layer_done"], 1)
                sp.wait_ge(sems["layer_done"], L * 5 + 5)
                sp.sem_inc(sems["all_arrived"], 1)
                for s in cleared:
                    sp.sem_clear(s)
                sp.sem_inc(sems["layer_go"], 1)
            sp.dma_start(y_out[0:NP].rearrange("(n p) d -> p n d", p=128), X[:, 0:4, :]) \
                .then_inc(sems["y_stored"], 16)
            sp.dma_start(y_out[NP:T], X[0:NS, 4, :]).then_inc(sems["y_stored"], 16)
            sp.wait_ge(sems["y_stored"], 32)

        @block.tensor
        def _(pe):
            def bank(*name):
                ring, j = JOB[name]
                if j >= 3:
                    pe.wait_ge(free[ring], j - 2)
                return BANKS[ring][j % 3]

            def done(last, *name):
                last.then_inc(full[JOB[name][0]], 1)

            def weights(i):
                pe.wait_ge(w_loaded[i % SLOTW], 16 * (i // SLOTW + 1))
                return WR[:, i % SLOTW, :]

            def consumed(last):
                last.then_inc(sems["w_consumed"], 1)

            def to_features(stage):
                for n in range(5):
                    w = WID[n]
                    if stage == 1:
                        pe.wait_ge(sems["x1_ready"], n + 1)
                    for kg in range(2):
                        b = bank("xt", stage, n, kg)
                        for k in range(4):
                            last = nc.tensor.transpose(b[:, k * w:(k + 1) * w],
                                                       X[0:w, n, (4 * kg + k) * 128:(4 * kg + k + 1) * 128],
                                                       ident[0:w, 0:w])
                        done(last, "xt", stage, n, kg)
                wait_emptied(pe, "xt", stage, 4, 0)
                wait_emptied(pe, "xt", stage, 4, 1)

            def project(i, c, rhs, *name):
                w = weights(i).rearrange("p (k n) -> p k n", k=KT)
                for half in range(2):
                    b = bank(*name, half)
                    for k in range(KT):
                        last = nc.tensor.matmul(b[:, 0:HALF], w[:, k, c * 128:(c + 1) * 128],
                                                rhs[:, k, half * HALF:(half + 1) * HALF],
                                                start=(k == 0), stop=(k == KT - 1))
                    done(last, *name, half)
                return last

            pe.wait_ge(sems["consts_loaded"], 64)
            with pe.Fori(0, DEPTH) as L:
                to_features(0)
                for m, name in enumerate(FEATURES):
                    last = project(m // 2, m % 2, XT, "z", m)
                    if m % 2 or m == len(FEATURES) - 1:
                        pe.wait_ge(full["D"], JOB["z", m, 1][1] + 1)
                        pe.sem_inc(sems["w_consumed"], 1)
                    if name == "hq0":
                        pe.wait_ge(sems["small_loaded"], 16)
                        wait_emptied(pe, "z", 2, 0)
                        wait_emptied(pe, "z", 2, 1)
                        for g in range(2):
                            for half in range(2):
                                b = bank("ga", g, half)
                                done(nc.tensor.matmul(b[:, 0:HALF], SM[0:16, 12 + g * 128:12 + (g + 1) * 128],
                                                      T1[0:16, 0, half * HALF:(half + 1) * HALF],
                                                      start=True, stop=True), "ga", g, half)
                for i in range(4):
                    w = weights(I_V + i).rearrange("p (k n) -> p k n", k=KT)
                    for n in range(5):
                        b = bank("v", i, n)
                        for k in range(KT):
                            last = nc.tensor.matmul(b[0:WID[n], 0:256], XT[:, k, n * 128:n * 128 + WID[n]],
                                                    w[:, k, :], start=(k == 0), stop=(k == KT - 1))
                        done(last, "v", i, n)
                    pe.wait_ge(full["A"], JOB["v", i, 4][1] + 1)
                    pe.sem_inc(sems["w_consumed"], 1)
                wait_emptied(pe, "v", 3, 4)
                for s in range(4):
                    m = FEATURES.index(("rq0", "rq1", "rk0", "rk1")[s])
                    wait_emptied(pe, "z", m, 0)
                    wait_emptied(pe, "z", m, 1)
                    for half in range(2):
                        b = bank("rot", s, half)
                        done(nc.tensor.matmul(b[:, 0:HALF], const("perm"),
                                              Z[:, 12 + s, half * HALF:(half + 1) * HALF],
                                              start=True, stop=True), "rot", s, half)

                for f in range(6):
                    q, k = (8 + f, 4 + f) if f < 4 else (8 + f, 10 + f)
                    if f < 4:
                        b = bank("sc", f)[:, 0:128].rearrange("p (n i h) -> p n i h", n=4, h=2)
                        for iq in range(4):
                            step = 4 * f + iq
                            pe.wait_ge(sems["p_ready"], step + 1)
                            for n in range(4):
                                for i in range(4):
                                    last = nc.tensor.matmul(
                                        b[:, n, 4 * iq + i, :],
                                        P[:, step % 2, i, n * CT:(n + 1) * CT, :].rearrange("p c j -> p (c j)"),
                                        const("headsel"), start=True, stop=True)
                            if iq < 3:
                                last.then_inc(sems["p_used"], 1)
                        last.then_inc(full["D"], 1)
                    else:
                        if f == 4:
                            pe.wait_ge(sems["z_ready"], 1)
                        for h in range(2):
                            b = bank("rsc", f, h)
                            r = slice(h * 64, h * 64 + 64)
                            for n in range(4):
                                c = slice(n * 128, (n + 1) * 128)
                                last = nc.tensor.matmul(b[:, c], Z[r, k, c], Z[r, q, c], start=True, stop=True)
                            done(last, "rsc", f, h)
                    pe.wait_ge(sems["kq_ready"], f + 1)
                    b = bank("kt", f)
                    for n in range(4):
                        last = nc.tensor.transpose(b[:, n * 128:(n + 1) * 128], Z[:, k, n * 128:(n + 1) * 128],
                                                   ident)
                    done(last, "kt", f)
                    b = bank("kts", f)
                    done(nc.tensor.transpose(b[0:NS, 0:128], Z[:, k, NP:T], ident), "kts", f)
                    if f < 4:
                        for n in range(4):
                            pe.wait_ge(sems["km_ready"], 4 * f + n + 1)
                            for half in range(2):
                                b = bank("dl", f, n, half)[:, 0:384].rearrange("p (c v) -> p c v", c=4)
                                for c in range(4):
                                    for h in range(2):
                                        last = nc.tensor.matmul(
                                            b[h * 64:h * 64 + 64, c, 0:DV[f]],
                                            KM[:, n % 2, 4 * half + c, h * 64:h * 64 + 64],
                                            V[:, n, vcols(f, h)], start=True, stop=True)
                                done(last, "dl", f, n, half)
                    else:
                        pe.wait_ge(sems["km_ready"], 16 + f - 3)
                        b = bank("rdl", f)[:, 0:384].rearrange("p (c v) -> p c v", c=4)
                        for n in range(4):
                            for h in range(2):
                                last = nc.tensor.matmul(b[h * 64:h * 64 + 64, n, :],
                                                        KM[:, 0, n, h * 64:h * 64 + 64],
                                                        V[:, n, vcols(f, h)], start=True, stop=True)
                        done(last, "rdl", f)
                    pe.wait_ge(sems["kms_ready"], f + 1)
                    for half in range(2):
                        b = bank("dls", f, half)[:, 0:384].rearrange("p (c v) -> p c v", c=4)
                        for c in range(4):
                            for h in range(2):
                                last = nc.tensor.matmul(b[h * 64:h * 64 + 64, c, 0:DV[f]],
                                                        KMS[0:NS, 4 * half + c, h * 64:h * 64 + 64],
                                                        V[0:NS, 4, vcols(f, h)], start=True, stop=True)
                        done(last, "dls", f, half)
                    pe.wait_ge(sems["dls_done"], f + 1)
                    for h in range(2):
                        _, r0, rows = oplace(f, h)
                        r = slice(h * 64, h * 64 + 64)
                        b = bank("os", f, h)
                        for t in range(NS):
                            last = nc.tensor.matmul(b[r0:r0 + rows, t:t + 1], SS[r, t, 0:rows],
                                                    Z[r, q, NP + t:NP + t + 1], start=True, stop=True)
                        done(last, "os", f, h)
                    pe.wait_ge(sems["sct_ready"], f + 1)
                    if f < 4:
                        pe.wait_ge(sems["s_ready"], f + 1)
                    else:
                        pe.wait_ge(sems["rs_ready"], f - 3)
                    for h in range(2):
                        _, r0, rows = oplace(f, h)
                        r = slice(h * 64, h * 64 + 64)
                        b = bank("o", f, h)
                        step = CH if f < 4 else 128
                        for n in range(4):
                            chunks = [c for c in range(128 // step) if n or c]
                            last = nc.tensor.matmul(b[r0:r0 + rows, n * 128:(n + 1) * 128], V[:, n, vcols(f, h)],
                                                    SCT[:, h, n, :], start=True, stop=not chunks)
                            for c in chunks:
                                g = n * (128 // step) + c
                                state = S[r, g - 1, 0:rows] if f < 4 else SR[r, g - 1, 0:rows]
                                cols = slice(g * step, (g + 1) * step)
                                last = nc.tensor.matmul(b[r0:r0 + rows, cols], state, Z[r, q, cols],
                                                        start=False, stop=(c == chunks[-1]))
                        done(last, "o", f, h)

                for m in range(10):
                    last = project(I_GATE + m // 2, m % 2, XT, "g", m)
                    if m % 2:
                        pe.wait_ge(full["A"], JOB["g", m, 1][1] + 1)
                        pe.sem_inc(sems["w_consumed"], 1)
                wait_emptied(pe, "o", 5, 1)
                for s in range(4):
                    for half in range(2):
                        b = bank("mu", s, half)
                        done(nc.tensor.matmul(b[0:96, 0:HALF], const("onesg", 96),
                                              OT[0:96, 4 + s, half * HALF:(half + 1) * HALF],
                                              start=True, stop=True), "mu", s, half)
                for s in range(10):
                    rows = 96 if s < 8 else 128
                    pe.wait_ge(sems["sq_ready"], s + 1)
                    for half in range(2):
                        b = bank("ms", s, half)
                        done(nc.tensor.matmul(b[0:rows, 0:HALF], const("onesg" if s < 8 else "onesh", rows),
                                              SQ[0:rows, s % 2, half * HALF:(half + 1) * HALF],
                                              start=True, stop=True), "ms", s, half)
                pe.wait_ge(sems["on_ready"], 10)
                pe.wait_ge(sems["wout_loaded"], 16)
                for n in range(5):
                    for half in range(2):
                        b = bank("mix", n, half)
                        for s in range(10):
                            rows = 96 if s < 8 else 128
                            last = nc.tensor.matmul(b[0:WID[n], :], OT[0:rows, s, n * 128:n * 128 + WID[n]],
                                                    WO[0:rows, s, half * 512:(half + 1) * 512],
                                                    start=(s == 0), stop=(s == 9))
                        done(last, "mix", n, half)
                to_features(1)
                for m in range(16):
                    last = project(I_WQ + m // 2, m % 2, XT, "q", m)
                    if m % 2:
                        pe.wait_ge(full["D"], JOB["q", m, 1][1] + 1)
                        pe.sem_inc(sems["w_consumed"], 1)
                wait_emptied(pe, "q", 15, 0)
                wait_emptied(pe, "q", 15, 1)
                subs = [weights(I_SUB + i)[:, 0:1024].rearrange("p (s n) -> p s n", s=8) for i in range(2)]

                for n in range(5):
                    for c in range(4):
                        b = bank("s", n, c)
                        for j in range(4):
                            hs = 4 * c + j
                            last = nc.tensor.matmul(b[0:WID[n], j * 128:(j + 1) * 128],
                                                    QT[:, hs, n * 128:n * 128 + WID[n]],
                                                    subs[hs // 8][:, hs % 8, :], start=True, stop=True)
                        done(last, "s", n, c)
                wait_full(pe, "s", 4, 3)
                pe.sem_inc(sems["w_consumed"], 2)
                pw = weights(I_PP).rearrange("p (k n) -> p k n", k=2)
                pt = weights(I_PT)[:, 0:2 * T].rearrange("p (k n) -> p k n", k=2)
                for n in range(5):
                    for half in range(2):
                        b = bank("pp", n, half)
                        for k in range(2):
                            last = nc.tensor.matmul(b[0:WID[n], :], pt[:, k, n * 128:n * 128 + WID[n]],
                                                    pw[:, k, half * 512:(half + 1) * 512],
                                                    start=(k == 0), stop=(k == 1))
                        done(last, "pp", n, half)
                wait_full(pe, "pp", 4, 1)
                pe.sem_inc(sems["w_consumed"], 2)

                def embedding_gate(n):
                    w = WID[n]
                    pe.wait_ge(sems["x2_ready"], n + 1)
                    for kg in range(2):
                        b = bank("x2t", n, kg)
                        for k in range(4):
                            last = nc.tensor.transpose(b[:, k * w:(k + 1) * w],
                                                       X[0:w, n, (4 * kg + k) * 128:(4 * kg + k + 1) * 128],
                                                       ident[0:w, 0:w])
                        done(last, "x2t", n, kg)
                    wait_emptied(pe, "x2t", n, 1)
                    for c in range(4):
                        wg = weights(I_PG + c).rearrange("p (k n) -> p k n", k=KT)
                        b = bank("pg", n, c)
                        for k in range(KT):
                            last = nc.tensor.matmul(b[0:w, 0:256], X2T[:, k, 0:w], wg[:, k, :],
                                                    start=(k == 0), stop=(k == KT - 1))
                        done(last, "pg", n, c)

                for n in range(4):
                    def output_rows(g, start=False, stop=False):
                        for i, k in enumerate(PE_ROWS):
                            pe.wait_ge(sems["diag_ready"], g * PEG + (n * NGRP * PEG + i + 1))
                            pe.wait_ge(fetched[k], L * (16 * USES) + g * 16 + 16 * (n * 2 * NGRP + NGRP + 1))
                            for half in range(2):
                                c = slice(half * 512, (half + 1) * 512)
                                last = nc.tensor.matmul(Y[:, c], DIAG[:, k, :], G[:, k, c],
                                                        start=start and i == 0, stop=stop and i == PEG - 1)
                            last.then_inc(sems["v_used"], 1)
                        return last

                    if n:
                        embedding_gate(n - 1)
                        pe.wait_ge(sems["y_read"], n)
                    output_rows(0, start=True)
                    with pe.Fori(1, NGRP - 1) as g:
                        output_rows(g)
                    output_rows(NGRP - 1, stop=True)
                    wait_own = n * NGRP * PEG + NGRP * PEG + PEG
                    pe.wait_ge(sems["v_used"], wait_own)
                    pe.sem_inc(sems["acc_ready"], 1)

                pe.wait_ge(sems["et_ready"], 1)
                b = bank("et")
                done(nc.tensor.transpose(b[:, 0:NS], EFS[0:NS], ident[0:NS, 0:NS]), "et")
                pe.wait_ge(sems["et_ready"], 2)
                b = bank("gt")
                done(nc.tensor.transpose(b[:, 0:NS], GATE[0:NS, 4, :], ident[0:NS, 0:NS]), "gt")
                pe.wait_ge(sems["y_read"], 4)
                for t in range(NS):
                    if t:
                        pe.wait_ge(sems["xb_used"], t)
                    for half in range(2):
                        c = slice(half * 512, (half + 1) * 512)
                        last = nc.tensor.matmul(Y[:, c], ident[0:NS, t:t + 1].to_broadcast([NS, 128]),
                                                X[0:NS, 4, c], start=True, stop=True)
                    last.then_inc(sems["xb_ready"], 1)
                embedding_gate(3)
                pe.wait_ge(sems["wsam_ready"], 1)
                for half in range(2):
                    c = slice(half * 512, (half + 1) * 512)
                    nc.tensor.matmul(Y[0:NS, c], const("aident", NS)[:, 0:NS], X[0:NS, 4, c],
                                     start=True, stop=False)
                for t in range(NS):
                    pe.wait_ge(fetched[t], L * (16 * USES) + 16 * USES)
                    for half in range(2):
                        c = slice(half * 512, (half + 1) * 512)
                        last = nc.tensor.matmul(Y[0:NS, c], WS8[:, t, :], G[:, t, c], start=False,
                                                stop=(t == NS - 1))
                last.then_inc(sems["acc_ready"], 1)
                embedding_gate(4)
                arrive(pe, L)

        @block.gpsimd
        def _(pool):
            def fetch(L, n, phase, table):
                with pool.Fori(0, NGRP // 2) as gg:
                    if phase == 0:
                        pool.wait_ge(sems["idx_ready"], gg + (n * PH + 1))
                        pool.sem_inc(sems["idx_known"], 1)
                    for par in range(2):
                        nc.gpsimd.tensor_copy(IST[:, par, :], IDX[:, n, ds(gg * (2 * RING) + par * RING, RING)]) \
                            .then_inc(sems["idx_staged"], 1)
                        pool.wait_ge(sems["idx_staged"],
                                     gg * 2 + ((n * 2 + phase) * NGRP + par + 1))
                        for half in range(2):
                            upto = half + 1
                            if phase == 0:
                                pool.wait_ge(sems["u_used"],
                                             gg * (2 * RING) + (n * SLOTS + par * RING + upto * RING // 2))
                                pool.wait_ge(sems["v_used"], n * NGRP * PEG + upto * PEG // 2)
                                pool.wait_ge(sems["vd_used"], n * NGRP * DVG + upto * DVG // 2)
                            else:
                                pool.wait_ge(sems["v_used"],
                                             gg * (2 * PEG) + ((n * NGRP + par) * PEG + upto * PEG // 2))
                                pool.wait_ge(sems["vd_used"],
                                             gg * (2 * DVG) + ((n * NGRP + par) * DVG + upto * DVG // 2))
                                pool.wait_ge(sems["u_used"], (n + 1) * SLOTS + upto * RING // 2)
                            pool.sem_inc(sems["places_free"], 1)
                            for k in range(half * RING // 2, (half + 1) * RING // 2):
                                pool.indirect_dma_start(
                                    G[:, k, :], None, table,
                                    bass.IndirectOffsetOnAxis(ap=IST[:, par, k:k + 1], axis=0)) \
                                    .then_inc(fetched[k], 16)

            pool.wait_ge(sems["consts_loaded"], 64)
            with pool.Fori(0, DEPTH) as L:
                pool.sem_inc(sems["u_used"], RING)
                pool.sem_inc(sems["v_used"], PEG)
                pool.sem_inc(sems["vd_used"], DVG)
                pool.wait_ge(sems["b_ready"], 1)
                for step in range(16):
                    f, iq = step // 4, step % 4
                    w = 4 * iq + 4
                    if step >= 2:
                        if (step - 2) % 4 == 3:
                            wait_full(pool, "sc", (step - 2) // 4)
                        else:
                            pool.wait_ge(sems["p_used"], (step - 2) - (step - 2) // 4 + 1)
                    b = Z[:, f, 0:NP].rearrange("p (c i) -> p c i", i=CH)
                    if w < CH:
                        nc.gpsimd.memset(P[:, step % 2, :, :, w:CH], 0.0)
                    for i in range(4):
                        at = 4 * iq + i
                        last = nc.gpsimd.tensor_tensor(P[:, step % 2, i, :, 0:w],
                                                       b[:, :, at:at + 1].to_broadcast([128, NC, w]),
                                                       b[:, :, 0:w], ALU.subtract)
                    last.then_inc(sems["diff_ready"], 1)
                for s in range(10):
                    rows = 96 if s < 8 else 128
                    if s >= 2:
                        wait_full(pool, "ms", s - 2, 1)
                    if s == 0:
                        wait_emptied(pool, "o", 5, 1)
                        wait_emptied(pool, "g", 9, 1)
                    if 4 <= s < 8:
                        pool.wait_ge(sems["mu_done"], s - 3)
                    nc.gpsimd.tensor_tensor(SQ[0:rows, s % 2, :], OT[0:rows, s, :], OT[0:rows, s, :], ALU.mult) \
                        .then_inc(sems["sq_ready"], 1)
                for n in range(4):
                    fetch(L, n, 0, utab)
                    fetch(L, n, 1, vtab)
                pool.wait_ge(sems["idx_ready"], 4 * PH + 1)
                pool.wait_ge(sems["v_used"], (4 * NGRP + 1) * PEG)
                pool.wait_ge(sems["vd_used"], (4 * NGRP + 1) * DVG)
                for phase, table in ((0, utab), (1, vtab)):
                    for t in range(NS):
                        if phase:
                            pool.wait_ge(sems["u_used"], RING + 4 * SLOTS + t + 1)
                        pool.indirect_dma_start(G[:, t, :], None, table,
                                                bass.IndirectOffsetOnAxis(ap=IDXS[:, t:t + 1], axis=0)) \
                            .then_inc(fetched[t], 16)
                arrive(pool, L)

        @block.scalar
        def _(act):
            def emptied(ins, *name):
                ins.then_inc(free[JOB[name][0]], 1)

            def to_features(stage):
                for n in range(5):
                    w = WID[n]
                    b = wait_full(act, "xt", stage, n, 0)
                    emptied(nc.scalar.activation(XT[:, 0:4, n * 128:n * 128 + w],
                                                 b[:, 0:4 * w].rearrange("p (k t) -> p k t", k=4), ACT.Copy),
                            "xt", stage, n, 0)

            def rstd(n, count):
                w = WID[n]
                act.wait_ge(sems["mv_ready"], count)
                nc.scalar.activation(ST[0:w, n, 14:15], ST[0:w, n, 13:14], ACT.Ln, bias=const("eps", w))
                act.drain()
                nc.scalar.activation(ST[0:w, n, 15:16], ST[0:w, n, 14:15], ACT.Exp, scale=-0.5) \
                    .then_inc(sems["rstd_ready"], 1)

            def value(i, n):
                b = wait_full(act, "v", i, n)
                emptied(nc.scalar.activation(V[0:WID[n], n, i * 256:(i + 1) * 256], b[0:WID[n], 0:256],
                                             ACT.Copy), "v", i, n)

            act.wait_ge(sems["consts_loaded"], 64)
            act.wait_ge(sems["small_init"], 1)
            nc.scalar.activation(LB[:, 0:4], LB[:, 0:4], ACT.Exp).then_inc(sems["small_init"], 1)
            with act.Fori(0, DEPTH) as L:
                to_features(0)
                act.wait_ge(sems["lb_ready"], 1)
                nc.scalar.activation(LB[:, 10:14], LB[:, 6:10], ACT.Ln).then_inc(sems["lb_ready"], 1)
                for m, name in enumerate(FEATURES):
                    b = wait_full(act, "z", m, 0)
                    if name == "glr":
                        emptied(nc.scalar.activation(T1[0:16, 0, 0:HALF], b[0:16, 0:HALF], ACT.Copy), "z", m, 0)
                    else:
                        emptied(nc.scalar.activation(Z[:, ZSLOT[name], 0:HALF], b[:, 0:HALF], ACT.Copy,
                                                     scale=48 ** -0.5 if name[:2] == "gq" else 1.0), "z", m, 0)
                wait_emptied(act, "z", len(FEATURES) - 1, 1)
                act.drain()
                nc.scalar.activation(Z[:, 6:8, :], Z[:, 2:4, :], ACT.Sigmoid, scale=-1.0)
                nc.scalar.activation(Z[:, 10:12, :], Z[:, 10:12, :], ACT.Silu).then_inc(sems["sigm_ready"], 1)
                for n in range(5):
                    value(0, n)
                act.wait_ge(sems["abs_ready"], 1)
                nc.scalar.activation(T1, T1, ACT.Exp, scale=-1.0)
                act.drain()
                nc.scalar.activation(T2, T1, ACT.Ln, bias=1.0).then_inc(sems["log1p_ready"], 1)
                for n in range(5):
                    value(1, n)
                act.wait_ge(sems["hdiff_ready"], 1)
                nc.scalar.activation(T1[:, 0:2, :], T1[:, 0:2, :], ACT.Exp, scale=-1.0)
                act.drain()
                nc.scalar.activation(T2[:, 0:2, :], T1[:, 0:2, :], ACT.Ln, bias=1.0) \
                    .then_inc(sems["hlog_ready"], 1)
                for n in range(5):
                    value(2, n)
                act.wait_ge(sems["b_ready"], 1)
                nc.scalar.activation(DEC[:, :, 1:NC],
                                     Z[:, 0:4, 0:NP].rearrange("p f (c i) -> p f c i", i=CH)[:, :, 1:NC, CH - 1],
                                     ACT.Exp)
                nc.scalar.activation(DEC[:, :, NC:NC + NS], Z[:, 0:4, NP:T], ACT.Exp) \
                    .then_inc(sems["dec_ready"], 1)
                for n in range(5):
                    value(3, n)

                def pexp(step):
                    w = 4 * (step % 4) + 4
                    act.wait_ge(sems["min_ready"], step + 1)
                    p = P[:, step % 2, :, :, 0:w]
                    nc.scalar.activation(p, p, ACT.Exp).then_inc(sems["pexp_ready"], 1)

                def outputs(f):
                    if f < 4:
                        act.wait_ge(sems["ek_ready"], f + 1)
                        nc.scalar.activation(SCT, SCT, ACT.Exp).then_inc(sems["eq_ready"], 1)
                    if f < 4:
                        if f >= 1:
                            act.wait_ge(s_stored, 16 * f)
                        for n in range(4):
                            for half in range(2):
                                b = wait_full(act, "dl", f, n, half)
                                emptied(nc.scalar.activation(
                                    S[:, n * CT + 4 * half:n * CT + 4 * half + 4, 0:DV[f]],
                                    b[:, 0:384].rearrange("p (c v) -> p c v", c=4)[:, :, 0:DV[f]],
                                    ACT.Copy), "dl", f, n, half)
                    else:
                        if f == 5:
                            act.wait_ge(s_stored, 16 * f)
                        b = wait_full(act, "rdl", f)
                        emptied(nc.scalar.activation(SR, b[:, 0:384].rearrange("p (c v) -> p c v", c=4),
                                                     ACT.Copy), "rdl", f)
                    for kind, c0, c1 in (("os", NP, T), ("o", 0, NP)):
                        for h in range(2):
                            at, r0, rows = oplace(f, h)
                            b = wait_full(act, kind, f, h)
                            emptied(nc.scalar.activation(OT[r0:r0 + rows, at, c0:c1],
                                                         b[r0:r0 + rows, 0:c1 - c0], ACT.Copy), kind, f, h)

                for f in range(4):
                    for iq in range(4):
                        pexp(4 * f + iq)
                    outputs(f)
                outputs(4)
                outputs(5)
                for m in range(10):
                    for half in range(2):
                        b = wait_full(act, "g", m, half)
                        emptied(nc.scalar.activation(ZG[:, m, half * HALF:(half + 1) * HALF], b[:, 0:HALF],
                                                     ACT.Silu), "g", m, half)
                for s in range(10):
                    rows = 96 if s < 8 else 128
                    if s >= 2:
                        act.wait_ge(sems["on_ready"], s - 1)
                    for half in range(2):
                        b = wait_full(act, "ms", s, half)
                        emptied(nc.scalar.activation(RS[0:rows, s % 2, half * HALF:(half + 1) * HALF],
                                                     b[0:rows, 0:HALF], ACT.Ln, bias=const("eps", rows)),
                                "ms", s, half)
                    act.drain()
                    nc.scalar.activation(RS[0:rows, s % 2, :], RS[0:rows, s % 2, :], ACT.Exp, scale=-0.5) \
                        .then_inc(sems["rms_ready"], 1)
                for n in range(5):
                    rstd(n, n + 1)
                to_features(1)
                for m in range(16):
                    b = wait_full(act, "q", m, 0)
                    emptied(nc.scalar.activation(QT[:, m, 0:HALF], b[:, 0:HALF], ACT.Copy), "q", m, 0)
                for n in range(5):
                    for c in range(4):
                        b = wait_full(act, "s", n, c)
                        emptied(nc.scalar.activation(SC[n][0:WID[n], c * 512:(c + 1) * 512], b[0:WID[n], :],
                                                     ACT.Copy), "s", n, c)
                for n in range(5):
                    for half in range(2):
                        b = wait_full(act, "pp", n, half)
                        emptied(nc.scalar.activation(PP[0:WID[n], n, half * 512:(half + 1) * 512],
                                                     b[0:WID[n], :], ACT.Copy), "pp", n, half)

                def gates(n):
                    act.wait_ge(sems["rprod_ready"], n + 1)
                    g = GATE[0:WID[n], n, :]
                    nc.scalar.activation(g, g, ACT.Exp).then_inc(sems["silu_ready"], 1)

                def embedding_gate(n):
                    w = WID[n]
                    for kg in range(2):
                        b = wait_full(act, "x2t", n, kg)
                        emptied(nc.scalar.activation(X2T[:, 4 * kg:4 * kg + 4, 0:w],
                                                     b[:, 0:4 * w].rearrange("p (k t) -> p k t", k=4), ACT.Copy),
                                "x2t", n, kg)
                    if n:
                        act.wait_ge(sems["x_ready"], n)
                    for c in range(4):
                        b = wait_full(act, "pg", n, c)
                        emptied(nc.scalar.activation(SG[0:w, c * 256:(c + 1) * 256], b[0:w, 0:256],
                                                     ACT.Sigmoid), "pg", n, c)

                gates(0)
                for n in range(4):
                    if n:
                        embedding_gate(n - 1)
                    act.wait_ge(sems["score_ready"], n + 1)
                    nc.scalar.activation(WGT, SCORE, ACT.Gelu).then_inc(sems["gelu_ready"], 1)
                    act.wait_ge(sems["w_ready"], n + 1)
                    with act.Fori(0, NGRP) as g:
                        for i, k in enumerate(PE_ROWS):
                            if i % (PEG // 2) == 0:
                                act.wait_ge(sems["v_used"], g * PEG + (n * NGRP * PEG + i + PEG // 2))
                            nc.scalar.activation(DIAG[:, k, :], ident, ACT.Copy,
                                                 scale=WGT[:, ds(g * RING + k, 1)]) \
                                .then_inc(sems["diag_ready"], 1)
                    gates(n + 1)
                    rstd(n, n + 6)
                act.wait_ge(sems["score_ready"], 5)
                nc.scalar.activation(WS, SSC, ACT.Gelu).then_inc(sems["gelu_ready"], 1)
                embedding_gate(3)
                rstd(4, 10)
                embedding_gate(4)
                arrive(act, L)

        @block.vector
        def _(dve):
            def emptied(ins, *name):
                ins.then_inc(free[JOB[name][0]], 1)

            def to_features(stage):
                for n in range(5):
                    w = WID[n]
                    b = wait_full(dve, "xt", stage, n, 1)
                    emptied(nc.vector.tensor_copy(XT[:, 4:8, n * 128:n * 128 + w],
                                                  b[:, 0:4 * w].rearrange("p (k t) -> p k t", k=4)),
                            "xt", stage, n, 1)

            def statistics(n, src):
                w = WID[n]
                for j in range(2):
                    nc.vector.bn_stats(ST[0:w, n, 6 * j:6 * j + 6], src[0:w, j * 512:(j + 1) * 512])
                dve.drain()
                nc.vector.bn_aggr(ST[0:w, n, 12:14], ST[0:w, n, 0:12].rearrange("p (a b) -> p a b", a=2)) \
                    .then_inc(sems["mv_ready"], 1)

            def normalize(n, src, which, count, signal):
                w = WID[n]
                dve.wait_ge(sems["rstd_ready"], count)
                x = X[0:w, n, :]
                nc.vector.tensor_scalar(x, src[0:w, :], ST[0:w, n, 12:13], ST[0:w, n, 15:16],
                                        ALU.subtract, ALU.mult)
                dve.drain()
                nc.vector.tensor_tensor(x, x, LNP[0:w, 2 * which, :], ALU.mult)
                dve.drain()
                return nc.vector.tensor_tensor(x, x, LNP[0:w, 2 * which + 1, :], ALU.add) \
                    .then_inc(sems[signal], 1)

            def best8(src, vals, inds, strike):
                dve.drain()
                for s, v in zip(src, vals):
                    nc.vector.max(v, s)
                dve.drain()
                for s, v, i in zip(src, vals, inds):
                    nc.vector.max_index(i, v, s)
                if strike:
                    dve.drain()
                    for s, v in zip(src, vals):
                        nc.vector.match_replace(s, v, s, -3.0e38)

            def top(n, h, part):
                w = WID[n]
                if part == 0:
                    nc.vector.tensor_copy(STG[0:w].rearrange("p s n -> p (s n)"),
                                          SC[n][0:w, ds(h * (2 * NKEY), 2 * NKEY)])
                if part < 2:
                    c = slice(part * 8, part * 8 + 8)
                    best8([STG[0:w, s, :] for s in range(2)], [VV[0:w, s, c] for s in range(2)],
                          [II[0:w, s, c] for s in range(2)], part == 0)
                if part == 2:
                    dve.drain()
                    nc.vector.tensor_copy(IF[0:w], II[0:w])
                    nc.vector.tensor_tensor(CAND[0:w], VV[0:w, 0, :].unsqueeze(2).to_broadcast([w, 16, 16]),
                                            VV[0:w, 1, :].unsqueeze(1).to_broadcast([w, 16, 16]), ALU.add)
                    cand = CAND[0:w].rearrange("p a b -> p (a b)")
                    for c in (slice(0, 8), slice(8, 16)):
                        best8([cand], [BEST[0:w, c]], [CI[0:w, c]], c.start == 0)
                if part == 3:
                    dve.drain()
                    nc.vector.tensor_scalar(GATE[0:w, n, ds(h * TOPK, TOPK)], BEST[0:w], BEST[0:w, 0:1], None,
                                            ALU.subtract)
                    nc.vector.tensor_single_scalar(CAB[0:w, 0], CI[0:w], 4, ALU.logical_shift_right)
                    nc.vector.tensor_single_scalar(CAB[0:w, 1], CI[0:w], 15, ALU.bitwise_and)
                    dve.drain()
                    nc.vector.tensor_copy(ABF[0:w], CAB[0:w])
                    dve.drain()
                    for s in range(2):
                        nc.vector.tensor_tensor(EQT[0:w, s], ABF[0:w, s].unsqueeze(2).to_broadcast([w, 16, 16]),
                                                iota16[0:w, :].unsqueeze(1).to_broadcast([w, 16, 16]),
                                                ALU.is_equal)
                    dve.drain()
                    for s in range(2):
                        nc.vector.tensor_tensor(EQT[0:w, s], EQT[0:w, s],
                                                IF[0:w, s, :].unsqueeze(1).to_broadcast([w, 16, 16]), ALU.mult)
                    dve.drain()
                    nc.vector.tensor_reduce(SEL[0:w], EQT[0:w], AX.X, ALU.add)
                    dve.drain()
                    nc.vector.scalar_tensor_tensor(out=EF[0:w], in0=SEL[0:w, 0], scalar=float(NKEY),
                                                   in1=SEL[0:w, 1], op0=ALU.mult, op1=ALU.add)
                    dve.drain()
                    out = IDX[:, n, ds(h * TOPK, TOPK)] if n < 4 else EFS[0:w, ds(h * TOPK, TOPK)]
                    last = nc.vector.tensor_scalar(out, EF[0:w], LBASE[0:w, 0:1], None, ALU.add)
                    if n < 4:
                        last.then_inc(sems["idx_ready"], 1)

            def softmax_sums(n):
                w = WID[n]
                gate = GATE[0:w, n, :].rearrange("p (h k) -> p h k", k=TOPK)
                dve.wait_ge(sems["silu_ready"], n + 1)
                nc.vector.tensor_reduce(SUM[0:w, 0], gate, AX.X, ALU.add)
                dve.drain()
                nc.vector.reciprocal(SUM[0:w, 1], SUM[0:w, 0])
                dve.drain()
                return nc.vector.tensor_tensor(gate, gate, SUM[0:w, 1].unsqueeze(2).to_broadcast([w, PH, TOPK]),
                                               ALU.mult)

            def dots(L, n, h, j0, j1):
                for j in range(j0, j1):
                    k = j % RING
                    dve.wait_ge(fetched[k], L * (16 * USES) + h * (16 * GPH) + 16 * (n * 2 * NGRP + j // RING + 1))
                    nc.vector.scalar_tensor_tensor(
                        out=G[:, k, :], in0=G[:, k, :], scalar=1.0, in1=X[:, n, :], op0=ALU.mult,
                        op1=ALU.mult, accum_out=SCORE[:, ds(h * TOPK + j, 1)]) \
                        .then_inc(sems["u_used"], 1)

            def add_embedding(n):
                w = WID[n]
                wait_emptied(dve, "pg", n, 3)
                nc.vector.tensor_tensor(SG[0:w], SG[0:w], PP[0:w, n, :], ALU.mult)
                dve.drain()
                nc.vector.tensor_tensor(X[0:w, n, :], X[0:w, n, :], SG[0:w], ALU.add).then_inc(sems["x_ready"], 1)

            iota16 = const("iota")
            dve.wait_ge(sems["consts_loaded"], 64)
            nc.vector.tensor_tensor(LB[:, 4:6], LB[:, 0:2], LB[:, 2:4], ALU.max)
            dve.drain()
            nc.vector.tensor_tensor(LB[:, 0:2], LB[:, 0:2], LB[:, 4:6], ALU.subtract)
            nc.vector.tensor_tensor(LB[:, 2:4], LB[:, 2:4], LB[:, 4:6], ALU.subtract).then_inc(sems["small_init"], 1)
            dve.wait_ge(sems["small_init"], 2)
            nc.vector.tensor_tensor(LB[:, 4:6], LB[:, 0:2], LB[:, 2:4], ALU.add)
            dve.drain()
            nc.vector.reciprocal(LB[:, 6:8], LB[:, 4:6])
            dve.drain()
            nc.vector.tensor_tensor(LB[:, 14:16], LB[:, 2:4], LB[:, 6:8], ALU.mult)
            nc.vector.memset(LB[:, 4:6], 0.0)
            nc.vector.memset(LBASE[:, :], 0.0)

            with dve.Fori(0, DEPTH) as L:
                dve.drain()
                nc.vector.tensor_scalar(LB[:, 6:8], LB[:, 4:6], 2.0 ** -63, None, ALU.max)
                nc.vector.tensor_scalar(LB[:, 8:10], LB[:, 4:6], -1.0, 1.0, ALU.mult, ALU.add)
                dve.drain()
                nc.vector.tensor_scalar(LB[:, 8:10], LB[:, 8:10], 2.0 ** -63, None, ALU.max)
                dve.drain().then_inc(sems["lb_ready"], 1)
                to_features(0)
                for m, name in enumerate(FEATURES):
                    b = wait_full(dve, "z", m, 1)
                    if name == "glr":
                        emptied(nc.vector.tensor_copy(T1[0:16, 0, HALF:T], b[0:16, 0:HALF]), "z", m, 1)
                    else:
                        emptied(nc.vector.tensor_scalar(Z[:, ZSLOT[name], HALF:T], b[:, 0:HALF],
                                                        48 ** -0.5 if name[:2] == "gq" else 1.0, None, ALU.mult),
                                "z", m, 1)
                    if name == "hq0":
                        for g in range(2):
                            for half in range(2):
                                b = wait_full(dve, "ga", g, half)
                                emptied(nc.vector.tensor_scalar(Z[:, g, half * HALF:(half + 1) * HALF],
                                                                b[:, 0:HALF], SM[:, g:g + 1], None, ALU.add),
                                        "ga", g, half)
                dve.wait_ge(sems["sigm_ready"], 1)
                nc.vector.scalar_tensor_tensor(out=T1, in0=Z[:, 0:4, :], scalar=-1.0, in1=Z[:, 0:4, :],
                                               op0=ALU.mult, op1=ALU.max).then_inc(sems["abs_ready"], 1)
                for h in range(2):
                    nc.vector.tensor_scalar(Z[:, 6 + h, :], Z[:, 6 + h, :], LB[:, 8 + h:9 + h], None, ALU.mult)
                dve.wait_ge(sems["log1p_ready"], 1)
                nc.vector.scalar_tensor_tensor(out=Z[:, 0:4, :], in0=Z[:, 0:4, :], scalar=0.0, in1=T2,
                                               op0=ALU.min, op1=ALU.subtract)
                dve.wait_ge(sems["lb_ready"], 2)
                dve.drain()
                nc.vector.tensor_scalar(Z[:, 0:2, :], Z[:, 0:2, :], 1.0 / 16.0, None, ALU.mult)
                for h in range(2):
                    nc.vector.tensor_scalar(Z[:, 2 + h, :], Z[:, 2 + h, :], LB[:, 12 + h:13 + h], None, ALU.add)
                dve.drain()
                for h in range(2):
                    nc.vector.tensor_scalar(T1[:, h, :], Z[:, 2 + h, :], LB[:, 10 + h:11 + h], None, ALU.subtract)
                dve.drain()
                nc.vector.scalar_tensor_tensor(out=T1[:, 0:2, :], in0=T1[:, 0:2, :], scalar=-1.0,
                                               in1=T1[:, 0:2, :], op0=ALU.mult, op1=ALU.max).then_inc(sems["hdiff_ready"], 1)
                dve.wait_ge(sems["hlog_ready"], 1)
                for h in range(2):
                    nc.vector.scalar_tensor_tensor(out=Z[:, 2 + h, :], in0=Z[:, 2 + h, :],
                                                   scalar=LB[:, 10 + h:11 + h], in1=T2[:, h, :],
                                                   op0=ALU.max, op1=ALU.add)
                dve.drain()
                for f in range(4):
                    last = nc.vector.tensor_tensor_scan(Z[:, f, :], const("chunkmask"), Z[:, f, :], 0.0,
                                                        ALU.mult, ALU.add)
                last.then_inc(sems["b_ready"], 1)
                for s in range(4):
                    scale = 1.0 if s < 2 else 48 ** -0.5
                    for half in range(2):
                        c = slice(half * HALF, (half + 1) * HALF)
                        b = wait_full(dve, "rot", s, half)
                        emptied(nc.vector.scalar_tensor_tensor(out=ROT[:, half, :], in0=b[:, 0:HALF], scalar=scale,
                                                               in1=const("sin")[:, c], op0=ALU.mult,
                                                               op1=ALU.mult), "rot", s, half)
                        nc.vector.scalar_tensor_tensor(out=Z[:, 12 + s, c], in0=Z[:, 12 + s, c], scalar=scale,
                                                       in1=const("cos")[:, c], op0=ALU.mult, op1=ALU.mult)
                        dve.drain()
                        last = nc.vector.tensor_tensor(Z[:, 12 + s, c], Z[:, 12 + s, c], ROT[:, half, :], ALU.add)
                        if s == 3 and half == 1:
                            last.then_inc(sems["z_ready"], 1)

                def low(step):
                    iq = step % 4
                    w = 4 * iq + 4
                    dve.wait_ge(sems["diff_ready"], step + 1)
                    m = const("causal").rearrange("p (i j) -> p i j", j=CH)
                    for i in range(4):
                        p = P[:, step % 2, i, :, 0:w]
                        last = nc.vector.tensor_tensor(
                            p, p, m[:, 4 * iq + i:4 * iq + i + 1, 0:w].to_broadcast([128, NC, w]), ALU.min)
                    last.then_inc(sems["min_ready"], 1)

                def products(step):
                    f, iq = step // 4, step % 4
                    w = 4 * iq + 4
                    dve.wait_ge(sems["pexp_ready"], step + 1)
                    kk = Z[:, 4 + f, 0:NP].rearrange("p (c j) -> p c j", j=CH)
                    qq = Z[:, 8 + f, 0:NP].rearrange("p (c i) -> p c i", i=CH)
                    for i in range(4):
                        p = P[:, step % 2, i, :, 0:w]
                        nc.vector.tensor_tensor(p, p, kk[:, :, 0:w], ALU.mult)
                    dve.drain()
                    for i in range(4):
                        p = P[:, step % 2, i, :, 0:w]
                        at = 4 * iq + i
                        last = nc.vector.tensor_tensor(p, p, qq[:, :, at:at + 1].to_broadcast([128, NC, w]),
                                                       ALU.mult)
                    last.then_inc(sems["p_ready"], 1)

                def keys_and_states(f):
                    k = 4 + f if f < 4 else 10 + f
                    mask = const("mask16")
                    b = wait_full(dve, "kt", f)
                    for n in range(4):
                        if f < 4:
                            if 4 * f + n >= 2:
                                g = 4 * f + n - 2
                                wait_full(dve, "dl", g // 4, g % 4, 1)
                            last = nc.vector.tensor_tensor(
                                KM[:, n % 2], b[:, n * 128:(n + 1) * 128].unsqueeze(1).to_broadcast([128, CT, 128]),
                                mask.unsqueeze(2).to_broadcast([128, CT, 128]), ALU.mult)
                            last.then_inc(sems["km_ready"], 1)
                    if f < 4:
                        dve.wait_ge(sems["km_ready"], 4 * f + 4)
                        dve.sem_inc(free["D"], 1)
                    else:
                        if f == 4:
                            wait_full(dve, "dl", 3, 3, 1)
                        else:
                            wait_full(dve, "rdl", 4)
                        last = nc.vector.tensor_copy(KM[:, 0, 0:4, :], b[:, :].rearrange("p (n d) -> p n d", n=4))
                        emptied(last, "kt", f)
                        dve.wait_ge(free["D"], JOB["kt", f][1] + 1)
                        dve.sem_inc(sems["km_ready"], 1)
                    b = wait_full(dve, "kts", f)
                    if f:
                        wait_full(dve, "dls", f - 1, 1)
                    emptied(nc.vector.tensor_tensor(
                        KMS[0:NS], b[0:NS, 0:128].unsqueeze(1).to_broadcast([NS, NS, 128]),
                        ident[0:NS, 0:NS].unsqueeze(2).to_broadcast([NS, NS, 128]), ALU.mult), "kts", f)
                    wait_emptied(dve, "kts", f)
                    dve.sem_inc(sems["kms_ready"], 1)
                    dve.wait_ge(ss_loaded, 16 * (f + 1))
                    if f < 4:
                        nc.vector.tensor_tensor(SS[:, :, 0:DV[f]], SS[:, :, 0:DV[f]],
                                                DEC[:, f, NC:NC + NS].unsqueeze(2).to_broadcast([128, NS, DV[f]]),
                                                ALU.mult)
                    else:
                        nc.vector.tensor_scalar(SS[:, :, :], SS[:, :, :], const("gam")[:, f - 4:f - 3], None,
                                                ALU.mult)
                    dve.drain()
                    for half in range(2):
                        b = wait_full(dve, "dls", f, half)
                        ss = SS[:, 4 * half:4 * half + 4, 0:DV[f]]
                        emptied(nc.vector.tensor_tensor(
                            ss, ss, b[:, 0:384].rearrange("p (c v) -> p c v", c=4)[:, :, 0:DV[f]], ALU.add),
                            "dls", f, half)
                    wait_emptied(dve, "dls", f, 1)
                    dve.sem_inc(sems["dls_done"], 1)
                    if f < 4:
                        wait_emptied(dve, "dl", f, 3, 1)
                        for c in range(1, NC):
                            last = nc.vector.scalar_tensor_tensor(
                                out=S[:, c, 0:DV[f]], in0=S[:, c - 1, 0:DV[f]], scalar=DEC[:, f, c:c + 1],
                                in1=S[:, c, 0:DV[f]], op0=ALU.mult, op1=ALU.add)
                            if c < NC - 1:
                                dve.drain()
                        last.then_inc(sems["s_ready"], 1)
                    else:
                        wait_emptied(dve, "rdl", f)
                        for n in range(1, 4):
                            last = nc.vector.scalar_tensor_tensor(
                                out=SR[:, n, :], in0=SR[:, n - 1, :], scalar=const("g128")[:, f - 4:f - 3],
                                in1=SR[:, n, :], op0=ALU.mult, op1=ALU.add)
                            if n < 3:
                                dve.drain()
                        last.then_inc(sems["rs_ready"], 1)

                dve.wait_ge(sems["dec_ready"], 1)
                low(0)
                for f in range(4):
                    for iq in range(4):
                        step = 4 * f + iq
                        if iq < 3:
                            low(step + 1)
                        products(step)
                    if f:
                        wait_full(dve, "o", f - 1, 1)
                    q, k, bb = Z[:, 8 + f, 0:NP], Z[:, 4 + f, 0:NP], Z[:, f, 0:NP]
                    qx = SCT[:, 0].rearrange("p n t -> p (n t)")
                    kx = SCT[:, 1].rearrange("p n t -> p (n t)")
                    nc.vector.tensor_copy(qx, bb)
                    b3 = bb.rearrange("p (c i) -> p c i", i=CH)
                    nc.vector.tensor_tensor(kx.rearrange("p (c i) -> p c i", i=CH),
                                            b3[:, :, CH - 1:CH].to_broadcast([128, NC, CH]), b3, ALU.subtract) \
                        .then_inc(sems["ek_ready"], 1)
                    dve.wait_ge(sems["eq_ready"], f + 1)
                    nc.vector.tensor_tensor(q, q, qx, ALU.mult)
                    nc.vector.tensor_tensor(k, k, kx, ALU.mult).then_inc(sems["kq_ready"], 1)
                    b = wait_full(dve, "sc", f)[:, 0:128].rearrange("p (n i h) -> p n i h", n=4, h=2)
                    dve.wait_ge(sems["kq_ready"], f + 1)
                    for h in range(2):
                        for n in range(4):
                            last = nc.vector.tensor_tensor(
                                SCT[:, h, n, :].rearrange("p (c i) -> p c i", i=CH),
                                b[:, n, :, h].unsqueeze(1).to_broadcast([128, CT, CH]),
                                const("mask16").unsqueeze(2).to_broadcast([128, CT, CH]), ALU.mult)
                    last.then_inc(free["D"], 1)
                    wait_emptied(dve, "sc", f)
                    dve.sem_inc(sems["sct_ready"], 1)
                    keys_and_states(f)
                    if f < 3:
                        low(4 * f + 4)
                for f in (4, 5):
                    wait_full(dve, "o", f - 1, 1)
                    for h in range(2):
                        b = wait_full(dve, "rsc", f, h)
                        dm = const("dmat").rearrange("p (h i) -> p h i", h=4)[:, 2 * (f - 4) + h, :]
                        emptied(nc.vector.tensor_tensor(SCT[:, h], b[:, :].rearrange("p (n i) -> p n i", n=4),
                                                        dm.unsqueeze(1).to_broadcast([128, 4, 128]), ALU.mult),
                                "rsc", f, h)
                    wait_emptied(dve, "rsc", f, 1)
                    dve.sem_inc(sems["sct_ready"], 1)
                    for at, table in ((8 + f, "rqdec"), (10 + f, "rkdec")):
                        z = Z[:, at, 0:NP].rearrange("p (n i) -> p n i", n=4)
                        t = const(table).rearrange("p (f i) -> p f i", f=2)[:, f - 4, :]
                        last = nc.vector.tensor_tensor(z, z, t.unsqueeze(1).to_broadcast([128, 4, 128]), ALU.mult)
                    last.then_inc(sems["kq_ready"], 1)
                    keys_and_states(f)

                for s in range(4):
                    for half in range(2):
                        b = wait_full(dve, "mu", s, half)
                        o = OT[0:96, 4 + s, half * HALF:(half + 1) * HALF]
                        last = nc.vector.tensor_tensor(o, o, b[0:96, 0:HALF], ALU.subtract)
                        emptied(last, "mu", s, half)
                    wait_emptied(dve, "mu", s, 1)
                    dve.sem_inc(sems["mu_done"], 1)
                for s in range(10):
                    rows = 96 if s < 8 else 128
                    o = OT[0:rows, s, :]
                    dve.wait_ge(sems["rms_ready"], s + 1)
                    nc.vector.scalar_tensor_tensor(out=o, in0=o, scalar=SM[0:rows, 2 + s:3 + s],
                                                   in1=RS[0:rows, s % 2, :], op0=ALU.mult, op1=ALU.mult)
                    dve.drain()
                    nc.vector.tensor_tensor(o, o, ZG[0:rows, s, :], ALU.mult).then_inc(sems["on_ready"], 1)
                dve.wait_ge(sems["lnp_loaded"], 64)
                for n in range(5):
                    w = WID[n]
                    for half in range(2):
                        c = slice(half * 512, (half + 1) * 512)
                        b = wait_full(dve, "mix", n, half)
                        emptied(nc.vector.scalar_tensor_tensor(out=X[0:w, n, c], in0=X[0:w, n, c], scalar=ALPHA,
                                                               in1=b[0:w, :], op0=ALU.mult, op1=ALU.add),
                                "mix", n, half)
                    dve.drain()
                    statistics(n, X[:, n, :])
                    if n:
                        normalize(n - 1, X[:, n - 1, :], 0, n, "x1_ready")
                normalize(4, X[:, 4, :], 0, 5, "x1_ready")
                to_features(1)
                for m in range(16):
                    b = wait_full(dve, "q", m, 1)
                    emptied(nc.vector.tensor_copy(QT[:, m, HALF:T], b[:, 0:HALF]), "q", m, 1)
                wait_emptied(dve, "s", 0, 3)
                for part in range(4):
                    top(0, 0, part)
                for n in range(4):
                    if n == 0:
                        with dve.Fori(0, PH - 1) as h:
                            for part in range(4):
                                dots(L, 0, h, 4 * part, 4 * part + 4)
                                top(0, h + 1, part)
                        dots(L, 0, PH - 1, 0, TOPK)
                    else:
                        with dve.Fori(0, PH) as h:
                            dots(L, n, h, 0, TOPK)
                    dve.drain().then_inc(sems["score_ready"], 1)
                    if n == 0:
                        dve.sem_inc(sems["rprod_ready"], 1)
                        softmax_sums(0)
                    nc.vector.tensor_scalar(X[:, n, :], X[:, n, :], ALPHA, None, ALU.mult)
                    dve.drain()
                    dve.wait_ge(sems["gelu_ready"], n + 1)
                    nc.vector.tensor_tensor(WGT, WGT, GATE[:, n, :], ALU.mult).then_inc(sems["w_ready"], 1)
                    if n:
                        add_embedding(n - 1)
                    wait_emptied(dve, "s", n + 1, 3)
                    with dve.Fori(0, PH) as h:
                        for part in range(4):
                            j = RING // 2 * part + RING // 2 - 1
                            k = j % RING
                            dve.drain()
                            dve.wait_ge(fetched[k], L * (16 * USES) + h * (16 * GPH)
                                        + 16 * (n * 2 * NGRP + NGRP + j // RING + 1))
                            nc.vector.scalar_tensor_tensor(
                                out=X[:, n, :], in0=G[:, k, :], scalar=WGT[:, ds(h * TOPK + j, 1)],
                                in1=X[:, n, :], op0=ALU.mult, op1=ALU.add).then_inc(sems["vd_used"], 1)
                            top(n + 1, h, part)
                    dve.drain().then_inc(sems["rprod_ready"], 1)
                    if n == 3:
                        dve.sem_inc(sems["et_ready"], 1)
                        b = wait_full(dve, "et")
                        emptied(nc.vector.tensor_copy(IDXS, b[:, 0:NS]), "et")
                        wait_emptied(dve, "et")
                        dve.sem_inc(sems["idx_ready"], 1)
                    dve.wait_ge(sems["acc_ready"], n + 1)
                    nc.vector.tensor_tensor(X[:, n, :], X[:, n, :], Y[:, :], ALU.add).then_inc(sems["y_read"], 1)
                    dve.drain()
                    statistics(n, X[:, n, :])
                    last = softmax_sums(n + 1)
                    if n == 3:
                        last.then_inc(sems["et_ready"], 1)
                    normalize(n, X[:, n, :], 1, n + 6, "x2_ready")
                b = wait_full(dve, "gt")
                emptied(nc.vector.tensor_copy(GATES, b[:, 0:NS]), "gt")
                for t in range(NS):
                    dve.wait_ge(fetched[t], L * (16 * USES) + 16 * (USES - 1))
                    dve.wait_ge(sems["xb_ready"], t + 1)
                    nc.vector.scalar_tensor_tensor(out=G[:, t, :], in0=G[:, t, :], scalar=1.0, in1=Y[:, :],
                                                   op0=ALU.mult, op1=ALU.mult, accum_out=SSC[:, t:t + 1]) \
                        .then_inc(sems["u_used"], 1)
                    dve.wait_ge(sems["u_used"], RING + 4 * SLOTS + t + 1)
                    dve.sem_inc(sems["xb_used"], 1)
                dve.drain().then_inc(sems["score_ready"], 1)
                dve.wait_ge(sems["gelu_ready"], 5)
                nc.vector.tensor_tensor(WS, WS, GATES, ALU.mult)
                dve.drain()
                nc.vector.tensor_tensor(WS8, WS.unsqueeze(2).to_broadcast([128, NS, NS]),
                                        const("eye8").rearrange("p (a b) -> p a b", a=8), ALU.mult) \
                    .then_inc(sems["wsam_ready"], 1)
                add_embedding(3)
                dve.wait_ge(sems["acc_ready"], 5)
                statistics(4, Y)
                normalize(4, Y, 1, 10, "x2_ready")
                add_embedding(4)
                nc.vector.tensor_scalar(LBASE[:, :], LBASE[:, :], float(NEXP), None, ALU.add)
                nc.vector.tensor_copy(LB[:, 4:6], LB[:, 14:16])
                arrive(dve, L)


def kernel(x_prompt, x_sample, p_prompt, p_sample, state_gla, state_ret, state_hgrn,
           w_in, gla_w_gate, gla_b_gate, gla_norm, ret_norm, hgrn_lb_logits, hgrn_norm, w_out,
           ln1_g, ln1_b, ln2_g, ln2_b, peer_w_q, peer_subkeys, peer_u, peer_v, ple_proj, ple_gate):
    import numpy as np
    import concourse.bacc as bacc
    from concourse.bass_utils import run_bass_kernel_spmd

    f32 = np.float32
    cols = {n: np.zeros((128, w), f32) for n, (_, w) in CONSTS.items()}
    p = np.arange(128)
    cols["ident"][:] = np.eye(128)
    cols["aident"][:] = np.eye(128) * ALPHA
    cols["onesg"][:96] = f32(1 / 96)
    cols["onesh"][:] = (p[:, None] // 64 == p[None] // 64) / 64
    cols["headsel"][:] = p[:, None] // 64 == np.arange(2)
    cols["mask16"][:] = p[:, None] // CH == np.arange(CT)
    cols["causal"][:] = np.where(np.arange(CH)[:, None] >= np.arange(CH)[None], 0.0, -1e30).reshape(1, -1)
    cols["eye8"][:] = np.eye(8).reshape(1, 64)
    cols["eps"][:] = EPS
    cols["iota"][:] = np.arange(16)
    t = np.arange(T)
    cols["chunkmask"][:] = (t < NP) & (t % CH != 0)
    inv = (f32(1) / (f32(10000.0) ** (np.arange(0, 48, 2, dtype=f32) / f32(48)))).astype(f32)
    pos = np.where(t < NP, t, 4096).astype(f32)
    ang = pos[None, :] * inv[:, None]
    gamma = np.log1p(-np.exp2(-5.0 - np.arange(4)))
    for h in range(2):
        for i in range(24):
            a, b = 64 * h + i, 64 * h + 24 + i
            cols["perm"][a, b] = cols["perm"][b, a] = 1
            cols["cos"][a] = cols["cos"][b] = np.cos(ang[i])
            cols["sin"][a], cols["sin"][b] = -np.sin(ang[i]), np.sin(ang[i])
    i = np.arange(128)
    for h in range(4):
        f, rows = h // 2, slice(64 * (h % 2), 64 * (h % 2) + 64)
        dist = i[None, :] - i[:, None]
        cols["dmat"][:, h * 128:(h + 1) * 128] = np.where(dist >= 0, np.exp(gamma[h] * np.maximum(dist, 0)), 0)
        cols["rqdec"][rows, f * 128:(f + 1) * 128] = np.exp(gamma[h] * (i + 1))
        cols["rkdec"][rows, f * 128:(f + 1) * 128] = np.exp(gamma[h] * (127 - i))
        cols["g128"][rows, f] = np.exp(gamma[h] * 128)
        cols["gam"][rows, f] = np.exp(gamma[h])
    consts = np.concatenate(list(cols.values()), axis=1)

    def arr(a):
        return np.ascontiguousarray(a)

    w_in, w_out = arr(w_in), arr(w_out)

    def pairs(at, width, f):
        out = np.zeros((DEPTH, D, 128), f32)
        for h in range(2):
            o = at + (2 * f + h) * width
            out[:, :, 64 * h:64 * h + width] = w_in[:, :, o:o + width]
        return out

    def wide(at, width, count):
        out = np.zeros((DEPTH, D, 128), f32)
        out[:, :, :width] = w_in[:, :, at:at + width]
        return out

    tiles = {"hf0": pairs(2576, 64, 0), "hf1": pairs(2576, 64, 1), "glr": wide(1152, 16, 1),
             "hq0": pairs(2320, 64, 0), "hq1": pairs(2320, 64, 1), "gk0": pairs(192, 48, 0),
             "gk1": pairs(192, 48, 1), "gq0": pairs(0, 48, 0), "gq1": pairs(0, 48, 1),
             "rq0": pairs(1168, 48, 0), "rq1": pairs(1168, 48, 1), "rk0": pairs(1360, 48, 0),
             "rk1": pairs(1360, 48, 1)}
    feat = np.concatenate([tiles[n] for n in FEATURES] + [np.zeros((DEPTH, D, 128), f32)], axis=2)
    vals = np.concatenate([w_in[:, :, 384:768], w_in[:, :, 1552:1936], w_in[:, :, 2832:3088]], axis=2)
    gate = np.concatenate([wide(768 + 96 * h, 96, 1) for h in range(4)]
                          + [wide(1936 + 96 * h, 96, 1) for h in range(4)]
                          + [pairs(3088, 64, 0), pairs(3088, 64, 1)], axis=2)
    ws = np.zeros((DEPTH, ITEMS, 128, 2048), f32)

    def put(first, m):
        n = m.shape[2] // 256
        v = m.reshape(DEPTH, KT, 128, n, 256).transpose(0, 3, 2, 1, 4)
        ws[:, first:first + n] = v.reshape(DEPTH, n, 128, 2048)

    put(0, feat)
    put(I_V, vals)
    put(I_GATE, gate)
    put(I_WQ, arr(peer_w_q))
    put(I_PG, arr(ple_gate))
    sub = arr(peer_subkeys).reshape(DEPTH, 16, 128, 128).transpose(0, 3, 1, 2)
    ws[:, I_SUB, :, :1024] = sub[:, :, :8].reshape(DEPTH, 128, 1024)
    ws[:, I_SUB + 1, :, :1024] = sub[:, :, 8:].reshape(DEPTH, 128, 1024)
    ws[:, I_PP] = arr(ple_proj).reshape(DEPTH, 2, 128, D).transpose(0, 2, 1, 3).reshape(DEPTH, 128, 2048)
    pt = np.concatenate([arr(p_prompt).reshape(DEPTH, NP, 256), arr(p_sample).reshape(DEPTH, NS, 256)], axis=1)
    pt = pt.transpose(0, 2, 1).reshape(DEPTH, 2, 128, T).transpose(0, 2, 1, 3)
    ws[:, I_PT, :, :2 * T] = pt.reshape(DEPTH, 128, 2 * T)
    wo = np.zeros((DEPTH, 128, 10, D), f32)
    for h in range(8):
        wo[:, :96, h] = w_out[:, 96 * h:96 * h + 96]
    wo[:, :, 8], wo[:, :, 9] = w_out[:, 768:896], w_out[:, 896:1024]
    small = np.zeros((DEPTH, 128, NSMALL), f32)
    for f in range(2):
        for h in range(2):
            c = slice((2 * f + h) * 48, (2 * f + h + 1) * 48)
            small[:, 64 * h:64 * h + 48, f] = arr(gla_b_gate)[:, c]
            small[:, :16, 12 + f * 128 + 64 * h:12 + f * 128 + 64 * h + 48] = arr(gla_w_gate)[:, :, c]
    small[:, :96, 2:6] = arr(gla_norm).transpose(0, 2, 1)
    small[:, :96, 6:10] = arr(ret_norm).transpose(0, 2, 1)
    small[:, :, 10:12] = arr(hgrn_norm).reshape(DEPTH, 2, 128).transpose(0, 2, 1)
    lnp = np.stack([arr(a) for a in (ln1_g, ln1_b, ln2_g, ln2_b)], axis=1)
    lblog = arr(arr(hgrn_lb_logits).reshape(DEPTH, 2, 128).transpose(2, 0, 1).reshape(128, 4))
    st_in = np.zeros((DEPTH, 6, 128, NS, 96), f32)
    places = ((arr(state_gla), 0, 48, 96), (arr(state_hgrn), 2, 64, 64), (arr(state_ret), 4, 48, 96))
    for state, f0, dk, dv in places:
        for h in range(4):
            st_in[:, f0 + h // 2, 64 * (h % 2):64 * (h % 2) + dk, :, :dv] = state[:, :, h].transpose(0, 2, 1, 3)
    x = np.concatenate([arr(x_prompt).reshape(NP, D), arr(x_sample).reshape(NS, D)])
    u, v = arr(peer_u).reshape(DEPTH * NEXP, D), arr(peer_v).reshape(DEPTH * NEXP, D)

    nc = bacc.Bacc("TRN2", target_bir_lowering=False, num_devices=1)
    arrays = {"x": x, "wstream": ws, "wout": wo, "small": small, "lnp": lnp, "lblog": lblog, "st_in": st_in,
              "consts": consts, "utab": u, "vtab": v}
    outs = {"y": (T, D), "st_p": (DEPTH, 6, 128, 96), "st_s": (DEPTH, 6, 128, NS, 96)}
    fp32 = mybir.dt.float32
    args = [nc.dram_tensor(f"in_{n}", a.shape, fp32, kind="ExternalInput").ap() for n, a in arrays.items()]
    args += [nc.dram_tensor(f"out_{n}", s, fp32, kind="ExternalOutput").ap() for n, s in outs.items()]
    build(nc, *args)
    r = run_bass_kernel_spmd(nc, [{f"in_{n}": a for n, a in arrays.items()}], core_ids=[0]).results[0]
    y, st_p, st_s = (r[f"out_{n}"] for n in outs)

    def heads(st, f0, dk, dv):
        return np.stack([st[:, f0 + h // 2, 64 * (h % 2):64 * (h % 2) + dk, ..., :dv] for h in range(4)], axis=2)

    new_p, new_s = [], []
    for f0, dk, dv in ((0, 48, 96), (4, 48, 96), (2, 64, 64)):
        new_p.append(heads(st_p, f0, dk, dv).transpose(0, 2, 1, 3)[:, None])
        new_s.append(heads(st_s, f0, dk, dv).transpose(0, 3, 2, 1, 4))
    return (y[:NP].reshape(1, NP, D), y[NP:].reshape(NS, 1, D), *map(arr, new_p), *map(arr, new_s))
```

```python
import concourse.bass as bass
from concourse import mybir
from contextlib import ExitStack

D, T, NP, NS = 1024, 520, 512, 8
WID = [128, 128, 128, 128, 8]
KT = D // 128
HALF = T // 2
CH = 16
NC = NP // CH
CT = 128 // CH
DEPTH = 2
ALPHA = (2 * DEPTH) ** 0.25
EPS = 1e-5
PH, TOPK, NKEY = 8, 16, 128
SLOTS = PH * TOPK
NEXP = NKEY * NKEY
RING = 8
NGRP = SLOTS // RING
USES = 2 * 4 * NGRP + 2
GPH = TOPK // RING
PE_ROWS = [[0, 1, 2, 4, 5, 6]] * 3 + [[0, 2, 4, 6]]
DVE_ROWS = [[3, 7]] * 3 + [[1, 3, 5, 7]]
PEG, DVG = len(PE_ROWS[0]), len(DVE_ROWS[0])
TAIL = [0, 1, 2, 4, 3]


def rows_used(rows, n, done):
    per = len(rows[n])
    return len(rows[0]) * (n * NGRP + 1) - per + done * per // 2, per


BREAKS = [3, 6, 9, 12]


def fetches_before(n, phase):
    return (2 * n + phase) * NGRP + (1 + phase if n == 3 else 0)


DV = [96, 96, 64, 64, 96, 96]
VCOL = [0, 192, 768, 896, 384, 576]
SEQ = [4, 5, 0, 1, 2, 3]
STEPS = [[0, 1], [2, 3], [4, 5, 6, 7], [8, 9, 10, 11], [12, 13, 14, 15], []]
HEADS = {4: [4, 5], 5: [6, 7], 0: [0, 1], 1: [2, 3], 2: [8], 3: [9]}
ORDER = [s for f in SEQ for s in HEADS[f]]
ZGATE = {4: 12, 5: 14, 6: 13, 7: 15, 0: 0, 1: 4, 2: 1, 3: 5, 8: 2, 9: 8}
EARLY, LATE = [5, 6, 7, 8], [0, 1, 2, 3, 4, 9]
ITEMS, SLOTW = 34, 4

FEATURES = ["hf0", "hf1", "glr", "hq0", "hq1", "gk0", "gk1", "gq0", "gq1", "rq0", "rq1", "rk0", "rk1"]
ZSLOT = {"hf0": 2, "hf1": 3, "hq0": 10, "hq1": 11, "gk0": 4, "gk1": 5, "gq0": 8, "gq1": 9,
         "rq0": 12, "rq1": 13, "rk0": 14, "rk1": 15}
I_V, I_GATE, I_WQ, I_PP, I_PT, I_PG = 7, 11, 16, 28, 29, 30
I_Q = [I_WQ + j + j // 2 for j in range(8)]
I_SUB = [I_WQ + 3 * c + 2 for c in range(4)]

CONSTS = {}
_at = 0
for _n, _w in (("ident", 128), ("perm", 128), ("onesg", 96), ("onesh", 128), ("dmat", 512), ("cos", 520),
               ("sin", 520), ("chunkmask", 520), ("mask16", 8), ("causal", 256), ("rqdec", 256),
               ("rkdec", 256), ("headsel", 62), ("g128", 2), ("gam", 2), ("eye8", 64), ("eps", 1),
               ("aident", 128), ("iota", 16)):
    CONSTS[_n] = (_at, _w)
    _at += _w
NCONST = _at
NSMALL = 268


ROTATED = [[0], [1], [2, 3], []]


def jobs():
    found, count = {}, {"A": 0, "D": 0}

    def add(ring, *name):
        found[name] = (ring, count[ring])
        count[ring] += 1

    def to_features(stage):
        for n in range(5):
            add("A", "xt", stage, n, 0)
            add("D", "xt", stage, n, 1)

    to_features(0)
    for m, name in enumerate(FEATURES):
        add("A", "z", m, 0)
        add("D", "z", m, 1)
        if name == "hq0":
            for g in range(2):
                for half in range(2):
                    add("D", "ga", g, half)
    for i in range(4):
        for n in range(5):
            add("A", "v", i, n)
        for s in ROTATED[i]:
            for half in range(2):
                add("D", "rot", s, half)
    def gate(s):
        for half in range(2):
            add("A", "g", s, half)

    def means(s):
        for half in range(2):
            if 4 <= s < 8:
                add("D", "mu", s, half)

    def squares(s):
        for half in range(2):
            add("A", "ms", s, half)

    for i, f in enumerate(SEQ):
        before = HEADS[SEQ[i - 1]] if i else []
        for s in before:
            means(s)
        if f >= 4:
            add("D", "rsc", f, 0)
            add("D", "rsc", f, 1)
        add("D", "kt", f)
        add("D", "kts", f)
        if f < 4:
            for n in range(4):
                for half in range(2):
                    add("A", "dl", f, n, half)
        else:
            add("A", "rdl", f)
        for half in range(2):
            add("D", "dls", f, half)
        for h in range(2):
            add("A", "os", f, h)
        for s in before:
            squares(s)
        for s in before + (HEADS[f] if i == 5 else []):
            gate(s)
        for h in range(2):
            add("A", "o", f, h)
    for s in HEADS[SEQ[-1]]:
        squares(s)
    for n in range(5):
        for half in range(2):
            add("D", "mix", n, half)
    to_features(1)
    for c in range(4):
        for m in range(4 * c, 4 * c + 4):
            add("A", "q", m, 0)
            add("A", "q", m, 1)
        for n in range(5):
            add("A", "s", n, c)
    for n in range(5):
        for half in range(2):
            add("A", "pp", n, half)
    add("D", "et")
    add("D", "gt")
    for t in range(NS):
        for half in range(2):
            add("D", "xb", t, half)
    for half in range(2):
        add("D", "sacc", half)
    for n in TAIL:
        for kg in range(2):
            add("A", "x2t", n, kg)
        for c in range(4):
            add("A", "pg", n, c)
    return found


SIGNALS = """w_consumed layer_arrived sigm_ready abs_ready log1p_ready hdiff_ready hlog_ready b_ready
dec_ready eq_ready ek_ready kq_ready diff_ready min_ready pexp_ready p_ready p_used sc_copied sc_turned sc_read sct_ready
km_ready kms_ready dls_done s_ready rs_ready rq_ready ss_scaled z_ready mu_done sq_ready
rms_ready on_scaled on_ready mv_ready rstd_ready x1_ready idx_staged lb_ready
u_used v_used vd_used y_read idx_known score_ready gelu_ready w_ready sample_idx sample_score sample_gelu sample_v_used diag_ready acc_ready idx_ready et_ready
wsam_ready x2_ready ple_sig_ready x_ready silu_ready rprod_ready small_init places_free all_arrived
""".split()
DMASIGNALS = "x_loaded small_loaded lnp_loaded wout_loaded".split()
KEPT = "consts_loaded layer_go layer_done y_stored".split()


def build(nc, x_in, wstream, wout, small, lnp, lblog, st_in, consts, utab, vtab, y_out, st_p, st_s):
    fp32, i32, u32 = mybir.dt.float32, mybir.dt.int32, mybir.dt.uint32
    ALU = mybir.AluOpType
    ACT = mybir.ActivationFunctionType
    AX = mybir.AxisListType
    JOB = jobs()
    ds = bass.ds

    ctx = ExitStack()
    with ctx:
        def sb(name, *shape, dt=fp32):
            return ctx.enter_context(nc.sbuf_tensor(name, list(shape), dt))

        X = sb("X", 128, 5, D)
        XT = sb("XT", 128, KT, T)
        C = sb("C", 128, NCONST)
        WR = sb("WR", 128, SLOTW, 2048)
        SM = sb("SM", 128, NSMALL)
        LB = sb("LB", 128, 16)
        ST = sb("ST", 128, 5, 16)
        R = sb("R", 128, 30288)

        def view(at, *dims):
            n = 1
            for d in dims:
                n *= d
            v = R[:, at:at + n]
            if len(dims) == 1:
                return v
            names = "abcde"[:len(dims)]
            return v.rearrange(f"p ({' '.join(names)}) -> p {' '.join(names)}",
                               **{names[i]: dims[i] for i in range(1, len(dims))})

        Z = view(0, 16, T)
        OT = view(8320, 10, T)
        V = view(13520, 5, D)
        P = view(18640, 2, 4, NC, CH)
        T1 = view(18640, 4, T)
        T2 = view(20720, 4, T)
        S = view(22736, NC, 96)
        ROT = view(22800, 2, HALF)
        WO = view(13520, 10, D)
        SR = view(25808, 4, 96)
        KM = view(26192, 2, CT, 128)
        KMS = view(28240, CT, 128)
        SCT = view(29264, 2, 4, 128)
        LNP = view(25808, 4, D)
        QT = view(0, 8, T)
        G = view(8320, RING, D)
        XTF = XT.rearrange("p k t -> p (k t)")
        PP = [view(1024 * n, D) for n in range(4)] + [XTF[:, 2048:2048 + D]]
        SG = XTF[:, 0:D]
        X2T = XTF[:, D:2 * D].rearrange("p (k t) -> p k t", k=KT)
        IDXS = view(30096, NS).bitcast(i32)
        GATES = view(30104, NS)
        SSC = view(30112, NS)
        WS = view(30120, NS)
        WS8 = view(30128, NS, NS)
        SSH = view(30192, 2, NS)
        IDX = view(16512, 4, SLOTS).bitcast(i32)
        GATE = view(17024, 5, SLOTS)
        WGT = view(17664, SLOTS)
        SCORE = view(17792, SLOTS)
        SC = [view(at, 2 * PH * NKEY) for at in (17920, 4160, 6208, 22016, 19968)]
        DIAG = view(24064, RING, 128)
        STG = view(25088, 2, NKEY)
        CAND = view(25344, TOPK, TOPK)
        EQT = view(25088, 2, TOPK, TOPK)
        VV = view(25600, 2, TOPK)
        II = view(25632, 2, TOPK).bitcast(u32)
        IF = view(25664, 2, TOPK)
        BEST = view(25696, TOPK)
        CI = view(25712, TOPK).bitcast(u32)
        CAB = view(25728, 2, TOPK).bitcast(u32)
        ABF = view(25760, 2, TOPK)
        IST = view(25792, 2, RING).bitcast(i32)
        SEL = view(29904, 2, TOPK)
        SUM = view(29936, 2, PH)
        EF = view(29952, TOPK)
        EFS = view(29968, SLOTS)
        SS = sb("SS", 128, NS, 96)
        RS = sb("RS", 128, T)
        DEC = sb("DEC", 128, 4, NC + NS)
        LBASE = sb("LBASE", 128, 1)

        A = [ctx.enter_context(nc.psum_tensor(f"A{i}", [128, 512], fp32)) for i in range(3)]
        DB = [ctx.enter_context(nc.psum_tensor(f"D{i}", [128, 512], fp32)) for i in range(3)]
        Y = ctx.enter_context(nc.psum_tensor("Y", [128, D], fp32))
        BANKS = {"A": A, "D": DB}

        sems = {n: ctx.enter_context(nc.semaphore(n)) for n in SIGNALS + DMASIGNALS + KEPT}
        full = {r: ctx.enter_context(nc.semaphore(f"{r}_full")) for r in "AD"}
        free = {r: ctx.enter_context(nc.semaphore(f"{r}_free")) for r in "AD"}
        w_loaded = [ctx.enter_context(nc.semaphore(f"w_loaded{i}")) for i in range(SLOTW)]
        fetched = [ctx.enter_context(nc.semaphore(f"fetched{i}")) for i in range(RING)]
        ss_loaded = ctx.enter_context(nc.semaphore("ss_loaded"))
        ss_stored = ctx.enter_context(nc.semaphore("ss_stored"))
        s_stored = ctx.enter_context(nc.semaphore("s_stored"))
        cleared = [sems[n] for n in SIGNALS + DMASIGNALS] + list(full.values()) + list(free.values()) \
            + w_loaded + [ss_loaded, ss_stored, s_stored]

        block = ctx.enter_context(nc.Block())

        def const(name, rows=128):
            at, n = CONSTS[name]
            return C[0:rows, at:at + n]

        ident = const("ident")

        def wait_full(eng, *name):
            ring, j = JOB[name]
            eng.wait_ge(full[ring], j + 1)
            return BANKS[ring][j % 3]

        def wait_emptied(eng, *name):
            ring, j = JOB[name]
            eng.wait_ge(free[ring], j + 1)

        def arrive(eng, L):
            eng.drain()
            eng.sem_inc(sems["layer_done"], 1)
            eng.wait_ge(sems["layer_go"], L + 1)

        def roots(s):
            if s in (1, 3):
                return Z[:, 8 + s // 2, :]
            return OT[:, 8, :] if s in (5, 7) else RS

        SCROWS = slice(64, 64 + 2 * CH)
        SCSUM = Y[SCROWS, 0:512].rearrange("p (c j) -> p c j", j=CH)
        SCB = Y[:, 512:512 + 128].rearrange("p (n i h) -> p n i h", n=4, h=2)
        SCCOPY = R[SCROWS, 28240:28240 + NP]

        def quarter(step):
            return step // 4, 3 - step % 4

        KM_COUNT = {f: sum(1 if e >= 4 else 4 for e in SEQ[:i]) for i, f in enumerate(SEQ)}

        def oplace(f, h):
            if f in (2, 3):
                return 8 + f - 2, h * 64, 64
            return (2 * f + h if f < 2 else 4 + 2 * (f - 4) + h), 0, 96

        def vcols(f, h):
            return slice(VCOL[f] + h * DV[f], VCOL[f] + (h + 1) * DV[f])

        @block.sync
        def _(sp):
            sp.dma_start(C[:, :], consts).then_inc(sems["consts_loaded"], 16)
            sp.dma_start(X[:, 0:4, :], x_in[0:NP].rearrange("(n p) d -> p n d", p=128)) \
                .then_inc(sems["consts_loaded"], 16)
            sp.dma_start(X[0:NS, 4, :], x_in[NP:T]).then_inc(sems["consts_loaded"], 16)
            sp.dma_start(LB[:, 0:4], lblog).then_inc(sems["consts_loaded"], 16)

            def item(L, i):
                if i >= SLOTW:
                    sp.wait_ge(sems["w_consumed"], i - SLOTW + 1)
                n = 512 if i in I_SUB else 2 * T if i == I_PT else 2048
                sp.dma_start(WR[:, i % SLOTW, 0:n], wstream[L, i, :, 0:n]).then_inc(w_loaded[i % SLOTW], 16)

            with sp.Fori(0, DEPTH) as L:
                sp.dma_start(SM[:, :], small[L]).then_inc(sems["small_loaded"], 16)
                for i in range(I_GATE):
                    item(L, i)
                def new_states(i):
                    f = SEQ[i]
                    sp.wait_ge(sems["dls_done"], i + 1)
                    sp.dma_start(st_s[L, f], SS[:, :, :]).then_inc(ss_stored, 16)
                    if i < 5:
                        wait_full(sp, "os", f, 1)
                        sp.wait_ge(ss_stored, 16 * (i + 1))
                        sp.dma_start(SS[:, :, :], st_in[L, SEQ[i + 1]]).then_inc(ss_loaded, 16)
                    if f < 4:
                        sp.wait_ge(sems["s_ready"], f + 1)
                        sp.dma_start(st_p[L, f], S[:, NC - 1, :]).then_inc(s_stored, 16)
                    else:
                        sp.wait_ge(sems["rs_ready"], f - 3)
                        sp.dma_start(st_p[L, f], SR[:, 3, :]).then_inc(s_stored, 16)

                sp.dma_start(SS[:, :, :], st_in[L, SEQ[0]]).then_inc(ss_loaded, 16)
                for i in range(I_GATE, I_GATE + SLOTW):
                    item(L, i)
                for i in range(5):
                    new_states(i)
                    if i == 2:
                        item(L, I_WQ - 1)
                sp.wait_ge(sems["p_used"], 16)
                sp.dma_start(WO[:, 5:9, :], wout[L][:, 5:9, :]).then_inc(sems["wout_loaded"], 16)
                new_states(5)
                wait_full(sp, "o", 3, 1)
                sp.wait_ge(s_stored, 96)
                sp.wait_ge(sems["wout_loaded"], 16)
                sp.dma_start(WO[:, 0:5, :], wout[L][:, 0:5, :]).then_inc(sems["wout_loaded"], 16)
                sp.dma_start(WO[:, 9, :], wout[L][:, 9, :]).then_inc(sems["wout_loaded"], 16)
                sp.wait_ge(ss_stored, 96)
                for j in range(4):
                    sp.dma_start(LNP[:, j, :], lnp[L, j:j + 1, :].to_broadcast([128, D])) \
                        .then_inc(sems["lnp_loaded"], 16)
                for i in range(I_WQ, ITEMS):
                    item(L, i)
                for s in range(SLOTW):
                    sp.wait_ge(w_loaded[s], 16 * len(range(s, ITEMS, SLOTW)))
                sp.sem_inc(sems["layer_done"], 1)
                sp.wait_ge(sems["layer_done"], L * 5 + 5)
                sp.sem_inc(sems["all_arrived"], 1)
                for s in cleared:
                    sp.sem_clear(s)
                sp.sem_inc(sems["layer_go"], 1)
            sp.dma_start(y_out[0:NP].rearrange("(n p) d -> p n d", p=128), X[:, 0:4, :]) \
                .then_inc(sems["y_stored"], 16)
            sp.dma_start(y_out[NP:T], X[0:NS, 4, :]).then_inc(sems["y_stored"], 16)
            sp.wait_ge(sems["y_stored"], 32)

        @block.tensor
        def _(pe):
            def bank(*name):
                ring, j = JOB[name]
                if j >= 3:
                    pe.wait_ge(free[ring], j - 2)
                return BANKS[ring][j % 3]

            def done(last, *name):
                last.then_inc(full[JOB[name][0]], 1)

            def weights(i):
                pe.wait_ge(w_loaded[i % SLOTW], 16 * (i // SLOTW + 1))
                return WR[:, i % SLOTW, :]

            def consumed(last):
                last.then_inc(sems["w_consumed"], 1)

            def to_features(stage):
                for n in range(5):
                    w = WID[n]
                    if stage == 1:
                        pe.wait_ge(sems["x1_ready"], n + 1)
                    for kg in range(2):
                        b = bank("xt", stage, n, kg)
                        for k in range(4):
                            last = nc.tensor.transpose(b[:, k * w:(k + 1) * w],
                                                       X[0:w, n, (4 * kg + k) * 128:(4 * kg + k + 1) * 128],
                                                       ident[0:w, 0:w])
                        done(last, "xt", stage, n, kg)
                wait_emptied(pe, "xt", stage, 4, 0)
                wait_emptied(pe, "xt", stage, 4, 1)

            def project(i, c, rhs, *name):
                w = weights(i).rearrange("p (k n) -> p k n", k=KT)
                for half in range(2):
                    b = bank(*name, half)
                    for k in range(KT):
                        last = nc.tensor.matmul(b[:, 0:HALF], w[:, k, c * 128:(c + 1) * 128],
                                                rhs[:, k, half * HALF:(half + 1) * HALF],
                                                start=(k == 0), stop=(k == KT - 1))
                    done(last, *name, half)
                return last

            pe.wait_ge(sems["consts_loaded"], 64)
            with pe.Fori(0, DEPTH) as L:
                to_features(0)
                for m, name in enumerate(FEATURES):
                    last = project(m // 2, m % 2, XT, "z", m)
                    if m % 2 or m == len(FEATURES) - 1:
                        pe.wait_ge(full["D"], JOB["z", m, 1][1] + 1)
                        pe.sem_inc(sems["w_consumed"], 1)
                    if name == "hq0":
                        pe.wait_ge(sems["small_loaded"], 16)
                        wait_emptied(pe, "z", 2, 0)
                        wait_emptied(pe, "z", 2, 1)
                        for g in range(2):
                            for half in range(2):
                                b = bank("ga", g, half)
                                done(nc.tensor.matmul(b[:, 0:HALF], SM[0:16, 12 + g * 128:12 + (g + 1) * 128],
                                                      T1[0:16, 0, half * HALF:(half + 1) * HALF],
                                                      start=True, stop=True), "ga", g, half)
                for i in range(4):
                    w = weights(I_V + i).rearrange("p (k n) -> p k n", k=KT)
                    for n in range(5):
                        b = bank("v", i, n)
                        for k in range(KT):
                            last = nc.tensor.matmul(b[0:WID[n], 0:256], XT[:, k, n * 128:n * 128 + WID[n]],
                                                    w[:, k, :], start=(k == 0), stop=(k == KT - 1))
                        done(last, "v", i, n)
                    pe.wait_ge(full["A"], JOB["v", i, 4][1] + 1)
                    pe.sem_inc(sems["w_consumed"], 1)
                    for s in ROTATED[i]:
                        m = FEATURES.index(("rq0", "rq1", "rk0", "rk1")[s])
                        wait_emptied(pe, "z", m, 0)
                        wait_emptied(pe, "z", m, 1)
                        for half in range(2):
                            b = bank("rot", s, half)
                            done(nc.tensor.matmul(b[:, 0:HALF], const("perm"),
                                                  Z[:, 12 + s, half * HALF:(half + 1) * HALF],
                                                  start=True, stop=True), "rot", s, half)
                wait_emptied(pe, "v", 3, 4)

                def score_step(step):
                    f, iq = quarter(step)
                    if step % 4 == 0 and f:
                        pe.wait_ge(sems["sc_copied"], f)
                    pe.wait_ge(sems["p_ready"], step + 1)
                    w = 4 * iq + 4
                    at, _ = CONSTS["headsel"]
                    for k in range(4):
                        i = 4 * iq + k
                        last = nc.tensor.matmul(SCSUM[:, :, 0:w], C[:, at + 30 - 2 * i:at + 62 - 2 * i],
                                                P[:, step % 2, k, :, 0:w],
                                                start=(step % 4 == 0 and k == 0), stop=(step % 4 == 3 and k == 3))
                    last.then_inc(sems["p_used"], 1)

                def turn_scores(f):
                    pe.wait_ge(sems["sc_copied"], f + 1)
                    if f:
                        pe.wait_ge(sems["sc_read"], f)
                    for n in range(4):
                        last = nc.tensor.transpose(SCB[:, n].rearrange("p i h -> p (i h)"),
                                                   SCCOPY[:, n * 128:(n + 1) * 128], ident[SCROWS, SCROWS])
                    last.then_inc(sems["sc_turned"], 1)

                def output_gate(s):
                    t = ORDER.index(s)
                    project(I_GATE + t // 2, t % 2, XT, "g", s)
                    if t % 2:
                        pe.wait_ge(full["A"], JOB["g", s, 1][1] + 1)
                        pe.sem_inc(sems["w_consumed"], 1)

                def means(s):
                    for half in range(2):
                        if 4 <= s < 8:
                            b = bank("mu", s, half)
                            done(nc.tensor.matmul(b[0:96, 0:HALF], const("onesg", 96),
                                                  OT[0:96, s, half * HALF:(half + 1) * HALF],
                                                  start=True, stop=True), "mu", s, half)

                def mean_squares(s):
                    rows = 96 if s < 8 else 128
                    pe.wait_ge(sems["sq_ready"], ORDER.index(s) + 1)
                    for half in range(2):
                        b = bank("ms", s, half)
                        done(nc.tensor.matmul(b[0:rows, 0:HALF], const("onesg" if s < 8 else "onesh", rows),
                                              roots(s)[0:rows, half * HALF:(half + 1) * HALF],
                                              start=True, stop=True), "ms", s, half)

                for i, f in enumerate(SEQ):
                    q, k = (8 + f, 4 + f) if f < 4 else (8 + f, 10 + f)
                    steps, before = STEPS[i], HEADS[SEQ[i - 1]] if i else []
                    for step in steps[0:2] if i == 0 else []:
                        score_step(step)
                    if before:
                        wait_emptied(pe, "o", SEQ[i - 1], 1)
                    for s in before:
                        means(s)
                    if f >= 4:
                        if f == 4:
                            pe.wait_ge(sems["z_ready"], 1)
                        for h in range(2):
                            b = bank("rsc", f, h)
                            r = slice(h * 64, h * 64 + 64)
                            for n in range(4):
                                c = slice(n * 128, (n + 1) * 128)
                                last = nc.tensor.matmul(b[:, c], Z[r, k, c], Z[r, q, c], start=True, stop=True)
                            done(last, "rsc", f, h)
                    for step in steps[2:3]:
                        score_step(step)
                    pe.wait_ge(sems["kq_ready"], i + 1)
                    b = bank("kt", f)
                    for n in range(4):
                        last = nc.tensor.transpose(b[:, n * 128:(n + 1) * 128], Z[:, k, n * 128:(n + 1) * 128],
                                                   ident)
                    done(last, "kt", f)
                    b = bank("kts", f)
                    done(nc.tensor.transpose(b[0:NS, 0:128], Z[:, k, NP:T], ident), "kts", f)
                    if f < 4:
                        for n in range(4):
                            pe.wait_ge(sems["km_ready"], KM_COUNT[f] + n + 1)
                            for half in range(2):
                                b = bank("dl", f, n, half)[:, 0:384].rearrange("p (c v) -> p c v", c=4)
                                for c in range(4):
                                    for h in range(2):
                                        last = nc.tensor.matmul(
                                            b[h * 64:h * 64 + 64, c, 0:DV[f]],
                                            KM[:, n % 2, 4 * half + c, h * 64:h * 64 + 64],
                                            V[:, n, vcols(f, h)], start=True, stop=True)
                                done(last, "dl", f, n, half)
                    else:
                        pe.wait_ge(sems["km_ready"], KM_COUNT[f] + 1)
                        b = bank("rdl", f)[:, 0:384].rearrange("p (c v) -> p c v", c=4)
                        for n in range(4):
                            for h in range(2):
                                last = nc.tensor.matmul(b[h * 64:h * 64 + 64, n, :],
                                                        KM[:, 0, n, h * 64:h * 64 + 64],
                                                        V[:, n, vcols(f, h)], start=True, stop=True)
                        done(last, "rdl", f)
                    pe.wait_ge(sems["kms_ready"], i + 1)
                    for half in range(2):
                        b = bank("dls", f, half)[:, 0:384].rearrange("p (c v) -> p c v", c=4)
                        for c in range(4):
                            for h in range(2):
                                last = nc.tensor.matmul(b[h * 64:h * 64 + 64, c, 0:DV[f]],
                                                        KMS[0:NS, 4 * half + c, h * 64:h * 64 + 64],
                                                        V[0:NS, 4, vcols(f, h)], start=True, stop=True)
                        done(last, "dls", f, half)
                    for step in steps[3:4]:
                        score_step(step)
                    pe.wait_ge(sems["dls_done"], i + 1)
                    for h in range(2):
                        _, r0, rows = oplace(f, h)
                        r = slice(h * 64, h * 64 + 64)
                        b = bank("os", f, h)
                        for t in range(NS):
                            last = nc.tensor.matmul(b[r0:r0 + rows, t:t + 1], SS[r, t, 0:rows],
                                                    Z[r, q, NP + t:NP + t + 1], start=True, stop=True)
                        done(last, "os", f, h)
                    for s in before:
                        mean_squares(s)
                    if 1 <= i < 5:
                        turn_scores(STEPS[i][-1] // 4)
                    for s in before + (HEADS[f] if i == 5 else []):
                        output_gate(s)
                    pe.wait_ge(sems["sct_ready"], i + 1)
                    if f < 4:
                        pe.wait_ge(sems["s_ready"], f + 1)
                    else:
                        pe.wait_ge(sems["rs_ready"], f - 3)
                    for h in range(2):
                        _, r0, rows = oplace(f, h)
                        r = slice(h * 64, h * 64 + 64)
                        b = bank("o", f, h)
                        step = CH if f < 4 else 128
                        for n in range(4):
                            chunks = [c for c in range(128 // step) if n or c]
                            last = nc.tensor.matmul(b[r0:r0 + rows, n * 128:(n + 1) * 128], V[:, n, vcols(f, h)],
                                                    SCT[:, h, n, :], start=True, stop=not chunks)
                            for c in chunks:
                                g = n * (128 // step) + c
                                state = S[r, g - 1, 0:rows] if f < 4 else SR[r, g - 1, 0:rows]
                                cols = slice(g * step, (g + 1) * step)
                                last = nc.tensor.matmul(b[r0:r0 + rows, cols], state, Z[r, q, cols],
                                                        start=False, stop=(c == chunks[-1]))
                        done(last, "o", f, h)
                        for step in STEPS[i + 1][h:h + 1] if i < 5 else []:
                            score_step(step)
                wait_emptied(pe, "o", SEQ[-1], 1)
                for s in HEADS[SEQ[-1]]:
                    mean_squares(s)
                def mix(n, half, slots):
                    for s in slots:
                        rows = 96 if s < 8 else 128
                        last = nc.tensor.matmul(BANKS["D"][JOB["mix", n, half][1] % 3][0:WID[n], :],
                                                OT[0:rows, s, n * 128:n * 128 + WID[n]],
                                                WO[0:rows, s, half * 512:(half + 1) * 512],
                                                start=(s == EARLY[0]), stop=(s == LATE[-1]))
                    return last

                pe.wait_ge(sems["on_ready"], 9)
                pe.wait_ge(sems["wout_loaded"], 16)
                tiles = [(n, half) for n in range(5) for half in range(2)]
                for n, half in tiles[0:3]:
                    bank("mix", n, half)
                    mix(n, half, EARLY)
                pe.wait_ge(sems["on_ready"], 10)
                pe.wait_ge(sems["wout_loaded"], 48)
                for n, half in tiles:
                    if (n, half) not in tiles[0:3]:
                        bank("mix", n, half)
                        mix(n, half, EARLY)
                    done(mix(n, half, LATE), "mix", n, half)
                to_features(1)
                for c in range(4):
                    for m in range(4 * c, 4 * c + 4):
                        project(I_Q[m // 2], m % 2, XT, "q", m)
                        if m % 2:
                            wait_full(pe, "q", m, 1)
                            pe.sem_inc(sems["w_consumed"], 1)
                    wait_emptied(pe, "q", 4 * c + 3, 1)
                    sub = weights(I_SUB[c])[:, 0:512].rearrange("p (s n) -> p s n", s=4)
                    for n in range(5):
                        b = bank("s", n, c)
                        for j in range(4):
                            last = nc.tensor.matmul(b[0:WID[n], j * 128:(j + 1) * 128],
                                                    QT[:, (4 * c + j) % 8, n * 128:n * 128 + WID[n]],
                                                    sub[:, j, :], start=True, stop=True)
                        done(last, "s", n, c)
                    wait_full(pe, "s", 4, c)
                    pe.sem_inc(sems["w_consumed"], 1)
                pw = weights(I_PP).rearrange("p (k n) -> p k n", k=2)
                pt = weights(I_PT)[:, 0:2 * T].rearrange("p (k n) -> p k n", k=2)
                for n in range(5):
                    for half in range(2):
                        b = bank("pp", n, half)
                        for k in range(2):
                            last = nc.tensor.matmul(b[0:WID[n], :], pt[:, k, n * 128:n * 128 + WID[n]],
                                                    pw[:, k, half * 512:(half + 1) * 512],
                                                    start=(k == 0), stop=(k == 1))
                        done(last, "pp", n, half)
                wait_full(pe, "pp", 4, 1)
                pe.sem_inc(sems["w_consumed"], 2)

                def embedding_gate(n, quarters=range(4)):
                    w = WID[n]
                    pe.wait_ge(sems["x2_ready"], TAIL.index(n) + 1)
                    for kg in range(2) if 0 in quarters else []:
                        b = bank("x2t", n, kg)
                        for k in range(4):
                            last = nc.tensor.transpose(b[:, k * w:(k + 1) * w],
                                                       X[0:w, n, (4 * kg + k) * 128:(4 * kg + k + 1) * 128],
                                                       ident[0:w, 0:w])
                        done(last, "x2t", n, kg)
                    wait_emptied(pe, "x2t", n, 1)
                    for c in quarters:
                        wg = weights(I_PG + c).rearrange("p (k n) -> p k n", k=KT)
                        b = bank("pg", n, c)
                        for k in range(KT):
                            last = nc.tensor.matmul(b[0:w, 0:256], X2T[:, k, 0:w], wg[:, k, :],
                                                    start=(k == 0), stop=(k == KT - 1))
                        done(last, "pg", n, c)

                for n in range(4):
                    def output_rows(g, start=False, stop=False):
                        rows = PE_ROWS[n]
                        for i, k in enumerate(rows):
                            pe.wait_ge(sems["diag_ready"], g * len(rows) + (n * NGRP * PEG + i + 1))
                            pe.wait_ge(fetched[k], L * (16 * USES) + g * 16 + 16 * (fetches_before(n, 1) + 1))
                            for half in range(2):
                                c = slice(half * 512, (half + 1) * 512)
                                last = nc.tensor.matmul(Y[:, c], DIAG[:, k, :], G[:, k, c],
                                                        start=start and i == 0,
                                                        stop=stop and i == len(rows) - 1)
                            last.then_inc(sems["v_used"], 1)
                        return last

                    if n == 2:
                        pe.wait_ge(sems["et_ready"], 1)
                        b = bank("et")
                        done(nc.tensor.transpose(b[:, 0:NS], EFS[0:NS], ident[0:NS, 0:NS]), "et")
                        pe.wait_ge(sems["et_ready"], 2)
                        b = bank("gt")
                        done(nc.tensor.transpose(b[:, 0:NS], GATE[0:NS, 4, :], ident[0:NS, 0:NS]), "gt")
                    if n == 3:
                        for t in range(NS):
                            for half in range(2):
                                b = bank("xb", t, half)
                                done(nc.tensor.matmul(b[:, :], ident[0:NS, t:t + 1].to_broadcast([NS, 128]),
                                                      X[0:NS, 4, half * 512:(half + 1) * 512],
                                                      start=True, stop=True), "xb", t, half)
                    if n:
                        embedding_gate(n - 1)
                    if n == 3:
                        pe.wait_ge(sems["wsam_ready"], 1)
                        banks = [bank("sacc", half) for half in range(2)]
                        for half in range(2):
                            nc.tensor.matmul(banks[half][0:NS, :], const("aident", NS)[:, 0:NS],
                                             X[0:NS, 4, half * 512:(half + 1) * 512], start=True, stop=False)
                        for t in range(NS):
                            pe.wait_ge(fetched[t], L * (16 * USES) + 16 * fetches_before(3, 1))
                            for half in range(2):
                                last = nc.tensor.matmul(banks[half][0:NS, :], WS8[:, t, :],
                                                        G[:, t, half * 512:(half + 1) * 512], start=False,
                                                        stop=(t == NS - 1))
                            last.then_inc(sems["sample_v_used"], 1)
                        pe.wait_ge(sems["sample_v_used"], NS)
                        pe.sem_inc(full["D"], 2)
                    if n:
                        pe.wait_ge(sems["y_read"], n)
                    output_rows(0, start=True)
                    at = 1
                    if n == 3:
                        for c, until in enumerate(BREAKS):
                            with pe.Fori(at, until) as g:
                                output_rows(g)
                            embedding_gate(4, [c])
                            at = until
                    with pe.Fori(at, NGRP - 1) as g:
                        output_rows(g)
                    output_rows(NGRP - 1, stop=True)
                    pe.wait_ge(sems["v_used"], PEG + n * NGRP * PEG + NGRP * len(PE_ROWS[n]))
                    pe.sem_inc(sems["acc_ready"], 1)

                embedding_gate(3)
                arrive(pe, L)

        @block.gpsimd
        def _(pool):
            def fetch(L, n, phase, table):
                sample = NS if n == 3 else 0
                with pool.Fori(0, NGRP // 2) as gg:
                    if phase == 0:
                        pool.wait_ge(sems["idx_ready"], gg + (n * PH + 1))
                        pool.sem_inc(sems["idx_known"], 1)
                    for par in range(2):
                        nc.gpsimd.tensor_copy(IST[:, par, :], IDX[:, n, ds(gg * (2 * RING) + par * RING, RING)]) \
                            .then_inc(sems["idx_staged"], 1)
                        pool.wait_ge(sems["idx_staged"],
                                     gg * 2 + ((n * 2 + phase) * NGRP + par + 1))
                        for half in range(2):
                            upto = half + 1
                            if phase == 0:
                                pool.wait_ge(sems["u_used"], gg * (2 * RING)
                                             + (n * SLOTS + sample + par * RING + upto * RING // 2))
                                pool.wait_ge(sems["v_used"], n * NGRP * PEG + upto * PEG // 2)
                                pool.wait_ge(sems["vd_used"], n * NGRP * DVG + upto * DVG // 2)
                            else:
                                for name, rows in (("v_used", PE_ROWS), ("vd_used", DVE_ROWS)):
                                    first, per = rows_used(rows, n, upto)
                                    pool.wait_ge(sems[name], gg * (2 * per) + (par * per + first))
                                pool.wait_ge(sems["u_used"], (n + 1) * SLOTS + sample + upto * RING // 2)
                                if n == 3:
                                    pool.wait_ge(sems["sample_v_used"], upto * NS // 2)
                            pool.sem_inc(sems["places_free"], 1)
                            for k in range(half * RING // 2, (half + 1) * RING // 2):
                                pool.indirect_dma_start(
                                    G[:, k, :], None, table,
                                    bass.IndirectOffsetOnAxis(ap=IST[:, par, k:k + 1], axis=0)) \
                                    .then_inc(fetched[k], 16)

            pool.wait_ge(sems["consts_loaded"], 64)
            with pool.Fori(0, DEPTH) as L:
                pool.sem_inc(sems["u_used"], RING)
                pool.sem_inc(sems["v_used"], PEG)
                pool.sem_inc(sems["vd_used"], DVG)
                def differences(step):
                    f, iq = quarter(step)
                    w = 4 * iq + 4
                    if step >= 2:
                        pool.wait_ge(sems["p_used"], step - 1)
                    b = Z[:, f, 0:NP].rearrange("p (c i) -> p c i", i=CH)
                    for i in range(4):
                        at = 4 * iq + i
                        last = nc.gpsimd.tensor_tensor(P[:, step % 2, i, :, 0:w],
                                                       b[:, :, at:at + 1].to_broadcast([128, NC, w]),
                                                       b[:, :, 0:w], ALU.subtract)
                    last.then_inc(sems["diff_ready"], 1)

                def squares(s):
                    rows, t = 96 if s < 8 else 128, ORDER.index(s)
                    if t and roots(s) is RS:
                        pool.wait_ge(sems["on_scaled"], t)
                    if 4 <= s < 8:
                        pool.wait_ge(sems["mu_done"], s - 3)
                    nc.gpsimd.tensor_tensor(roots(s)[0:rows, :], OT[0:rows, s, :], OT[0:rows, s, :], ALU.mult) \
                        .then_inc(sems["sq_ready"], 1)

                pool.wait_ge(sems["b_ready"], 1)
                differences(0)
                differences(1)
                def gated(s):
                    rows = 96 if s < 8 else 128
                    pool.wait_ge(sems["on_scaled"], ORDER.index(s) + 1)
                    wait_emptied(pool, "g", s, 1)
                    nc.gpsimd.tensor_tensor(OT[0:rows, s, :], OT[0:rows, s, :], Z[0:rows, ZGATE[s], :], ALU.mult) \
                        .then_inc(sems["on_ready"], 1)

                for i in range(6):
                    for step in STEPS[i][0:3]:
                        if step + 2 < 16:
                            differences(step + 2)
                    if i:
                        wait_emptied(pool, "o", SEQ[i - 1], 1)
                        for s in HEADS[SEQ[i - 1]]:
                            squares(s)
                    for step in STEPS[i][3:4]:
                        if step + 2 < 16:
                            differences(step + 2)
                    if i:
                        for s in HEADS[SEQ[i - 1]]:
                            gated(s)
                wait_emptied(pool, "o", SEQ[-1], 1)
                for s in HEADS[SEQ[-1]]:
                    squares(s)
                for s in HEADS[SEQ[-1]]:
                    gated(s)
                def fetch_sample(table):
                    for t in range(NS):
                        pool.indirect_dma_start(G[:, t, :], None, table,
                                                bass.IndirectOffsetOnAxis(ap=IDXS[:, t:t + 1], axis=0)) \
                            .then_inc(fetched[t], 16)

                for n in range(4):
                    if n == 3:
                        pool.wait_ge(sems["sample_idx"], 1)
                        pool.wait_ge(sems["v_used"], (3 * NGRP + 1) * PEG)
                        pool.wait_ge(sems["vd_used"], (3 * NGRP + 1) * DVG)
                        fetch_sample(utab)
                    fetch(L, n, 0, utab)
                    if n == 3:
                        pool.wait_ge(sems["u_used"], RING + 4 * SLOTS + NS)
                        fetch_sample(vtab)
                    fetch(L, n, 1, vtab)
                arrive(pool, L)

        @block.scalar
        def _(act):
            def emptied(ins, *name):
                ins.then_inc(free[JOB[name][0]], 1)

            def to_features(stage):
                for n in range(5):
                    w = WID[n]
                    b = wait_full(act, "xt", stage, n, 0)
                    emptied(nc.scalar.activation(XT[:, 0:4, n * 128:n * 128 + w],
                                                 b[:, 0:4 * w].rearrange("p (k t) -> p k t", k=4), ACT.Copy),
                            "xt", stage, n, 0)

            def rstd(n, count):
                w = WID[n]
                act.wait_ge(sems["mv_ready"], count)
                nc.scalar.activation(ST[0:w, n, 14:15], ST[0:w, n, 13:14], ACT.Ln, bias=const("eps", w))
                act.drain()
                nc.scalar.activation(ST[0:w, n, 15:16], ST[0:w, n, 14:15], ACT.Exp, scale=-0.5) \
                    .then_inc(sems["rstd_ready"], 1)

            def value(i, n):
                b = wait_full(act, "v", i, n)
                emptied(nc.scalar.activation(V[0:WID[n], n, i * 256:(i + 1) * 256], b[0:WID[n], 0:256],
                                             ACT.Copy), "v", i, n)

            act.wait_ge(sems["consts_loaded"], 64)
            act.wait_ge(sems["small_init"], 1)
            nc.scalar.activation(LB[:, 0:4], LB[:, 0:4], ACT.Exp).then_inc(sems["small_init"], 1)
            with act.Fori(0, DEPTH) as L:
                to_features(0)
                act.wait_ge(sems["lb_ready"], 1)
                nc.scalar.activation(LB[:, 10:14], LB[:, 6:10], ACT.Ln).then_inc(sems["lb_ready"], 1)
                for m, name in enumerate(FEATURES):
                    b = wait_full(act, "z", m, 0)
                    if name == "glr":
                        emptied(nc.scalar.activation(T1[0:16, 0, 0:HALF], b[0:16, 0:HALF], ACT.Copy), "z", m, 0)
                    else:
                        emptied(nc.scalar.activation(Z[:, ZSLOT[name], 0:HALF], b[:, 0:HALF], ACT.Copy,
                                                     scale=48 ** -0.5 if name[:2] == "gq" else 1.0), "z", m, 0)
                wait_emptied(act, "z", len(FEATURES) - 1, 1)
                act.drain()
                nc.scalar.activation(Z[:, 6:8, :], Z[:, 2:4, :], ACT.Sigmoid, scale=-1.0)
                nc.scalar.activation(Z[:, 10:12, :], Z[:, 10:12, :], ACT.Silu).then_inc(sems["sigm_ready"], 1)
                for n in range(5):
                    value(0, n)
                act.wait_ge(sems["abs_ready"], 1)
                nc.scalar.activation(T1, T1, ACT.Exp, scale=-1.0)
                act.drain()
                nc.scalar.activation(T2, T1, ACT.Ln, bias=1.0).then_inc(sems["log1p_ready"], 1)
                for n in range(5):
                    value(1, n)
                act.wait_ge(sems["hdiff_ready"], 1)
                nc.scalar.activation(T1[:, 0:2, :], T1[:, 0:2, :], ACT.Exp, scale=-1.0)
                act.drain()
                nc.scalar.activation(T2[:, 0:2, :], T1[:, 0:2, :], ACT.Ln, bias=1.0) \
                    .then_inc(sems["hlog_ready"], 1)
                for n in range(5):
                    value(2, n)
                act.wait_ge(sems["b_ready"], 1)
                nc.scalar.activation(DEC[:, :, 1:NC],
                                     Z[:, 0:4, 0:NP].rearrange("p f (c i) -> p f c i", i=CH)[:, :, 1:NC, CH - 1],
                                     ACT.Exp)
                nc.scalar.activation(DEC[:, :, NC:NC + NS], Z[:, 0:4, NP:T], ACT.Exp) \
                    .then_inc(sems["dec_ready"], 1)
                for n in range(5):
                    value(3, n)

                def pexp(step):
                    w = 4 * quarter(step)[1] + 4
                    act.wait_ge(sems["min_ready"], step + 1)
                    p = P[:, step % 2, :, :, 0:w]
                    nc.scalar.activation(p, p, ACT.Exp).then_inc(sems["pexp_ready"], 1)

                def output_gate(s):
                    rows = 96 if s < 8 else 128
                    for half in range(2):
                        b = wait_full(act, "g", s, half)
                        emptied(nc.scalar.activation(Z[0:rows, ZGATE[s], half * HALF:(half + 1) * HALF],
                                                     b[0:rows, 0:HALF], ACT.Silu), "g", s, half)

                def head_norms(heads):
                    for s in heads:
                        rows, r = 96 if s < 8 else 128, roots(s)
                        for half in range(2):
                            b = wait_full(act, "ms", s, half)
                            emptied(nc.scalar.activation(r[0:rows, half * HALF:(half + 1) * HALF],
                                                         b[0:rows, 0:HALF], ACT.Ln, bias=const("eps", rows)),
                                    "ms", s, half)
                    act.drain()
                    for s in heads:
                        rows, r = 96 if s < 8 else 128, roots(s)
                        nc.scalar.activation(r[0:rows, :], r[0:rows, :], ACT.Exp, scale=-0.5) \
                            .then_inc(sems["rms_ready"], 1)

                def output(kind, f, following=()):
                    c0, c1 = (NP, T) if kind == "os" else (0, NP)
                    for h in range(2):
                        at, r0, rows = oplace(f, h)
                        b = wait_full(act, kind, f, h)
                        emptied(nc.scalar.activation(OT[r0:r0 + rows, at, c0:c1],
                                                     b[r0:r0 + rows, 0:c1 - c0], ACT.Copy), kind, f, h)
                        for step in following[h:h + 1]:
                            if step < 15:
                                pexp(step + 1)

                pexp(0)
                for i, f in enumerate(SEQ):
                    steps, before = STEPS[i], HEADS[SEQ[i - 1]] if i else []
                    ahead = [[step + 1] if step < 15 else [] for step in steps]
                    for step in sum(ahead[0:2], []) if i == 0 else []:
                        pexp(step)
                    if f < 4:
                        act.wait_ge(sems["ek_ready"], f + 1)
                        nc.scalar.activation(SCT, SCT, ACT.Exp).then_inc(sems["eq_ready"], 1)
                    for step in sum(ahead[2:3], []):
                        pexp(step)
                    if i:
                        act.wait_ge(s_stored, 16 * i)
                    if f < 4:
                        for n in range(4):
                            for half in range(2):
                                b = wait_full(act, "dl", f, n, half)
                                emptied(nc.scalar.activation(
                                    S[:, n * CT + 4 * half:n * CT + 4 * half + 4, 0:DV[f]],
                                    b[:, 0:384].rearrange("p (c v) -> p c v", c=4)[:, :, 0:DV[f]],
                                    ACT.Copy), "dl", f, n, half)
                    else:
                        b = wait_full(act, "rdl", f)
                        emptied(nc.scalar.activation(SR, b[:, 0:384].rearrange("p (c v) -> p c v", c=4),
                                                     ACT.Copy), "rdl", f)
                    for step in sum(ahead[3:4], []):
                        pexp(step)
                    if 1 <= i < 5:
                        act.wait_ge(sems["p_used"], STEPS[i][-1] + 1)
                        if STEPS[i][-1] // 4:
                            act.wait_ge(sems["sc_turned"], STEPS[i][-1] // 4)
                        nc.scalar.activation(SCCOPY, Y[SCROWS, 0:512], ACT.Copy).then_inc(sems["sc_copied"], 1)
                    if f == 2:
                        act.wait_ge(sems["on_scaled"], 4)
                    output("os", f)
                    head_norms(before)
                    for s in before + (HEADS[f] if i == 5 else []):
                        output_gate(s)
                    output("o", f, STEPS[i + 1] if i < 5 else ())
                head_norms(HEADS[SEQ[-1]])
                for n in range(5):
                    rstd(n, n + 1)
                to_features(1)
                for c in range(4):
                    for m in range(4 * c, 4 * c + 4):
                        for half in range(2):
                            b = wait_full(act, "q", m, half)
                            emptied(nc.scalar.activation(QT[:, m % 8, half * HALF:(half + 1) * HALF],
                                                         b[:, 0:HALF], ACT.Copy), "q", m, half)
                    for n in range(5):
                        b = wait_full(act, "s", n, c)
                        emptied(nc.scalar.activation(SC[n][0:WID[n], c * 512:(c + 1) * 512], b[0:WID[n], :],
                                                     ACT.Copy), "s", n, c)
                for n in range(5):
                    for half in range(2):
                        b = wait_full(act, "pp", n, half)
                        emptied(nc.scalar.activation(PP[n][0:WID[n], half * 512:(half + 1) * 512],
                                                     b[0:WID[n], :], ACT.Copy), "pp", n, half)

                def gates(n):
                    act.wait_ge(sems["rprod_ready"], TAIL.index(n) + 1)
                    g = GATE[0:WID[n], n, :]
                    nc.scalar.activation(g, g, ACT.Exp).then_inc(sems["silu_ready"], 1)

                def embedding_gate(n, quarters=range(4)):
                    w = WID[n]
                    for kg in range(2) if 0 in quarters else []:
                        b = wait_full(act, "x2t", n, kg)
                        emptied(nc.scalar.activation(X2T[:, 4 * kg:4 * kg + 4, 0:w],
                                                     b[:, 0:4 * w].rearrange("p (k t) -> p k t", k=4), ACT.Copy),
                                "x2t", n, kg)
                    if n:
                        act.wait_ge(sems["x_ready"], TAIL.index(n))
                    for c in quarters:
                        b = wait_full(act, "pg", n, c)
                        emptied(nc.scalar.activation(SG[0:w, c * 256:(c + 1) * 256], b[0:w, 0:256],
                                                     ACT.Sigmoid), "pg", n, c)

                gates(0)
                for n in range(4):
                    if n == 3:
                        act.wait_ge(sems["sample_score"], 1)
                        nc.scalar.activation(WS, SSC, ACT.Gelu).then_inc(sems["sample_gelu"], 1)
                    if n:
                        rstd(n - 1, n + 5)
                        embedding_gate(n - 1)
                    act.wait_ge(sems["score_ready"], n + 1)
                    nc.scalar.activation(WGT, SCORE, ACT.Gelu).then_inc(sems["gelu_ready"], 1)
                    act.wait_ge(sems["w_ready"], n + 1)
                    if n == 3:
                        rstd(4, 9)

                    def diagonals(g):
                        per = len(PE_ROWS[n])
                        for i, k in enumerate(PE_ROWS[n]):
                            if i % (per // 2) == 0:
                                act.wait_ge(sems["v_used"],
                                            g * per + rows_used(PE_ROWS, n, 1 + i // (per // 2))[0])
                            nc.scalar.activation(DIAG[:, k, :], ident, ACT.Copy,
                                                 scale=WGT[:, ds(g * RING + k, 1)]) \
                                .then_inc(sems["diag_ready"], 1)

                    at = 0
                    if n == 3:
                        for c, until in enumerate(BREAKS):
                            with act.Fori(at, until) as g:
                                diagonals(g)
                            embedding_gate(4, [c])
                            at = until
                    with act.Fori(at, NGRP) as g:
                        diagonals(g)
                    if n < 3:
                        gates(n + 1)
                    if n == 1:
                        gates(4)
                rstd(3, 10)
                embedding_gate(3)
                arrive(act, L)

        @block.vector
        def _(dve):
            def emptied(ins, *name):
                ins.then_inc(free[JOB[name][0]], 1)

            def to_features(stage):
                for n in range(5):
                    w = WID[n]
                    b = wait_full(dve, "xt", stage, n, 1)
                    emptied(nc.vector.tensor_copy(XT[:, 4:8, n * 128:n * 128 + w],
                                                  b[:, 0:4 * w].rearrange("p (k t) -> p k t", k=4)),
                            "xt", stage, n, 1)

            def statistics(n, src):
                w = WID[n]
                for j in range(2):
                    nc.vector.bn_stats(ST[0:w, n, 6 * j:6 * j + 6], src[0:w, j * 512:(j + 1) * 512])
                dve.drain()
                nc.vector.bn_aggr(ST[0:w, n, 12:14], ST[0:w, n, 0:12].rearrange("p (a b) -> p a b", a=2)) \
                    .then_inc(sems["mv_ready"], 1)

            def normalize(n, src, which, count, signal):
                w = WID[n]
                dve.wait_ge(sems["rstd_ready"], count)
                x = X[0:w, n, :]
                nc.vector.tensor_scalar(x, src[0:w, :], ST[0:w, n, 12:13], ST[0:w, n, 15:16],
                                        ALU.subtract, ALU.mult)
                dve.drain()
                nc.vector.tensor_tensor(x, x, LNP[0:w, 2 * which, :], ALU.mult)
                dve.drain()
                return nc.vector.tensor_tensor(x, x, LNP[0:w, 2 * which + 1, :], ALU.add) \
                    .then_inc(sems[signal], 1)

            def best8(src, vals, inds, strike):
                dve.drain()
                for s, v in zip(src, vals):
                    nc.vector.max(v, s)
                dve.drain()
                for s, v, i in zip(src, vals, inds):
                    nc.vector.max_index(i, v, s)
                if strike:
                    dve.drain()
                    for s, v in zip(src, vals):
                        nc.vector.match_replace(s, v, s, -3.0e38)

            def top(n, h, part):
                w = WID[n]
                if part == 0:
                    nc.vector.tensor_copy(STG[0:w].rearrange("p s n -> p (s n)"),
                                          SC[n][0:w, ds(h * (2 * NKEY), 2 * NKEY)])
                if part < 2:
                    c = slice(part * 8, part * 8 + 8)
                    best8([STG[0:w, s, :] for s in range(2)], [VV[0:w, s, c] for s in range(2)],
                          [II[0:w, s, c] for s in range(2)], part == 0)
                if part == 2:
                    dve.drain()
                    nc.vector.tensor_copy(IF[0:w], II[0:w])
                    nc.vector.tensor_tensor(CAND[0:w], VV[0:w, 0, :].unsqueeze(2).to_broadcast([w, 16, 16]),
                                            VV[0:w, 1, :].unsqueeze(1).to_broadcast([w, 16, 16]), ALU.add)
                    cand = CAND[0:w].rearrange("p a b -> p (a b)")
                    for c in (slice(0, 8), slice(8, 16)):
                        best8([cand], [BEST[0:w, c]], [CI[0:w, c]], c.start == 0)
                if part == 3:
                    dve.drain()
                    nc.vector.tensor_scalar(GATE[0:w, n, ds(h * TOPK, TOPK)], BEST[0:w], BEST[0:w, 0:1], None,
                                            ALU.subtract)
                    nc.vector.tensor_single_scalar(CAB[0:w, 0], CI[0:w], 4, ALU.logical_shift_right)
                    nc.vector.tensor_single_scalar(CAB[0:w, 1], CI[0:w], 15, ALU.bitwise_and)
                    dve.drain()
                    nc.vector.tensor_copy(ABF[0:w], CAB[0:w])
                    dve.drain()
                    for s in range(2):
                        nc.vector.tensor_tensor(EQT[0:w, s], ABF[0:w, s].unsqueeze(2).to_broadcast([w, 16, 16]),
                                                iota16[0:w, :].unsqueeze(1).to_broadcast([w, 16, 16]),
                                                ALU.is_equal)
                    dve.drain()
                    for s in range(2):
                        nc.vector.tensor_tensor(EQT[0:w, s], EQT[0:w, s],
                                                IF[0:w, s, :].unsqueeze(1).to_broadcast([w, 16, 16]), ALU.mult)
                    dve.drain()
                    nc.vector.tensor_reduce(SEL[0:w], EQT[0:w], AX.X, ALU.add)
                    dve.drain()
                    nc.vector.scalar_tensor_tensor(out=EF[0:w], in0=SEL[0:w, 0], scalar=float(NKEY),
                                                   in1=SEL[0:w, 1], op0=ALU.mult, op1=ALU.add)
                    dve.drain()
                    out = IDX[:, n, ds(h * TOPK, TOPK)] if n < 4 else EFS[0:w, ds(h * TOPK, TOPK)]
                    last = nc.vector.tensor_scalar(out, EF[0:w], LBASE[0:w, 0:1], None, ALU.add)
                    if n < 4:
                        last.then_inc(sems["idx_ready"], 1)

            def softmax_sums(n):
                w = WID[n]
                gate = GATE[0:w, n, :].rearrange("p (h k) -> p h k", k=TOPK)
                dve.wait_ge(sems["silu_ready"], TAIL.index(n) + 1)
                nc.vector.tensor_reduce(SUM[0:w, 0], gate, AX.X, ALU.add)
                dve.drain()
                nc.vector.reciprocal(SUM[0:w, 1], SUM[0:w, 0])
                dve.drain()
                return nc.vector.tensor_tensor(gate, gate, SUM[0:w, 1].unsqueeze(2).to_broadcast([w, PH, TOPK]),
                                               ALU.mult)

            def dots(L, n, h, j0, j1):
                for j in range(j0, j1):
                    k = j % RING
                    dve.wait_ge(fetched[k], L * (16 * USES) + h * (16 * GPH)
                                + 16 * (fetches_before(n, 0) + j // RING + 1))
                    nc.vector.scalar_tensor_tensor(
                        out=G[:, k, :], in0=G[:, k, :], scalar=1.0, in1=X[:, n, :], op0=ALU.mult,
                        op1=ALU.mult, accum_out=SCORE[:, ds(h * TOPK + j, 1)]) \
                        .then_inc(sems["u_used"], 1)

            def add_embedding(n):
                w = WID[n]
                wait_emptied(dve, "pg", n, 3)
                nc.vector.tensor_tensor(SG[0:w], SG[0:w], PP[n][0:w], ALU.mult)
                dve.drain()
                nc.vector.tensor_tensor(X[0:w, n, :], X[0:w, n, :], SG[0:w], ALU.add).then_inc(sems["x_ready"], 1)

            iota16 = const("iota")
            dve.wait_ge(sems["consts_loaded"], 64)
            nc.vector.tensor_tensor(LB[:, 4:6], LB[:, 0:2], LB[:, 2:4], ALU.max)
            dve.drain()
            nc.vector.tensor_tensor(LB[:, 0:2], LB[:, 0:2], LB[:, 4:6], ALU.subtract)
            nc.vector.tensor_tensor(LB[:, 2:4], LB[:, 2:4], LB[:, 4:6], ALU.subtract).then_inc(sems["small_init"], 1)
            dve.wait_ge(sems["small_init"], 2)
            nc.vector.tensor_tensor(LB[:, 4:6], LB[:, 0:2], LB[:, 2:4], ALU.add)
            dve.drain()
            nc.vector.reciprocal(LB[:, 6:8], LB[:, 4:6])
            dve.drain()
            nc.vector.tensor_tensor(LB[:, 14:16], LB[:, 2:4], LB[:, 6:8], ALU.mult)
            nc.vector.memset(LB[:, 4:6], 0.0)
            nc.vector.memset(LBASE[:, :], 0.0)

            with dve.Fori(0, DEPTH) as L:
                dve.drain()
                nc.vector.tensor_scalar(LB[:, 6:8], LB[:, 4:6], 2.0 ** -63, None, ALU.max)
                nc.vector.tensor_scalar(LB[:, 8:10], LB[:, 4:6], -1.0, 1.0, ALU.mult, ALU.add)
                dve.drain()
                nc.vector.tensor_scalar(LB[:, 8:10], LB[:, 8:10], 2.0 ** -63, None, ALU.max)
                dve.drain().then_inc(sems["lb_ready"], 1)
                to_features(0)
                for m, name in enumerate(FEATURES):
                    b = wait_full(dve, "z", m, 1)
                    if name == "glr":
                        emptied(nc.vector.tensor_copy(T1[0:16, 0, HALF:T], b[0:16, 0:HALF]), "z", m, 1)
                    else:
                        emptied(nc.vector.tensor_scalar(Z[:, ZSLOT[name], HALF:T], b[:, 0:HALF],
                                                        48 ** -0.5 if name[:2] == "gq" else 1.0, None, ALU.mult),
                                "z", m, 1)
                    if name == "hq0":
                        for g in range(2):
                            for half in range(2):
                                b = wait_full(dve, "ga", g, half)
                                emptied(nc.vector.tensor_scalar(Z[:, g, half * HALF:(half + 1) * HALF],
                                                                b[:, 0:HALF], SM[:, g:g + 1], None, ALU.add),
                                        "ga", g, half)
                def rotate(s):
                    scale = 1.0 if s < 2 else 48 ** -0.5
                    for half in range(2):
                        c = slice(half * HALF, (half + 1) * HALF)
                        b = wait_full(dve, "rot", s, half)
                        emptied(nc.vector.scalar_tensor_tensor(out=ROT[:, half, :], in0=b[:, 0:HALF], scalar=scale,
                                                               in1=const("sin")[:, c], op0=ALU.mult,
                                                               op1=ALU.mult), "rot", s, half)
                    for half in range(2):
                        c = slice(half * HALF, (half + 1) * HALF)
                        nc.vector.scalar_tensor_tensor(out=Z[:, 12 + s, c], in0=Z[:, 12 + s, c], scalar=scale,
                                                       in1=const("cos")[:, c], op0=ALU.mult, op1=ALU.mult)
                    dve.drain()
                    for half in range(2):
                        c = slice(half * HALF, (half + 1) * HALF)
                        nc.vector.tensor_tensor(Z[:, 12 + s, c], Z[:, 12 + s, c], ROT[:, half, :], ALU.add)
                    dve.drain()

                dve.wait_ge(sems["sigm_ready"], 1)
                nc.vector.scalar_tensor_tensor(out=T1, in0=Z[:, 0:4, :], scalar=-1.0, in1=Z[:, 0:4, :],
                                               op0=ALU.mult, op1=ALU.max).then_inc(sems["abs_ready"], 1)
                for h in range(2):
                    nc.vector.tensor_scalar(Z[:, 6 + h, :], Z[:, 6 + h, :], LB[:, 8 + h:9 + h], None, ALU.mult)
                rotate(0)
                dve.wait_ge(sems["log1p_ready"], 1)
                nc.vector.scalar_tensor_tensor(out=Z[:, 0:4, :], in0=Z[:, 0:4, :], scalar=0.0, in1=T2,
                                               op0=ALU.min, op1=ALU.subtract)
                dve.wait_ge(sems["lb_ready"], 2)
                dve.drain()
                nc.vector.tensor_scalar(Z[:, 0:2, :], Z[:, 0:2, :], 1.0 / 16.0, None, ALU.mult)
                for h in range(2):
                    nc.vector.tensor_scalar(Z[:, 2 + h, :], Z[:, 2 + h, :], LB[:, 12 + h:13 + h], None, ALU.add)
                dve.drain()
                for h in range(2):
                    nc.vector.tensor_scalar(T1[:, h, :], Z[:, 2 + h, :], LB[:, 10 + h:11 + h], None, ALU.subtract)
                dve.drain()
                nc.vector.scalar_tensor_tensor(out=T1[:, 0:2, :], in0=T1[:, 0:2, :], scalar=-1.0,
                                               in1=T1[:, 0:2, :], op0=ALU.mult, op1=ALU.max).then_inc(sems["hdiff_ready"], 1)
                rotate(1)
                dve.wait_ge(sems["hlog_ready"], 1)
                for h in range(2):
                    nc.vector.scalar_tensor_tensor(out=Z[:, 2 + h, :], in0=Z[:, 2 + h, :],
                                                   scalar=LB[:, 10 + h:11 + h], in1=T2[:, h, :],
                                                   op0=ALU.max, op1=ALU.add)
                dve.drain()
                for f in range(4):
                    last = nc.vector.tensor_tensor_scan(Z[:, f, :], const("chunkmask"), Z[:, f, :], 0.0,
                                                        ALU.mult, ALU.add)
                last.then_inc(sems["b_ready"], 1)
                for s in ROTATED[2]:
                    rotate(s)
                dve.drain().then_inc(sems["z_ready"], 1)

                def low(step):
                    iq = quarter(step)[1]
                    w = 4 * iq + 4
                    dve.wait_ge(sems["diff_ready"], step + 1)
                    m = const("causal").rearrange("p (i j) -> p i j", j=CH)
                    for i in range(4):
                        p = P[:, step % 2, i, :, 0:w]
                        last = nc.vector.tensor_tensor(
                            p, p, m[:, 4 * iq + i:4 * iq + i + 1, 0:w].to_broadcast([128, NC, w]), ALU.min)
                    last.then_inc(sems["min_ready"], 1)

                def products(step):
                    f, iq = quarter(step)
                    w = 4 * iq + 4
                    dve.wait_ge(sems["pexp_ready"], step + 1)
                    kk = Z[:, 4 + f, 0:NP].rearrange("p (c j) -> p c j", j=CH)
                    qq = Z[:, 8 + f, 0:NP].rearrange("p (c i) -> p c i", i=CH)
                    for i in range(4):
                        p = P[:, step % 2, i, :, 0:w]
                        nc.vector.tensor_tensor(p, p, kk[:, :, 0:w], ALU.mult)
                    dve.drain()
                    for i in range(4):
                        p = P[:, step % 2, i, :, 0:w]
                        at = 4 * iq + i
                        last = nc.vector.tensor_tensor(p, p, qq[:, :, at:at + 1].to_broadcast([128, NC, w]),
                                                       ALU.mult)
                    last.then_inc(sems["p_ready"], 1)

                def keys(i, f):
                    mask = const("mask16")
                    b = wait_full(dve, "kt", f)
                    if f < 4:
                        for n in range(4):
                            if f == 0 and n == 0:
                                wait_full(dve, "rdl", 5)
                            if 4 * f + n >= 2:
                                g = 4 * f + n - 2
                                wait_full(dve, "dl", g // 4, g % 4, 1)
                            nc.vector.tensor_tensor(
                                KM[:, n % 2], b[:, n * 128:(n + 1) * 128].unsqueeze(1).to_broadcast([128, CT, 128]),
                                mask.unsqueeze(2).to_broadcast([128, CT, 128]), ALU.mult) \
                                .then_inc(sems["km_ready"], 1)
                        dve.wait_ge(sems["km_ready"], KM_COUNT[f] + 4)
                        dve.sem_inc(free["D"], 1)
                    else:
                        if f == 5:
                            wait_full(dve, "rdl", 4)
                        emptied(nc.vector.tensor_copy(KM[:, 0, 0:4, :], b[:, :].rearrange("p (n d) -> p n d", n=4)),
                                "kt", f)
                        wait_emptied(dve, "kt", f)
                        dve.sem_inc(sems["km_ready"], 1)
                    b = wait_full(dve, "kts", f)
                    if i:
                        wait_full(dve, "dls", SEQ[i - 1], 1)
                    emptied(nc.vector.tensor_tensor(
                        KMS[0:NS], b[0:NS, 0:128].unsqueeze(1).to_broadcast([NS, NS, 128]),
                        ident[0:NS, 0:NS].unsqueeze(2).to_broadcast([NS, NS, 128]), ALU.mult), "kts", f)
                    wait_emptied(dve, "kts", f)
                    dve.sem_inc(sems["kms_ready"], 1)

                def sample_states(i, f):
                    dve.wait_ge(ss_loaded, 16 * (i + 1))
                    if f < 4:
                        nc.vector.tensor_tensor(SS[:, :, 0:DV[f]], SS[:, :, 0:DV[f]],
                                                DEC[:, f, NC:NC + NS].unsqueeze(2).to_broadcast([128, NS, DV[f]]),
                                                ALU.mult)
                    else:
                        nc.vector.tensor_scalar(SS[:, :, :], SS[:, :, :], const("gam")[:, f - 4:f - 3], None,
                                                ALU.mult)
                    dve.drain()
                    for half in range(2):
                        b = wait_full(dve, "dls", f, half)
                        ss = SS[:, 4 * half:4 * half + 4, 0:DV[f]]
                        emptied(nc.vector.tensor_tensor(
                            ss, ss, b[:, 0:384].rearrange("p (c v) -> p c v", c=4)[:, :, 0:DV[f]], ALU.add),
                            "dls", f, half)
                    wait_emptied(dve, "dls", f, 1)
                    dve.sem_inc(sems["dls_done"], 1)

                def states(f):
                    if f < 4:
                        wait_emptied(dve, "dl", f, 3, 1)
                        for c in range(1, NC):
                            last = nc.vector.scalar_tensor_tensor(
                                out=S[:, c, 0:DV[f]], in0=S[:, c - 1, 0:DV[f]], scalar=DEC[:, f, c:c + 1],
                                in1=S[:, c, 0:DV[f]], op0=ALU.mult, op1=ALU.add)
                            if c < NC - 1:
                                dve.drain()
                        last.then_inc(sems["s_ready"], 1)
                    else:
                        wait_emptied(dve, "rdl", f)
                        for n in range(1, 4):
                            last = nc.vector.scalar_tensor_tensor(
                                out=SR[:, n, :], in0=SR[:, n - 1, :], scalar=const("g128")[:, f - 4:f - 3],
                                in1=SR[:, n, :], op0=ALU.mult, op1=ALU.add)
                            if n < 3:
                                dve.drain()
                        last.then_inc(sems["rs_ready"], 1)

                def subtract_mean(s):
                    for half in range(2):
                        b = wait_full(dve, "mu", s, half)
                        o = OT[0:96, s, half * HALF:(half + 1) * HALF]
                        emptied(nc.vector.tensor_tensor(o, o, b[0:96, 0:HALF], ALU.subtract), "mu", s, half)
                    wait_emptied(dve, "mu", s, 1)
                    dve.sem_inc(sems["mu_done"], 1)

                def head_norm(s):
                    rows = 96 if s < 8 else 128
                    o = OT[0:rows, s, :]
                    dve.wait_ge(sems["rms_ready"], ORDER.index(s) + 1)
                    nc.vector.scalar_tensor_tensor(out=o, in0=o, scalar=SM[0:rows, 2 + s:3 + s],
                                                   in1=roots(s)[0:rows, :], op0=ALU.mult, op1=ALU.mult) \
                        .then_inc(sems["on_scaled"], 1)

                def build_scores(step):
                    if step < 15:
                        low(step + 1)
                    products(step)

                dve.wait_ge(sems["dec_ready"], 1)
                low(0)
                for i, f in enumerate(SEQ):
                    steps, before = STEPS[i], HEADS[SEQ[i - 1]] if i else []
                    for step in steps[0:2]:
                        build_scores(step)
                    for s in before:
                        if 4 <= s < 8:
                            subtract_mean(s)
                    if i:
                        wait_full(dve, "o", SEQ[i - 1], 1)
                    if f < 4:
                        q, k, bb = Z[:, 8 + f, 0:NP], Z[:, 4 + f, 0:NP], Z[:, f, 0:NP]
                        qx = SCT[:, 0].rearrange("p n t -> p (n t)")
                        kx = SCT[:, 1].rearrange("p n t -> p (n t)")
                        nc.vector.tensor_copy(qx, bb)
                        b3 = bb.rearrange("p (c i) -> p c i", i=CH)
                        nc.vector.tensor_tensor(kx.rearrange("p (c i) -> p c i", i=CH),
                                                b3[:, :, CH - 1:CH].to_broadcast([128, NC, CH]), b3, ALU.subtract) \
                            .then_inc(sems["ek_ready"], 1)
                    else:
                        for h in range(2):
                            b = wait_full(dve, "rsc", f, h)
                            dm = const("dmat").rearrange("p (h i) -> p h i", h=4)[:, 2 * (f - 4) + h, :]
                            emptied(nc.vector.tensor_tensor(SCT[:, h], b[:, :].rearrange("p (n i) -> p n i", n=4),
                                                            dm.unsqueeze(1).to_broadcast([128, 4, 128]), ALU.mult),
                                    "rsc", f, h)
                        wait_emptied(dve, "rsc", f, 1)
                        dve.sem_inc(sems["sct_ready"], 1)
                    for step in steps[2:3]:
                        build_scores(step)
                    if f < 4:
                        dve.wait_ge(sems["eq_ready"], f + 1)
                        nc.vector.tensor_tensor(q, q, qx, ALU.mult)
                        nc.vector.tensor_tensor(k, k, kx, ALU.mult).then_inc(sems["kq_ready"], 1)
                        dve.wait_ge(sems["sc_turned"], f + 1)
                        dve.wait_ge(sems["kq_ready"], i + 1)
                        for h in range(2):
                            for n in range(4):
                                last = nc.vector.tensor_tensor(
                                    SCT[:, h, n, :].rearrange("p (c i) -> p c i", i=CH),
                                    SCB[:, n, :, h].unsqueeze(1).to_broadcast([128, CT, CH]),
                                    const("mask16").unsqueeze(2).to_broadcast([128, CT, CH]), ALU.mult)
                        last.then_inc(sems["sc_read"], 1)
                        dve.wait_ge(sems["sc_read"], f + 1)
                        dve.sem_inc(sems["sct_ready"], 1)
                    else:
                        for at, table in ((8 + f, "rqdec"), (10 + f, "rkdec")):
                            z = Z[:, at, 0:NP].rearrange("p (n i) -> p n i", n=4)
                            t = const(table).rearrange("p (f i) -> p f i", f=2)[:, f - 4, :]
                            last = nc.vector.tensor_tensor(z, z, t.unsqueeze(1).to_broadcast([128, 4, 128]),
                                                           ALU.mult)
                        last.then_inc(sems["kq_ready"], 1)
                    keys(i, f)
                    for step in steps[3:4]:
                        build_scores(step)
                    sample_states(i, f)
                    for s in before:
                        head_norm(s)
                    states(f)
                for s in HEADS[SEQ[-1]]:
                    head_norm(s)
                dve.wait_ge(sems["lnp_loaded"], 64)
                for n in range(5):
                    w = WID[n]
                    for half in range(2):
                        c = slice(half * 512, (half + 1) * 512)
                        b = wait_full(dve, "mix", n, half)
                        emptied(nc.vector.scalar_tensor_tensor(out=X[0:w, n, c], in0=X[0:w, n, c], scalar=ALPHA,
                                                               in1=b[0:w, :], op0=ALU.mult, op1=ALU.add),
                                "mix", n, half)
                    dve.drain()
                    statistics(n, X[:, n, :])
                    if n:
                        normalize(n - 1, X[:, n - 1, :], 0, n, "x1_ready")
                normalize(4, X[:, 4, :], 0, 5, "x1_ready")
                to_features(1)
                wait_emptied(dve, "s", 0, 0)
                for h in range(2):
                    for part in range(4):
                        top(0, h, part)

                def add_experts(n):
                    dve.wait_ge(sems["acc_ready"], n + 1)
                    nc.vector.tensor_tensor(X[:, n, :], X[:, n, :], Y[:, :], ALU.add).then_inc(sems["y_read"], 1)
                    dve.drain()
                    statistics(n, X[:, n, :])

                for n in range(4):
                    if n == 0:
                        for c in range(1, 4):
                            wait_emptied(dve, "s", 0, c)
                            with dve.Fori(2 * c - 2, 2 * c) as h:
                                for part in range(4):
                                    dots(L, 0, h, 4 * part, 4 * part + 4)
                                    top(0, h + 2, part)
                        dots(L, 0, PH - 2, 0, TOPK)
                        dots(L, 0, PH - 1, 0, TOPK)
                    else:
                        with dve.Fori(0, 2) as h:
                            dots(L, n, h, 0, TOPK)
                        softmax_sums(n)
                        if n == 2:
                            softmax_sums(4).then_inc(sems["et_ready"], 2)
                            b = wait_full(dve, "et")
                            emptied(nc.vector.tensor_copy(IDXS, b[:, 0:NS]), "et")
                            wait_emptied(dve, "et")
                            dve.sem_inc(sems["sample_idx"], 1)
                            b = wait_full(dve, "gt")
                            emptied(nc.vector.tensor_copy(GATES, b[:, 0:NS]), "gt")
                            wait_emptied(dve, "gt")
                        with dve.Fori(2, 4) as h:
                            dots(L, n, h, 0, TOPK)
                        add_experts(n - 1)
                        dots(L, n, 4, 0, TOPK)
                        normalize(n - 1, X[:, n - 1, :], 1, TAIL.index(n - 1) + 6, "x2_ready")
                        with dve.Fori(5, PH) as h:
                            dots(L, n, h, 0, TOPK)
                    dve.drain().then_inc(sems["score_ready"], 1)
                    if n == 0:
                        dve.sem_inc(sems["rprod_ready"], 1)
                        softmax_sums(0)
                    nc.vector.tensor_scalar(X[:, n, :], X[:, n, :], ALPHA, None, ALU.mult)
                    dve.drain()
                    dve.wait_ge(sems["gelu_ready"], n + 1)
                    nc.vector.tensor_tensor(WGT, WGT, GATE[:, n, :], ALU.mult).then_inc(sems["w_ready"], 1)
                    if n == 3:
                        dve.wait_ge(sems["sample_gelu"], 1)
                        nc.vector.tensor_tensor(WS, WS, GATES, ALU.mult)
                        dve.drain()
                        nc.vector.tensor_tensor(WS8, WS.unsqueeze(2).to_broadcast([128, NS, NS]),
                                                const("eye8").rearrange("p (a b) -> p a b", a=8), ALU.mult) \
                            .then_inc(sems["wsam_ready"], 1)
                    if n:
                        add_embedding(n - 1)
                    if n == 3:
                        for half in range(2):
                            b = wait_full(dve, "sacc", half)
                            emptied(nc.vector.tensor_copy(X[0:NS, 4, half * 512:(half + 1) * 512], b[0:NS, :]),
                                    "sacc", half)
                        dve.drain()
                        statistics(4, X[:, 4, :])
                        normalize(4, X[:, 4, :], 1, 9, "x2_ready")
                    if n < 3:
                        wait_emptied(dve, "s", n + 1, 3)
                    if n < 2:
                        wait_emptied(dve, "s", 4, 3)

                    def output_rows(h, searches):
                        mine = [g * RING + k for g in range(GPH) for k in DVE_ROWS[n]]
                        each = -(-len(searches) // len(mine))
                        for j in mine:
                            k = j % RING
                            dve.drain()
                            dve.wait_ge(fetched[k], L * (16 * USES) + h * (16 * GPH)
                                        + 16 * (fetches_before(n, 1) + j // RING + 1))
                            nc.vector.scalar_tensor_tensor(
                                out=X[:, n, :], in0=G[:, k, :], scalar=WGT[:, ds(h * TOPK + j, 1)],
                                in1=X[:, n, :], op0=ALU.mult, op1=ALU.add).then_inc(sems["vd_used"], 1)
                            for m, head, part in searches[:each]:
                                top(m, head, part)
                            searches = searches[each:]

                    if n < 2:
                        with dve.Fori(0, PH // 2) as h:
                            output_rows(h * 2, [(n + 1, h * 2, part) for part in range(4)]
                                        + [(4, h + n * (PH // 2), part) for part in range(4)])
                            output_rows(h * 2 + 1, [(n + 1, h * 2 + 1, part) for part in range(4)])
                    else:
                        with dve.Fori(0, PH) as h:
                            output_rows(h, [(n + 1, h, part) for part in range(4)] if n < 3 else [])
                    dve.drain()
                    dve.sem_inc(sems["rprod_ready"], 2 if n == 1 else 1)
                    if n == 2:
                        for t in range(NS):
                            dve.wait_ge(fetched[t], L * (16 * USES) + 16 * fetches_before(3, 0))
                            for half in range(2):
                                b = wait_full(dve, "xb", t, half)
                                g = G[:, t, half * 512:(half + 1) * 512]
                                emptied(nc.vector.scalar_tensor_tensor(
                                    out=g, in0=g, scalar=1.0, in1=b[:, :], op0=ALU.mult,
                                    op1=ALU.mult, accum_out=SSH[:, half, t:t + 1]), "xb", t, half)
                            wait_emptied(dve, "xb", t, 1)
                            dve.sem_inc(sems["u_used"], 1)
                        nc.vector.tensor_tensor(SSC, SSH[:, 0, :], SSH[:, 1, :], ALU.add) \
                            .then_inc(sems["sample_score"], 1)
                add_experts(3)
                normalize(3, X[:, 3, :], 1, TAIL.index(3) + 6, "x2_ready")
                add_embedding(4)
                add_embedding(3)
                nc.vector.tensor_scalar(LBASE[:, :], LBASE[:, :], float(NEXP), None, ALU.add)
                nc.vector.tensor_copy(LB[:, 4:6], LB[:, 14:16])
                arrive(dve, L)


def kernel(x_prompt, x_sample, p_prompt, p_sample, state_gla, state_ret, state_hgrn,
           w_in, gla_w_gate, gla_b_gate, gla_norm, ret_norm, hgrn_lb_logits, hgrn_norm, w_out,
           ln1_g, ln1_b, ln2_g, ln2_b, peer_w_q, peer_subkeys, peer_u, peer_v, ple_proj, ple_gate):
    import numpy as np
    import concourse.bacc as bacc
    from concourse.bass_utils import run_bass_kernel_spmd

    f32 = np.float32
    cols = {n: np.zeros((128, w), f32) for n, (_, w) in CONSTS.items()}
    p = np.arange(128)
    cols["ident"][:] = np.eye(128)
    cols["aident"][:] = np.eye(128) * ALPHA
    cols["onesg"][:96] = f32(1 / 96)
    cols["onesh"][:] = (p[:, None] // 64 == p[None] // 64) / 64
    cols["headsel"][:, 30:32] = p[:, None] // 64 == np.arange(2)
    cols["mask16"][:] = p[:, None] // CH == np.arange(CT)
    cols["causal"][:] = np.where(np.arange(CH)[:, None] >= np.arange(CH)[None], 0.0, -1e30).reshape(1, -1)
    cols["eye8"][:] = np.eye(8).reshape(1, 64)
    cols["eps"][:] = EPS
    cols["iota"][:] = np.arange(16)
    t = np.arange(T)
    cols["chunkmask"][:] = (t < NP) & (t % CH != 0)
    inv = (f32(1) / (f32(10000.0) ** (np.arange(0, 48, 2, dtype=f32) / f32(48)))).astype(f32)
    pos = np.where(t < NP, t, 4096).astype(f32)
    ang = pos[None, :] * inv[:, None]
    gamma = np.log1p(-np.exp2(-5.0 - np.arange(4)))
    for h in range(2):
        for i in range(24):
            a, b = 64 * h + i, 64 * h + 24 + i
            cols["perm"][a, b] = cols["perm"][b, a] = 1
            cols["cos"][a] = cols["cos"][b] = np.cos(ang[i])
            cols["sin"][a], cols["sin"][b] = -np.sin(ang[i]), np.sin(ang[i])
    i = np.arange(128)
    for h in range(4):
        f, rows = h // 2, slice(64 * (h % 2), 64 * (h % 2) + 64)
        dist = i[None, :] - i[:, None]
        cols["dmat"][:, h * 128:(h + 1) * 128] = np.where(dist >= 0, np.exp(gamma[h] * np.maximum(dist, 0)), 0)
        cols["rqdec"][rows, f * 128:(f + 1) * 128] = np.exp(gamma[h] * (i + 1))
        cols["rkdec"][rows, f * 128:(f + 1) * 128] = np.exp(gamma[h] * (127 - i))
        cols["g128"][rows, f] = np.exp(gamma[h] * 128)
        cols["gam"][rows, f] = np.exp(gamma[h])
    consts = np.concatenate(list(cols.values()), axis=1)

    def arr(a):
        return np.ascontiguousarray(a)

    w_in, w_out = arr(w_in), arr(w_out)

    def pairs(at, width, f):
        out = np.zeros((DEPTH, D, 128), f32)
        for h in range(2):
            o = at + (2 * f + h) * width
            out[:, :, 64 * h:64 * h + width] = w_in[:, :, o:o + width]
        return out

    def wide(at, width, count):
        out = np.zeros((DEPTH, D, 128), f32)
        out[:, :, :width] = w_in[:, :, at:at + width]
        return out

    tiles = {"hf0": pairs(2576, 64, 0), "hf1": pairs(2576, 64, 1), "glr": wide(1152, 16, 1),
             "hq0": pairs(2320, 64, 0), "hq1": pairs(2320, 64, 1), "gk0": pairs(192, 48, 0),
             "gk1": pairs(192, 48, 1), "gq0": pairs(0, 48, 0), "gq1": pairs(0, 48, 1),
             "rq0": pairs(1168, 48, 0), "rq1": pairs(1168, 48, 1), "rk0": pairs(1360, 48, 0),
             "rk1": pairs(1360, 48, 1)}
    feat = np.concatenate([tiles[n] for n in FEATURES] + [np.zeros((DEPTH, D, 128), f32)], axis=2)
    vals = np.concatenate([w_in[:, :, 384:768], w_in[:, :, 1552:1936], w_in[:, :, 2832:3088]], axis=2)
    gate = np.concatenate([wide(1936 + 96 * h, 96, 1) for h in range(4)]
                          + [wide(768 + 96 * h, 96, 1) for h in range(4)]
                          + [pairs(3088, 64, 0), pairs(3088, 64, 1)], axis=2)
    ws = np.zeros((DEPTH, ITEMS, 128, 2048), f32)

    def put(first, m):
        n = m.shape[2] // 256
        v = m.reshape(DEPTH, KT, 128, n, 256).transpose(0, 3, 2, 1, 4)
        ws[:, first:first + n] = v.reshape(DEPTH, n, 128, 2048)

    put(0, feat)
    put(I_V, vals)
    put(I_GATE, gate)
    for j, i in enumerate(I_Q):
        put(i, arr(peer_w_q)[:, :, 256 * j:256 * j + 256])
    put(I_PG, arr(ple_gate))
    sub = arr(peer_subkeys).reshape(DEPTH, 4, 4, 128, 128).transpose(0, 1, 4, 2, 3)
    for c, i in enumerate(I_SUB):
        ws[:, i, :, :512] = sub[:, c].reshape(DEPTH, 128, 512)
    ws[:, I_PP] = arr(ple_proj).reshape(DEPTH, 2, 128, D).transpose(0, 2, 1, 3).reshape(DEPTH, 128, 2048)
    pt = np.concatenate([arr(p_prompt).reshape(DEPTH, NP, 256), arr(p_sample).reshape(DEPTH, NS, 256)], axis=1)
    pt = pt.transpose(0, 2, 1).reshape(DEPTH, 2, 128, T).transpose(0, 2, 1, 3)
    ws[:, I_PT, :, :2 * T] = pt.reshape(DEPTH, 128, 2 * T)
    wo = np.zeros((DEPTH, 128, 10, D), f32)
    for h in range(8):
        wo[:, :96, h] = w_out[:, 96 * h:96 * h + 96]
    wo[:, :, 8], wo[:, :, 9] = w_out[:, 768:896], w_out[:, 896:1024]
    small = np.zeros((DEPTH, 128, NSMALL), f32)
    for f in range(2):
        for h in range(2):
            c = slice((2 * f + h) * 48, (2 * f + h + 1) * 48)
            small[:, 64 * h:64 * h + 48, f] = arr(gla_b_gate)[:, c]
            small[:, :16, 12 + f * 128 + 64 * h:12 + f * 128 + 64 * h + 48] = arr(gla_w_gate)[:, :, c]
    small[:, :96, 2:6] = arr(gla_norm).transpose(0, 2, 1)
    small[:, :96, 6:10] = arr(ret_norm).transpose(0, 2, 1)
    small[:, :, 10:12] = arr(hgrn_norm).reshape(DEPTH, 2, 128).transpose(0, 2, 1)
    lnp = np.stack([arr(a) for a in (ln1_g, ln1_b, ln2_g, ln2_b)], axis=1)
    lblog = arr(arr(hgrn_lb_logits).reshape(DEPTH, 2, 128).transpose(2, 0, 1).reshape(128, 4))
    st_in = np.zeros((DEPTH, 6, 128, NS, 96), f32)
    places = ((arr(state_gla), 0, 48, 96), (arr(state_hgrn), 2, 64, 64), (arr(state_ret), 4, 48, 96))
    for state, f0, dk, dv in places:
        for h in range(4):
            st_in[:, f0 + h // 2, 64 * (h % 2):64 * (h % 2) + dk, :, :dv] = state[:, :, h].transpose(0, 2, 1, 3)
    x = np.concatenate([arr(x_prompt).reshape(NP, D), arr(x_sample).reshape(NS, D)])
    u, v = arr(peer_u).reshape(DEPTH * NEXP, D), arr(peer_v).reshape(DEPTH * NEXP, D)

    nc = bacc.Bacc("TRN2", target_bir_lowering=False, num_devices=1)
    arrays = {"x": x, "wstream": ws, "wout": wo, "small": small, "lnp": lnp, "lblog": lblog, "st_in": st_in,
              "consts": consts, "utab": u, "vtab": v}
    outs = {"y": (T, D), "st_p": (DEPTH, 6, 128, 96), "st_s": (DEPTH, 6, 128, NS, 96)}
    fp32 = mybir.dt.float32
    args = [nc.dram_tensor(f"in_{n}", a.shape, fp32, kind="ExternalInput").ap() for n, a in arrays.items()]
    args += [nc.dram_tensor(f"out_{n}", s, fp32, kind="ExternalOutput").ap() for n, s in outs.items()]
    build(nc, *args)
    r = run_bass_kernel_spmd(nc, [{f"in_{n}": a for n, a in arrays.items()}], core_ids=[0]).results[0]
    y, st_p, st_s = (r[f"out_{n}"] for n in outs)

    def heads(st, f0, dk, dv):
        return np.stack([st[:, f0 + h // 2, 64 * (h % 2):64 * (h % 2) + dk, ..., :dv] for h in range(4)], axis=2)

    new_p, new_s = [], []
    for f0, dk, dv in ((0, 48, 96), (4, 48, 96), (2, 64, 64)):
        new_p.append(heads(st_p, f0, dk, dv).transpose(0, 2, 1, 3)[:, None])
        new_s.append(heads(st_s, f0, dk, dv).transpose(0, 3, 2, 1, 4))
    return (y[:NP].reshape(1, NP, D), y[NP:].reshape(NS, 1, D), *map(arr, new_p), *map(arr, new_s))
```
